# Optimizing a Trainium2 kernel written in Bass

```python
import jax, jax.numpy as jnp
from jax import lax
import numpy as np

D_MODEL = 1024
BATCH = 1
SEQ = 256
DEPTH = 2

MEM_LEN = 256
HEAD_DIM = 64
N_SELF_HEADS = 12
N_KV_HEADS_SWA = 3
N_CROSS_HEADS = 4
SWA_WINDOW = 128
BLOCK = 128
ROPE_THETA = 10000.0
D_FF = 3584
N_EXPERTS = 8
TOP_K = 2
RMS_EPS = 1e-6
N_MIXERS = 2
MAX_START = 4096

SELF_W = N_SELF_HEADS * HEAD_DIM
KV_W_SWA = N_KV_HEADS_SWA * HEAD_DIM
CROSS_W = N_CROSS_HEADS * HEAD_DIM
IN_W_SWA = SELF_W + 2 * KV_W_SWA + CROSS_W
IN_W_SB = 3 * SELF_W + CROSS_W
MIX_W = SELF_W + CROSS_W

kernel_name = "hybrid_swa_stickbreak_memx_moe"

def rms_norm(x, g):
    xf = x.astype(jnp.float32)
    var = jnp.mean(xf * xf, axis=-1, keepdims=True)
    return (xf * lax.rsqrt(var + RMS_EPS) * g.astype(jnp.float32)).astype(x.dtype)

def rope(x, positions):
    inv_freq = ROPE_THETA ** (-jnp.arange(0, HEAD_DIM, 2, dtype=jnp.float32) / HEAD_DIM)
    ang = positions.astype(jnp.float32)[..., None] * inv_freq
    cos = jnp.cos(ang)[:, :, None, :]
    sin = jnp.sin(ang)[:, :, None, :]
    xf = x.astype(jnp.float32)
    x1, x2 = jnp.split(xf, 2, axis=-1)
    out = jnp.concatenate([x1 * cos - x2 * sin, x2 * cos + x1 * sin], axis=-1)
    return out.astype(x.dtype)

def swa_sink_attention(q, k, v, sinks):
    B, S, Hq, hd = q.shape
    Hkv = k.shape[2]
    G = Hq // Hkv
    nb = S // BLOCK
    scale = hd ** -0.5
    qb = q.reshape(B, nb, BLOCK, Hkv, G, hd)

    def band(t):
        tb = t.reshape(B, nb, BLOCK, Hkv, hd)
        prev = jnp.pad(tb[:, :-1], ((0, 0), (1, 0), (0, 0), (0, 0), (0, 0)))
        return jnp.concatenate([prev, tb], axis=2)

    kband, vband = band(k), band(v)
    scores = jnp.einsum('bnqhgd,bnkhd->bnhgqk', qb, kband,
                        preferred_element_type=jnp.float32) * scale
    qi = jnp.arange(BLOCK)[:, None]
    kj = jnp.arange(2 * BLOCK)[None, :]
    diff = qi + BLOCK - kj
    in_win = (diff >= 0) & (diff < SWA_WINDOW)
    blk = jnp.arange(nb)[:, None]
    key_ok = (blk * BLOCK + kj - BLOCK) >= 0
    mask = in_win[None, :, :] & key_ok[:, None, :]
    scores = jnp.where(mask[None, :, None, None], scores, -jnp.inf)
    sink = sinks.astype(jnp.float32).reshape(Hkv, G)[None, None, :, :, None, None]
    m = jnp.maximum(jnp.max(scores, axis=-1, keepdims=True), sink)
    p = jnp.exp(scores - m)
    denom = jnp.sum(p, axis=-1, keepdims=True) + jnp.exp(sink - m)
    probs = (p / denom).astype(v.dtype)
    out = jnp.einsum('bnhgqk,bnkhd->bnqhgd', probs, vband)
    return out.reshape(B, S, Hq * hd)

def stick_breaking_attention(q, k, v):
    B, S, H, hd = q.shape
    nb = S // BLOCK
    scale = hd ** -0.5
    qb = q.reshape(B, nb, BLOCK, H, hd).transpose(1, 0, 3, 2, 4)
    kt = k.transpose(0, 2, 1, 3)
    vt = v.transpose(0, 2, 1, 3)
    s_idx = jnp.arange(S)

    def one_block(args):
        q_blk, blk = args
        z = jnp.einsum('bhqd,bhkd->bhqk', q_blk, kt,
                       preferred_element_type=jnp.float32) * scale
        t_idx = blk * BLOCK + jnp.arange(BLOCK)
        causal = s_idx[None, :] < t_idx[:, None]
        log_1m = jnp.where(causal, jax.nn.log_sigmoid(-z), 0.0)
        later = lax.cumsum(log_1m, axis=3, reverse=True) - log_1m
        w = jnp.where(causal, jnp.exp(jax.nn.log_sigmoid(z) + later), 0.0)
        return jnp.einsum('bhqk,bhkd->bhqd', w.astype(vt.dtype), vt)

    out = lax.map(one_block, (qb, jnp.arange(nb)))
    return out.transpose(1, 0, 3, 2, 4).reshape(B, S, H * hd)

def memory_cross_attention(qc, mem_n, w_mem_kv):
    B, S, _ = qc.shape
    kv = mem_n @ w_mem_kv
    km, vm = jnp.split(kv, 2, axis=-1)
    qh = qc.reshape(B, S, N_CROSS_HEADS, HEAD_DIM)
    km = km.reshape(B, MEM_LEN, N_CROSS_HEADS, HEAD_DIM)
    vm = vm.reshape(B, MEM_LEN, N_CROSS_HEADS, HEAD_DIM)
    scores = jnp.einsum('bshd,bmhd->bhsm', qh, km,
                        preferred_element_type=jnp.float32) * (HEAD_DIM ** -0.5)
    probs = jax.nn.softmax(scores, axis=-1).astype(vm.dtype)
    out = jnp.einsum('bhsm,bmhd->bshd', probs, vm)
    return out.reshape(B, S, CROSS_W)

def token_mixing(h, mem, positions, mixer, p):
    B, S, _ = h.shape
    xn = rms_norm(h, p['attn_pre_g'])
    proj = xn @ p['w_in']
    if mixer == 0:
        q, k, v, qc = jnp.split(proj, [SELF_W, SELF_W + KV_W_SWA, SELF_W + 2 * KV_W_SWA], axis=-1)
        q = rope(q.reshape(B, S, N_SELF_HEADS, HEAD_DIM), positions)
        k = rope(k.reshape(B, S, N_KV_HEADS_SWA, HEAD_DIM), positions)
        v = v.reshape(B, S, N_KV_HEADS_SWA, HEAD_DIM)
        self_out = swa_sink_attention(q, k, v, p['sinks'])
    else:
        q, k, v, qc = jnp.split(proj, [SELF_W, 2 * SELF_W, 3 * SELF_W], axis=-1)
        q = q.reshape(B, S, N_SELF_HEADS, HEAD_DIM)
        k = k.reshape(B, S, N_SELF_HEADS, HEAD_DIM)
        v = v.reshape(B, S, N_SELF_HEADS, HEAD_DIM)
        self_out = stick_breaking_attention(q, k, v)
    mem_n = rms_norm(mem, p['mem_g'])
    cross_out = memory_cross_attention(qc, mem_n, p['w_mem_kv'])
    mixed = jnp.concatenate([self_out, cross_out], axis=-1) @ p['w_out']
    return h + rms_norm(mixed, p['attn_post_g'])

def swiglu(x, w_gate, w_up, w_down):
    return (jax.nn.silu(x @ w_gate) * (x @ w_up)) @ w_down

def moe_swiglu(x, w_router, w_gate, w_up, w_down):
    B, S, D = x.shape
    xt = x.reshape(B * S, D)
    logits = jnp.matmul(xt, w_router, preferred_element_type=jnp.float32)
    top_vals, top_idx = lax.top_k(logits, TOP_K)
    top_w = jax.nn.softmax(top_vals, axis=-1)
    gates = jnp.sum(jax.nn.one_hot(top_idx, N_EXPERTS, dtype=jnp.float32) * top_w[..., None], axis=1)
    out = jnp.zeros((B * S, D), jnp.float32)
    for e in range(N_EXPERTS):
        y = swiglu(xt, w_gate[e], w_up[e], w_down[e]).astype(jnp.float32)
        out = out + gates[:, e:e + 1] * y
    return out.astype(x.dtype).reshape(B, S, D)

def channel_mixing(h, layer_idx, p):
    xn = rms_norm(h, p['ffn_pre_g'])
    if layer_idx % 2 == 0:
        y = swiglu(xn, p['w_gate'], p['w_up'], p['w_down'])
    else:
        y = moe_swiglu(xn, p['w_router'], p['w_gate'], p['w_up'], p['w_down'])
    return h + rms_norm(y, p['ffn_post_g'])

def setup_inputs(seed: int = 0) -> dict:
    key = jax.random.key(seed)
    ks = jax.random.split(key, 32)
    f32 = jnp.float32

    def nrm(k, shape, fan_in):
        return jax.random.normal(k, shape, f32) * (fan_in ** -0.5)

    def gain(k):
        return 1.0 + 0.05 * jax.random.normal(k, (D_MODEL,), f32)

    x = jax.random.normal(ks[0], (BATCH, SEQ, D_MODEL), f32)
    mem = jax.random.normal(ks[1], (BATCH, MEM_LEN, D_MODEL), f32)
    start = jax.random.randint(ks[2], (BATCH, 1), 0, MAX_START, dtype=jnp.int32)
    positions = start + jnp.arange(SEQ, dtype=jnp.int32)[None, :]
    return {
        "x": x,
        "mem": mem,
        "positions": positions,
        "l0_attn_pre_g": gain(ks[3]),
        "l0_mem_g": gain(ks[4]),
        "l0_w_in": nrm(ks[5], (D_MODEL, IN_W_SWA), D_MODEL),
        "l0_w_mem_kv": nrm(ks[6], (D_MODEL, 2 * CROSS_W), D_MODEL),
        "l0_sinks": 0.5 * jax.random.normal(ks[7], (N_SELF_HEADS,), f32),
        "l0_w_out": nrm(ks[8], (MIX_W, D_MODEL), MIX_W),
        "l0_attn_post_g": gain(ks[9]),
        "l0_ffn_pre_g": gain(ks[10]),
        "l0_w_gate": nrm(ks[11], (D_MODEL, D_FF), D_MODEL),
        "l0_w_up": nrm(ks[12], (D_MODEL, D_FF), D_MODEL),
        "l0_w_down": nrm(ks[13], (D_FF, D_MODEL), D_FF),
        "l0_ffn_post_g": gain(ks[14]),
        "l1_attn_pre_g": gain(ks[15]),
        "l1_mem_g": gain(ks[16]),
        "l1_w_in": nrm(ks[17], (D_MODEL, IN_W_SB), D_MODEL),
        "l1_w_mem_kv": nrm(ks[18], (D_MODEL, 2 * CROSS_W), D_MODEL),
        "l1_w_out": nrm(ks[19], (MIX_W, D_MODEL), MIX_W),
        "l1_attn_post_g": gain(ks[20]),
        "l1_ffn_pre_g": gain(ks[21]),
        "l1_w_router": nrm(ks[22], (D_MODEL, N_EXPERTS), D_MODEL),
        "l1_w_gate": nrm(ks[23], (N_EXPERTS, D_MODEL, D_FF), D_MODEL),
        "l1_w_up": nrm(ks[24], (N_EXPERTS, D_MODEL, D_FF), D_MODEL),
        "l1_w_down": nrm(ks[25], (N_EXPERTS, D_FF, D_MODEL), D_FF),
        "l1_ffn_post_g": gain(ks[26]),
    }

def reference(x, mem, positions,
              l0_attn_pre_g, l0_mem_g, l0_w_in, l0_w_mem_kv, l0_sinks, l0_w_out, l0_attn_post_g,
              l0_ffn_pre_g, l0_w_gate, l0_w_up, l0_w_down, l0_ffn_post_g,
              l1_attn_pre_g, l1_mem_g, l1_w_in, l1_w_mem_kv, l1_w_out, l1_attn_post_g,
              l1_ffn_pre_g, l1_w_router, l1_w_gate, l1_w_up, l1_w_down, l1_ffn_post_g):
    layers = [
        dict(attn_pre_g=l0_attn_pre_g, mem_g=l0_mem_g, w_in=l0_w_in, w_mem_kv=l0_w_mem_kv,
             sinks=l0_sinks, w_out=l0_w_out, attn_post_g=l0_attn_post_g,
             ffn_pre_g=l0_ffn_pre_g, w_gate=l0_w_gate, w_up=l0_w_up, w_down=l0_w_down,
             ffn_post_g=l0_ffn_post_g),
        dict(attn_pre_g=l1_attn_pre_g, mem_g=l1_mem_g, w_in=l1_w_in, w_mem_kv=l1_w_mem_kv,
             w_out=l1_w_out, attn_post_g=l1_attn_post_g,
             ffn_pre_g=l1_ffn_pre_g, w_router=l1_w_router, w_gate=l1_w_gate, w_up=l1_w_up,
             w_down=l1_w_down, ffn_post_g=l1_ffn_post_g),
    ]
    h = x
    for i in range(DEPTH):
        p = layers[i]
        h = token_mixing(h, mem, positions, i % N_MIXERS, p)
        h = channel_mixing(h, i, p)
    return h


_drawn_inputs = setup_inputs


def setup_inputs(seed=0):
    import zlib

    import numpy as np

    out = dict(_drawn_inputs(seed))
    spreads = {}
    factors = {'l1_mem_g': 8.0}
    for name, (base, spread) in spreads.items():
        noise = np.random.default_rng([zlib.crc32(name.encode()), seed]).standard_normal(out[name].shape)
        drawn = base * np.exp(spread * noise) if base else spread * noise
        out[name] = __import__('jax').numpy.asarray(drawn.astype(out[name].dtype))
    for name, factor in factors.items():
        out[name] = (out[name] * factor).astype(out[name].dtype)
    return out
```

```python
from contextlib import ExitStack

import concourse.bass as bass
from concourse import mybir

P = 128
D = 1024
KD = D // P
S = 256
NT = S // P
HD = 64
NH = 12
NKV = 3
NC = 4
GQ = NH // NKV
MEM = 256
FF = 3584
FB = 512
NB = FF // FB
CB = FB // P
NE = 8
CAP = P
MAX_JOBS = NE + NE // 2 - 1
EPS = 1e-6
SCALE = HD ** -0.5
THETA = 10000.0
SLOTS = 7
SLOT_W = KD * FB
NEG = -1.0e30
BIG = 3.0e38
TWO_PI = 6.283185307179586
TP1 = 6.28125
TP2 = 0.0019350051879882812
TP3 = TWO_PI - TP1 - TP2
ROUND = 12582912.0

ALU = mybir.AluOpType
ACT = mybir.ActivationFunctionType
AX = mybir.AxisListType
F32 = mybir.dt.float32
I32 = mybir.dt.int32
U32 = mybir.dt.uint32

NORMS = ["l0_mem_g", "l0_attn_pre_g", "l0_attn_post_g", "l0_ffn_pre_g", "l1_mem_g", "l0_ffn_post_g",
         "l1_attn_pre_g", "l1_attn_post_g", "l1_ffn_pre_g", "l1_ffn_post_g"]
MEM0, PRE0, POST0, FPRE0, MEM1, FPOST0, PRE1, POST1, FPRE1, FPOST1 = range(len(NORMS))
NG = 3


TURN = (1, 1, 4, 4, 5, 5, 2, 8)


class Banks:

    def __init__(self, filled, drained):
        self.filled, self.drained = filled, drained
        self.count = [0] * len(filled)
        self.at = {}

    def fill(self, label, bank, j=0):
        n = self.count[bank]
        self.count[bank] += 1
        self.at[label] = (bank, n + 1)
        return self.drained[bank], n + j * TURN[bank]

    def full(self, label, j=0):
        bank, n = self.at[label]
        return self.filled[bank], n + j * TURN[bank]

    def empty(self, label, j=0):
        bank, n = self.at[label]
        return self.drained[bank], n + j * TURN[bank]

    def full_sem(self, label):
        return self.filled[self.at[label][0]]

    def empty_sem(self, label):
        return self.drained[self.at[label][0]]


def trunk(nc, t):
    with ExitStack() as ctx:
        def sb(name, shape, dt=F32):
            return ctx.enter_context(nc.sbuf_tensor(name, shape, dt))

        def sem(name):
            return ctx.enter_context(nc.semaphore(name))

        ring = sb("ring", [P, SLOTS, SLOT_W])
        hres = sb("hres", [P, NT, D])
        memb = sb("memb", [P, NT, D])
        xn = sb("xn", [P, NT, D])
        reg_a = sb("reg_a", [P, 2 * D])
        reg_b = sb("reg_b", [P, 2 * D])
        mixT = sb("mixT", [P, KD, S])
        gains = sb("gains", [P, NG, D])
        work = sb("work", [P, 6144])
        ident = sb("ident", [P, P])
        upper_neg = sb("upper_neg", [P, P])
        ones_neg = sb("ones_neg", [P, P])
        ones = sb("ones", [P, P])
        before = sb("before", [P, P])
        band = sb("band", [P, 2 * P])
        clamp = sb("clamp", [P, P])
        iota_s = sb("iota_s", [P, P])
        iota_i = sb("iota_i", [P, P], I32)
        cos2 = sb("cos2", [P, NT, HD])
        sin2 = sb("sin2", [P, NT, HD])
        rope_s = sb("rope_s", [P, 4, NT, HD // 2])
        invf = sb("invf", [P, HD // 2])
        pos_i = sb("pos_i", [P, NT], I32)
        pos_f = sb("pos_f", [P, NT])
        sinks = sb("sinks", [P, NH])
        nsinks = sb("nsinks", [P, NH])
        mhalf = sb("mhalf", [P, 1])
        halfpi = sb("halfpi", [P, 1])
        ssq = sb("ssq", [P, len(NORMS), NT])
        rstd = sb("rstd", [P, len(NORMS), NT])
        NU = 2 * (NKV + 1) * NT
        nmax = sb("nmax", [P, NU, 4])
        psum_e = sb("psum_e", [P, NU, 4])
        esink = sb("esink", [P, NU, 4])
        recip = sb("recip", [P, NU, 4])
        wr = sb("wr", [P, KD, NE])
        logits = sb("logits", [P, NT, NE])
        top_v = sb("top_v", [P, NT, 8])
        top_i = sb("top_i", [P, NT, 8], U32)
        top_f = sb("top_f", [P, NT, 8])
        gate2 = sb("gate2", [P, NT, 4])
        mask2 = sb("mask2", [P, NT, 2, NE])
        chosen = sb("chosen", [P, NT, NE])
        gates = sb("gates", [P, NT, NE])
        rank = sb("rank", [P, NT, NE])
        over = sb("over", [P, 3, NE])
        over_sel = sb("over_sel", [P, 3, NE])
        junk8 = sb("junk8", [P, 16])
        slot_of = sb("slot_of", [P, NT, MAX_JOBS + 1])
        gate_of = sb("gate_of", [P, NT, MAX_JOBS + 1])
        job_f = sb("job_f", [P, 4])
        job_i = sb("job_i", [P, 4], I32)

        psum = ctx.enter_context(nc.psum_tensor("psum", [P, 8, 512], F32))

        memT = reg_a[:, :].rearrange("p (k s) -> p k s", k=KD)
        xT = reg_b[:, :].rearrange("p (k s) -> p k s", k=KD)
        probs = reg_a[:, :].rearrange("p (u b h k) -> p u b h k", u=2, b=2, h=2)
        probsT = reg_b[:, :].rearrange("p (u b h k q) -> p u b h k q", u=2, b=2, h=2, k=2)
        rope_q = reg_a[:, 0:1024].rearrange("p (u c) -> p u c", u=2)
        rope_a = reg_a[:, 1024:1536]
        rope_b = reg_a[:, 1536:2048]
        soft = reg_a[:, 0:1536].rearrange("p (u b c) -> p u b c", u=2, b=2)
        stick = reg_b[:, 0:1536].rearrange("p (u b c) -> p u b c", u=2, b=2)
        qT = work[:, 0:1536].rearrange("p (c s) -> p c s", c=6)
        kT = work[:, 1536:3072].rearrange("p (c s) -> p c s", c=6)
        v = work[:, 3072:4608].rearrange("p (t c) -> p t c", t=NT)
        kmT = work[:, 4608:5120].rearrange("p (c s) -> p c s", c=2)
        vm = work[:, 5120:5632].rearrange("p (t c) -> p t c", t=NT)
        qcT = work[:, 5632:6144].rearrange("p (c s) -> p c s", c=2)
        kdup = mixT[:, 0:3, :].rearrange("p k s -> p (k s)").rearrange("p (t g u c) -> p t g u c", t=NT, g=NKV, u=2)
        act0 = work[:, 0:1024].rearrange("p (t c) -> p t c", t=2)
        hid0 = work[:, 1024:3072].rearrange("p (u t c) -> p u t c", u=2, t=NT)
        hidT0 = work[:, 3072:4096].rearrange("p (t c) -> p t c", t=NT)
        act1 = act0
        hid1 = work[:, 1024:2048].rearrange("p (u c) -> p u c", u=2)
        hidT1 = work[:, 2048:2560]
        pick = work[:, 2560:2816].rearrange("p (t s) -> p t s", t=NT)
        pickT = work[:, 2816:3072].rearrange("p (t s) -> p t s", t=NT)
        picked = work[:, 3072:4096].rearrange("p (k s) -> p k s", k=KD)
        y_sb = work[:, 4096:5120]
        esum = memb

        def unit(u, layer, i, tt):
            if layer == 0 and i < NKV:
                return u, layer, i, tt, qT, kT, (0, (tt + 1) * P), v, 0
            return u, layer, i, tt, qcT, kmT, (0, MEM), vm, 0

        UNITS0 = [unit(NT * i + tt, 0, i, tt) for i in range(NKV + 1) for tt in range(NT)]
        UNITS1 = [unit(len(UNITS0) + tt, 1, NKV, tt) for tt in range(NT)]

        def bank(b, lo=0, hi=512):
            return psum[:, b, lo:hi]

        filled = [sem(f"bank{b}_filled") for b in range(8)]
        drained = [sem(f"bank{b}_drained") for b in range(8)]
        slot_full = [sem(f"slot{s}_full") for s in range(SLOTS)]
        downs = sem("downs")
        x_in, mem_in, small_in = sem("x_in"), sem("mem_in"), sem("small_in")
        gain_in = [sem(f"gain{i}_in") for i in range(NG)]
        consts = sem("consts")
        summed, rstd_ok, scaled, added = sem("summed"), sem("rstd_ok"), sem("scaled"), sem("added")
        act_chain, dve_chain, pool_chain = sem("act_chain"), sem("dve_chain"), sem("pool_chain")
        angles, sines = sem("angles"), sem("sines")
        roped = sem("roped")
        max_ok, exp_ok, norm_ok = sem("max_ok"), sem("exp_ok"), sem("norm_ok")
        soft_a, soft_b, stick_a, stick_b = sem("soft_a"), sem("soft_b"), sem("stick_a"), sem("stick_b")
        silu_ok = sem("silu_ok")
        gap_ok, gexp_ok, chosen_ok, tables_ok = sem("gap_ok"), sem("gexp_ok"), sem("chosen_ok"), sem("tables_ok")
        pick_ok = sem("pick_ok")
        silu1_ok = sem("silu1_ok")
        stored = sem("stored")

        bk = Banks(filled, drained)

        def cols(w, lo, hi):
            return w.rearrange("(k p) n -> p k n", p=P)[:, :, lo:hi]

        def down_rows(w, b):
            return w[b * FB:(b + 1) * FB, :].rearrange("(p c) n -> p c n", c=CB)

        def ffn_loads(wg, wu, wd):
            out = []
            for b in range(NB + 1):
                if b < NB:
                    out += [cols(wg, b * FB, (b + 1) * FB), cols(wu, b * FB, (b + 1) * FB)]
                if b >= 1:
                    out.append(down_rows(wd, b - 1))
            return out

        IN0 = [(0, 512), (512, 1024), (1024, 1408)]
        IN1 = [(i * 512, (i + 1) * 512) for i in range(5)]
        loads = [cols(t["l0_w_mem_kv"], 0, 512)]
        loads += [cols(t["l0_w_in"], lo, hi) for lo, hi in IN0]
        loads += [cols(t["l0_w_out"], lo, lo + 512) for lo in (0, 512)]
        loads += ffn_loads(t["l0_w_gate"], t["l0_w_up"], t["l0_w_down"])
        loads += [cols(t["l1_w_mem_kv"], 0, 512)]
        loads += [cols(t["l1_w_in"], lo, hi) for lo, hi in IN1]
        loads += [cols(t["l1_w_out"], lo, lo + 512) for lo in (0, 512)]
        PRE = len(loads)
        PER = 3 * NB
        assert PRE % SLOTS == 0 and PER % SLOTS == 0

        place, n = {}, 0
        for b in range(NB + 1):
            if b < NB:
                place["g", b], place["u", b] = n, n + 1
                n += 2
            if b >= 1:
                place["d", b - 1] = n
                n += 1

        def slot(n, c=KD, w=FB):
            return ring[:, n % SLOTS, 0:c * w].rearrange("p (c n) -> p c n", c=c)

        block = ctx.enter_context(nc.Block())

        free_after = []
        job_free = {}

        @block.tensor
        def _(pe):
            used = [0]

            def weights(c=KD, w=FB):
                n = used[0]
                pe.wait_ge(slot_full[n % SLOTS], 16 * (n // SLOTS + 1))
                used[0] += 1
                return slot(n, c, w)

            def begin(label, b):
                s, n = bk.fill(label, b)
                if n > 0:
                    pe.wait_ge(s, n)

            def end(ins, label):
                ins.then_inc(bk.full_sem(label), 1)

            def turn(norm, tag, banks):
                for tt in range(NT):
                    pe.wait_ge(scaled, NT * norm + tt + 1)
                    for hf in range(2):
                        label = (tag, tt, hf)
                        begin(label, banks[2 * tt + hf])
                        for c in range(4):
                            k = 4 * hf + c
                            ins = pe.transpose(bank(banks[2 * tt + hf], c * P, (c + 1) * P),
                                               xn[:, tt, k * P:(k + 1) * P], ident[:, :])
                        end(ins, label)

            def turned(tag, tt=None):
                for u in range(NT):
                    if tt in (None, u):
                        for hf in range(2):
                            pe.wait_ge(*bk.empty((tag, u, hf)))

            def memory_kv(layer, srcT, banks):
                w = weights()
                begin(("kmT", layer), banks[0])
                for c in range(2):
                    for k in range(KD):
                        ins = pe.matmul(bank(banks[0], c * S, (c + 1) * S), w[:, k, c * P:(c + 1) * P],
                                        srcT[:, k, :], start=(k == 0), stop=(k == KD - 1))
                end(ins, ("kmT", layer))
                begin(("vm", layer), banks[1])
                for tt in range(NT):
                    for k in range(KD):
                        ins = pe.matmul(bank(banks[1], tt * 256, (tt + 1) * 256),
                                        srcT[:, k, tt * P:(tt + 1) * P], w[:, k, 256:512],
                                        start=(k == 0), stop=(k == KD - 1))
                end(ins, ("vm", layer))

            def rows(label, b, srcT, tt, w, lo, hi, at=0, first=True, last=True):
                if first:
                    begin(label, b)
                for k in range(KD):
                    ins = pe.matmul(bank(b, at, at + hi - lo), srcT[:, k, tt * P:(tt + 1) * P],
                                    w[:, k, lo:hi], start=(k == 0), stop=(k == KD - 1))
                if last:
                    end(ins, label)
                return ins

            def turned_cols(label, b, w, los):
                begin(label, b)
                for i, lo in enumerate(los):
                    for k in range(KD):
                        ins = pe.matmul(bank(b, i * S, (i + 1) * S), w[:, k, lo:lo + P], xT[:, k, :],
                                        start=(k == 0), stop=(k == KD - 1))
                end(ins, label)
                return ins

            def slot_done(label):
                free_after.append(bk.full(label))

            def scores(u, layer, i, tt, q, k, keys):
                lo, hi = keys
                for b in range(2):
                    begin(("s", u, b), 2 * (u % 2) + b)
                for s2 in range(2):
                    for b in range(2):
                        r = slice(HD * b, HD * b + HD)
                        kc = k[r, i if layer == 0 and i < NKV else s2, lo:hi]
                        qc = q[r, (2 * i if i < NKV else 0) + s2, tt * P:(tt + 1) * P]
                        ins = pe.matmul(bank(2 * (u % 2) + b, s2 * (hi - lo), (s2 + 1) * (hi - lo)), qc, kc,
                                        start=True, stop=True)
                        if s2 == 1:
                            end(ins, ("s", u, b))

            def turn_probs(u, nk):
                pe.wait_ge(norm_ok, u + 1)
                for b in range(2):
                    begin(("pT", u, b), 4 + b)
                    for s2 in range(2):
                        for kt in range(nk):
                            ins = pe.transpose(bank(4 + b, (s2 * 2 + kt) * P, (s2 * 2 + kt + 1) * P),
                                               probs[:, u % 2, b, s2, kt * P:(kt + 1) * P], ident[:, :])
                    end(ins, ("pT", u, b))

            def weigh(u, i, nk, val, kt0):
                begin(("o", u), 6 + u % 2)
                for b in range(2):
                    pe.wait_ge(*bk.empty(("pT", u, b)))
                for s2 in range(2):
                    for b in range(2):
                        h = (0 if i < NKV else 2 * s2 + b) * HD + (i * HD if i < NKV else 0)
                        for kt in range(nk):
                            ins = pe.matmul(psum[HD * b:HD * b + HD, 6 + u % 2, s2 * P:(s2 + 1) * P],
                                            val[:, kt0 + kt, h:h + HD], probsT[:, u % 2, b, s2, kt, :],
                                            start=(kt == 0), stop=(kt == nk - 1), skip_group_check=True)
                end(ins, ("o", u))

            def attend(units):
                for s in range(len(units) + 2):
                    if s < len(units):
                        u, layer, i, tt, q, k, keys, val, kt0 = units[s]
                        scores(u, layer, i, tt, q, k, keys)
                    if 1 <= s <= len(units):
                        u, keys = units[s - 1][0], units[s - 1][6]
                        turn_probs(u, (keys[1] - keys[0]) // P)
                    if s >= 2:
                        u, i, keys, val, kt0 = (units[s - 2][x] for x in (0, 2, 6, 7, 8))
                        weigh(u, i, (keys[1] - keys[0]) // P, val, kt0)

            def project_out(layer, last_unit_labels):
                for label in last_unit_labels:
                    pe.wait_ge(*bk.empty(label))
                for hf in range(2):
                    w = weights()
                    for tt in range(NT):
                        rows(("mix", layer, tt, hf), 2 * tt + hf, mixT, tt, w, 0, FB)
                    slot_done(("mix", layer, NT - 1, hf))

            pe.wait_ge(consts, 1)
            turn(MEM0, "mem0T", (0, 1, 2, 3))
            turned("mem0T")
            memory_kv(0, memT, (6, 7))
            slot_done(("vm", 0))
            turn(PRE0, "x0T", (0, 1, 2, 3))
            turned("x0T")
            wa = weights()
            for tt in range(NT):
                rows(("qa", tt), tt, xT, tt, wa, 0, 512)
            slot_done(("qa", 1))
            wb = weights()
            for tt in range(NT):
                rows(("qb", tt), 2 + tt, xT, tt, wb, 0, 512)
            slot_done(("qb", 1))
            wc = weights(KD, IN0[2][1] - IN0[2][0])
            for tt in range(NT):
                rows(("vc", tt), 6 + tt, xT, tt, wc, 0, P)
            turned_cols(("qcT", 0), 4, wc, (P, 2 * P))
            slot_done(("qcT", 0))
            for n, (tag, tt) in enumerate([("a", 0), ("a", 1), ("b", 0), ("b", 1)]):
                pe.wait_ge(roped, n + 1)
                label = ("qT", tag, tt)
                begin(label, 5 if n % 2 == 0 else 0)
                b = bk.at[label][0]
                for c in range(4 if tag == "a" else 2):
                    ins = pe.transpose(bank(b, c * P, (c + 1) * P), rope_q[:, n % 2, c * P:(c + 1) * P],
                                       ident[:, :])
                end(ins, label)
                if tag == "b":
                    label = ("kT", tt)
                    begin(label, 1 + tt)
                    for g in range(NKV):
                        ins = pe.transpose(bank(1 + tt, g * P, (g + 1) * P),
                                           kdup[:, tt, g, :, :].rearrange("p u c -> p (u c)"), ident[:, :])
                    end(ins, label)
            for label in [("qT", x, tt) for x in "ab" for tt in range(NT)] + \
                    [("kT", 0), ("kT", 1), ("qcT", 0), ("kmT", 0), ("vm", 0), ("vc", 0), ("vc", 1)]:
                pe.wait_ge(*bk.empty(label))
            attend(UNITS0)
            project_out(0, [("o", u[0]) for u in UNITS0[-2:]])

            turn(FPRE0, "f0T", (4, 5, 6, 7))
            turned("f0T")
            rot = [0]

            def gate_up(b, tt, w, kind):
                rows((kind, b, tt), 4 + rot[0] % 3, xT, tt, w, 0, FB)
                rot[0] += 1

            def turn_hidden(b, tt):
                pe.wait_ge(*bk.empty(("u0", b, tt)))
                begin(("h0T", b, tt), 7)
                for c in range(CB):
                    ins = pe.transpose(bank(7, c * P, (c + 1) * P), hid0[:, b % 2, tt, c * P:(c + 1) * P],
                                       ident[:, :])
                end(ins, ("h0T", b, tt))

            def down(b, tt, w):
                if b == 0:
                    for hf in range(2):
                        begin(("y0", tt, hf), 2 * tt + hf)
                pe.wait_ge(*bk.empty(("h0T", b, tt)))
                for hf in range(2):
                    for c in range(CB):
                        ins = pe.matmul(bank(2 * tt + hf), hidT0[:, tt, c * P:(c + 1) * P],
                                        w[:, c, hf * 512:(hf + 1) * 512], start=(b == 0 and c == 0),
                                        stop=(b == NB - 1 and c == CB - 1), skip_group_check=True)
                    if b == NB - 1:
                        end(ins, ("y0", tt, hf))
                return ins

            for b in range(NB + 1):
                if b < NB:
                    wg, wu = weights(), weights()
                    gate_up(b, 0, wg, "g0")
                    gate_up(b, 0, wu, "u0")
                if b >= 1:
                    turn_hidden(b - 1, 0)
                if b < NB:
                    gate_up(b, 1, wg, "g0")
                if b >= 1:
                    wd = weights(CB, D)
                    down(b - 1, 0, wd)
                    turn_hidden(b - 1, 1)
                if b < NB:
                    gate_up(b, 1, wu, "u0")
                    slot_done(("g0", b, 1))
                    slot_done(("u0", b, 1))
                if b == NB:
                    down(b - 1, 1, wd)
                    slot_done(("y0", 1, 1))
                elif b >= 1:
                    down(b - 1, 1, wd).then_inc(downs, 1)
                    free_after.append((downs, b))

            turn(MEM1, "mem1T", (4, 5, 6, 7))
            turned("mem1T")
            memory_kv(1, memT, (4, 5))
            slot_done(("vm", 1))
            turn(PRE1, "x1T", (0, 1, 2, 3))
            turned("x1T")
            wa = weights()
            turned_cols(("p", 0), 6, wa, (0, 128))
            turned_cols(("p", 1), 7, wa, (256, 384))
            slot_done(("p", 1))
            wb = weights()
            turned_cols(("p", 2), 4, wb, (0, 128))
            turned_cols(("p", 3), 5, wb, (256, 384))
            slot_done(("p", 3))
            wc = weights()
            turned_cols(("p", 4), 6, wc, (0, 128))
            turned_cols(("p", 5), 7, wc, (256, 384))
            slot_done(("p", 5))
            wd = weights()
            for tt in range(NT):
                rows(("v1a", tt), tt, xT, tt, wd, 0, 512)
            slot_done(("v1a", 1))
            we = weights()
            for tt in range(NT):
                rows(("v1b", tt), 2 + tt, xT, tt, we, 0, 256)
            turned_cols(("qcT", 1), 4, we, (256, 384))
            slot_done(("qcT", 1))

            def stick_scores(p):
                for b in range(2):
                    bb = 2 * (p % 3) + b
                    begin(("z", p, b), bb)
                    r = slice(HD * b, HD * b + HD)
                    pe.matmul(bank(bb, 0, 256), kT[r, p, 0:P], qT[r, p, :], start=True, stop=False,
                              skip_group_check=True)
                    ins = pe.matmul(bank(bb, 256, 384), kT[r, p, P:2 * P], qT[r, p, P:2 * P], start=False,
                                    stop=False, skip_group_check=True)
                    end(ins, ("z", p, b))

            def stick_sum(p):
                pe.wait_ge(soft_b, p + 1)
                for b in range(2):
                    bb = 2 * (p % 3) + b
                    begin(("zc", p, b), bb)
                    pe.matmul(bank(bb, 0, 256), upper_neg[:, :], soft[:, p % 2, b, 0:256], start=False,
                              stop=False, skip_group_check=True)
                    pe.matmul(bank(bb, P, 2 * P), ones_neg[:, :], soft[:, p % 2, b, 256:384], start=False,
                              stop=False, skip_group_check=True)
                    ins = pe.matmul(bank(bb, 256, 384), upper_neg[:, :], soft[:, p % 2, b, 256:384],
                                    start=False, stop=True, skip_group_check=True)
                    end(ins, ("zc", p, b))

            def stick_weigh(p):
                pe.wait_ge(stick_b, p + 1)
                begin(("os", p), 6 + p % 2)
                for b in range(2):
                    h = (2 * p + b) * HD
                    o = psum[HD * b:HD * b + HD, 6 + p % 2, :]
                    pe.matmul(o[:, 0:256], v[:, 0, h:h + HD], stick[:, p % 2, b, 0:256], start=True,
                              stop=False, skip_group_check=True)
                    ins = pe.matmul(o[:, P:2 * P], v[:, 1, h:h + HD], stick[:, p % 2, b, 256:384],
                                    start=False, stop=True, skip_group_check=True)
                end(ins, ("os", p))

            for label in [("p", i) for i in range(6)] + [("v1a", 0), ("v1a", 1), ("v1b", 0), ("v1b", 1)]:
                pe.wait_ge(*bk.empty(label))
            NP = NH // 2
            for s in range(NP + 2):
                if s < NP:
                    stick_scores(s)
                if 1 <= s <= NP:
                    stick_sum(s - 1)
                if s >= 2:
                    stick_weigh(s - 2)
            for label in [("qcT", 1), ("kmT", 1), ("vm", 1)]:
                pe.wait_ge(*bk.empty(label))
            attend(UNITS1)
            project_out(1, [("os", NP - 1), ("os", NP - 2)] + [("o", u[0]) for u in UNITS1])

            turn(FPRE1, "f1T", (4, 5, 6, 7))
            turned("f1T")
            pe.wait_ge(small_in, 16 * 3)
            begin(("logits",), 4)
            for tt in range(NT):
                for k in range(KD):
                    ins = pe.matmul(bank(4, tt * NE, (tt + 1) * NE), xT[:, k, tt * P:(tt + 1) * P],
                                    wr[:, k, :], start=(k == 0), stop=(k == KD - 1))
            end(ins, ("logits",))
            pe.wait_ge(chosen_ok, 1)
            begin(("rank",), 5)
            pe.matmul(bank(5, 0, NE), before[:, :], chosen[:, 0, :], start=True, stop=True)
            pe.matmul(bank(5, NE, 2 * NE), ones[:, :], chosen[:, 0, :], start=True, stop=False)
            pe.matmul(bank(5, NE, 2 * NE), before[:, :], chosen[:, 1, :], start=False, stop=True)
            pe.matmul(bank(5, 2 * NE, 3 * NE), ones[:, :], chosen[:, 0, :], start=True, stop=False)
            ins = pe.matmul(bank(5, 2 * NE, 3 * NE), ones[:, :], chosen[:, 1, :], start=False, stop=True)
            end(ins, ("rank",))

            def gather(labels, waits):
                for hf in range(2):
                    s, n = waits[hf]
                    pe.wait_ge(s, n)
                    for c in range(4):
                        k = 4 * hf + c
                        for tt in range(NT):
                            ins = pe.matmul(bank(4 + hf, c * P, (c + 1) * P), xn[:, tt, k * P:(k + 1) * P],
                                            pick[:, tt, :], start=(tt == 0), stop=(tt == NT - 1))
                    end(ins, labels[hf])

            pe.wait_ge(pick_ok, 1)
            gather([("pre-gather", 0), ("pre-gather", 1)],
                   [bk.fill(("pre-gather", hf), 4 + hf) for hf in range(2)])
            base = list(bk.count)
            pe.wait_ge(tables_ok, 1)
            n_jobs = pe.value_load(job_i[0:1, 3:4], min_val=NE, max_val=MAX_JOBS)
            for hf in range(2):
                pe.wait_ge(*bk.empty(("pre-gather", hf)))
            with pe.Fori(0, n_jobs) as j:
                def jbegin(label, b):
                    pe.wait_ge(*bk.fill(label, b, j))

                def jslot(n, c=KD, w=FB):
                    pe.wait_ge(slot_full[n % SLOTS], (16 * 3) * j + 16 * (PRE // SLOTS + n // SLOTS + 1))
                    return slot(n, c, w)

                def expert_rows(kind, b):
                    label = (kind, b)
                    bb = 2 + 2 * (b % 2) + (kind == "u")
                    w = jslot(place[kind, b])
                    jbegin(label, bb)
                    for k in range(KD):
                        ins = pe.matmul(bank(bb), picked[:, k, :], w[:, k, :], start=(k == 0),
                                        stop=(k == KD - 1))
                    end(ins, label)
                    job_free[place[kind, b]] = label

                def expert_turn(b):
                    jbegin(("T", b), 7)
                    pe.wait_ge(*bk.empty(("u", b), j))
                    for c in range(CB):
                        ins = pe.transpose(bank(7, c * P, (c + 1) * P), hid1[:, b % 2, c * P:(c + 1) * P],
                                           ident[:, :])
                    end(ins, ("T", b))

                def expert_down(b):
                    w = jslot(place["d", b], CB, D)
                    if b == 0:
                        for hf in range(2):
                            jbegin(("y", hf), hf)
                    pe.wait_ge(*bk.empty(("T", b), j))
                    for hf in range(2):
                        for c in range(CB):
                            ins = pe.matmul(bank(hf), hidT1[:, c * P:(c + 1) * P],
                                            w[:, c, hf * 512:(hf + 1) * 512], start=(b == 0 and c == 0),
                                            stop=(b == NB - 1 and c == CB - 1), skip_group_check=True)
                        if b == NB - 1:
                            end(ins, ("y", hf))
                    if b < NB - 1:
                        ins.then_inc(downs, 1)
                        job_free[place["d", b]] = NB + b
                    else:
                        job_free[place["d", b]] = ("y", 1)

                for b in range(NB):
                    expert_rows("g", b)
                    expert_rows("u", b)
                    if b == 0:
                        jbegin(("pickT",), 6)
                        for tt in range(NT):
                            ins = pe.transpose(bank(6, tt * P, (tt + 1) * P), pick[:, tt, :], ident[:, :])
                        end(ins, ("pickT",))
                    if b >= 1:
                        expert_turn(b - 1)
                    if b >= 1:
                        expert_down(b - 1)
                expert_turn(NB - 1)
                expert_down(NB - 1)
                pe.wait_ge(pick_ok, j + 2)
                gather([("gather", 0), ("gather", 1)],
                       [bk.fill(("gather", hf), 4 + hf, j) for hf in range(2)])
                pe.wait_ge(*bk.empty(("pickT",), j))
                for hf in range(2):
                    pe.wait_ge(*bk.empty(("y", hf), j))
                for i, (tt, hf, bb) in enumerate([(0, 0, 6), (0, 1, 7), (1, 0, 4), (1, 1, 5)]):
                    jbegin(("back", tt, hf), bb)
                    ins = pe.matmul(bank(bb), pickT[:, tt, :], y_sb[:, hf * 512:(hf + 1) * 512],
                                    start=True, stop=True)
                    end(ins, ("back", tt, hf))
                for hf in range(2):
                    pe.wait_ge(*bk.empty(("gather", hf), j))
            assert tuple(bk.count[b] - base[b] for b in range(8)) == TURN

        @block.scalar
        def _(act):
            links = [0]

            def link(ins):
                links[0] += 1
                ins.then_inc(act_chain, 1)
                act.wait_ge(act_chain, links[0])

            def copy(label, out, src, scale=None):
                act.wait_ge(*bk.full(label))
                act.activation(out, src, ACT.Copy, scale=1.0 if scale is None else scale)\
                    .then_inc(bk.empty_sem(label), 1)

            def square_sum(norm, tt, out, src):
                act.activation(out, src, ACT.Square, accum_out=ssq[:, norm, tt:tt + 1]).then_inc(summed, 1)

            def drain_turned(tag, dst, banks_half=0):
                for tt in range(NT):
                    label = (tag, tt, 0)
                    copy(label, dst[:, 0:4, tt * P:(tt + 1) * P],
                         bank(bk.at[label][0]).rearrange("p (c s) -> p c s", c=4))

            def exps(u, i, layer, nk):
                act.wait_ge(max_ok, u + 1)
                for b in range(2):
                    for s2 in range(2):
                        x = probs[:, u % 2, b, s2, 0:nk * P]
                        ins = act.activation(x, x, ACT.Exp, bias=nmax[:, u, 2 * s2 + b:2 * s2 + b + 1],
                                             accum_out=psum_e[:, u, 2 * s2 + b:2 * s2 + b + 1])
                if layer == 0 and i < NKV:
                    ins = act.activation(esink[:, u, :], esink[:, u, :], ACT.Exp)
                ins.then_inc(exp_ok, 1)

            def attend(units):
                for s in range(len(units) + 2):
                    if s < len(units):
                        u, layer, i, keys = (units[s][x] for x in (0, 1, 2, 6))
                        exps(u, i, layer, (keys[1] - keys[0]) // P)
                    if 1 <= s <= len(units):
                        u, keys = units[s - 1][0], units[s - 1][6]
                        nk = (keys[1] - keys[0]) // P
                        copy(("pT", u, 0), probsT[:, u % 2, 0, :, 0:nk, :],
                             bank(4).rearrange("p (h k q) -> p h k q", h=2, k=2)[:, :, 0:nk, :])
                    if s >= 2:
                        u, i, tt = (units[s - 2][x] for x in (0, 2, 3))
                        c = 2 * i
                        copy(("o", u), mixT[:, c:c + 2, tt * P:(tt + 1) * P],
                             bank(6 + u % 2, 0, 256).rearrange("p (c s) -> p c s", c=2))

            act.wait_ge(mem_in, 16)
            for tt in range(NT):
                square_sum(MEM0, tt, xn[:, tt, :], memb[:, tt, :])
            drain_turned("mem0T", memT)
            act.wait_ge(x_in, 16)
            for tt in range(NT):
                act.wait_ge(*bk.full(("mem0T", tt, 1)))
                square_sum(PRE0, tt, xn[:, tt, :], hres[:, tt, :])
            act.wait_ge(angles, 1)
            act.wait_ge(consts, 1)
            act.activation(rope_s[:, 2, :, :], rope_s[:, 0, :, :], ACT.Sin)
            act.activation(rope_s[:, 3, :, :], rope_s[:, 1, :, :], ACT.Sin, scale=-1.0,
                           bias=halfpi[:, 0:1]).then_inc(sines, 1)
            copy(("kmT", 0), kmT, bank(6).rearrange("p (c s) -> p c s", c=2))
            copy(("vm", 0), vm, bank(7).rearrange("p (c s) -> p c s", c=2))
            drain_turned("x0T", xT)
            for tt in range(NT):
                copy(("vc", tt), v[:, tt, 64:192], bank(6 + tt, 0, 128))
            copy(("qcT", 0), qcT, bank(4).rearrange("p (c s) -> p c s", c=2))
            for tag in "ab":
                for tt in range(NT):
                    label = ("qT", tag, tt)
                    n = 4 if tag == "a" else 2
                    copy(label, qT[:, 0:4, tt * P:(tt + 1) * P] if tag == "a" else
                         qT[:, 4:6, tt * P:(tt + 1) * P],
                         bank(bk.at[label][0], 0, n * P).rearrange("p (c s) -> p c s", c=n))
            attend(UNITS0)

            def post_norm(norm, labels, src, out):
                for tt in range(NT):
                    for label in labels[tt]:
                        act.wait_ge(*bk.full(label))
                    square_sum(norm, tt, out[:, tt, :], src(tt))

            two_banks = lambda tt: psum[:, 2 * tt:2 * tt + 2, :].rearrange("p a b -> p (a b)")
            post_norm(POST0, [[("mix", 0, tt, hf) for hf in range(2)] for tt in range(NT)], two_banks, xn)

            def pre_norm(norm, n_added):
                for tt in range(NT):
                    act.wait_ge(added, n_added + tt + 1)
                    square_sum(norm, tt, xn[:, tt, :], hres[:, tt, :])

            pre_norm(FPRE0, 0)
            drain_turned("f0T", xT)
            for tt in range(NT):
                act.wait_ge(*bk.full(("f0T", tt, 1)))
                square_sum(MEM1, tt, xn[:, tt, :], memb[:, tt, :])

            for b in range(NB + 1):
                for tt in range(NT):
                    if b < NB:
                        label = ("g0", b, tt)
                        act.wait_ge(*bk.full(label))
                        act.activation(act0[:, tt, :], bank(bk.at[label][0]), ACT.Silu)\
                            .then_inc(bk.empty_sem(label), 1)
                    if b >= 1:
                        copy(("h0T", b - 1, tt), hidT0[:, tt, :], bank(7))
            drain_turned("mem1T", memT)
            post_norm(FPOST0, [[("y0", tt, hf) for hf in range(2)] for tt in range(NT)], two_banks,
                      mixT[:, :, :].rearrange("p (t a) s -> p t (a s)", t=NT))
            copy(("kmT", 1), kmT, bank(4).rearrange("p (c s) -> p c s", c=2))
            copy(("vm", 1), vm, bank(5).rearrange("p (c s) -> p c s", c=2))
            pre_norm(PRE1, 2)
            drain_turned("x1T", xT)

            def heads(i, dst, scale=None):
                copy(("p", i), dst, bank(bk.at["p", i][0]).rearrange("p (c s) -> p c s", c=2), scale)

            heads(0, qT[:, 0:2, :], SCALE)
            heads(2, qT[:, 4:6, :], SCALE)
            heads(4, kT[:, 2:4, :])
            copy(("v1a", 0), v[:, 0, 0:512], bank(0))
            copy(("v1b", 0), v[:, 0, 512:768], bank(2, 0, 256))
            copy(("qcT", 1), qcT, bank(4).rearrange("p (c s) -> p c s", c=2))

            def z_view(p):
                return psum[:, 2 * (p % 3):2 * (p % 3) + 2, 0:384]

            def log_terms(p):
                for b in range(2):
                    act.wait_ge(*bk.full(("z", p, b)))
                x = soft[:, p % 2, :, :]
                if p >= 2:
                    act.wait_ge(*bk.full(("zc", p - 2, 1)))
                link(act.activation(x, z_view(p), ACT.Abs))
                link(act.activation(x, x, ACT.Exp, scale=-1.0))
                act.activation(x, x, ACT.Ln, bias=1.0).then_inc(soft_a, 1)

            def stick_exp(p):
                for b in range(2):
                    act.wait_ge(*bk.full(("zc", p, b)))
                if p >= 2:
                    act.wait_ge(*bk.full(("os", p - 2)))
                for b in range(2):
                    ins = act.activation(stick[:, p % 2, b, :], bank(2 * (p % 3) + b, 0, 384), ACT.Exp)
                    ins.then_inc(bk.empty_sem(("zc", p, b)), 1)

            NP = NH // 2
            for s in range(NP + 2):
                if s < NP:
                    log_terms(s)
                if 1 <= s <= NP:
                    stick_exp(s - 1)
                if s >= 2:
                    copy(("os", s - 2), mixT[:, s - 2, :], bank(6 + s % 2, 0, 256))
            attend(UNITS1)
            post_norm(POST1, [[("mix", 1, tt, hf) for hf in range(2)] for tt in range(NT)], two_banks, xn)
            pre_norm(FPRE1, 4)
            drain_turned("f1T", xT)

            act.wait_ge(gap_ok, 1)
            act.activation(gate2[:, :, 1:2], gate2[:, :, 0:1], ACT.Exp).then_inc(gexp_ok, 1)

            copy(("pre-gather", 0), picked[:, 0:4, :], bank(4).rearrange("p (k s) -> p k s", k=4))
            act.wait_ge(tables_ok, 1)
            n_jobs = act.value_load(job_i[0:1, 3:4], min_val=NE, max_val=MAX_JOBS)
            with act.Fori(0, n_jobs) as j:
                def full(label):
                    act.wait_ge(*bk.full(label, j))

                def jcopy(label, out, src):
                    full(label)
                    act.activation(out, src, ACT.Copy).then_inc(bk.empty_sem(label), 1)

                for b in range(NB):
                    full(("g", b))
                    act.activation(act1[:, b % 2, :], bank(bk.at["g", b][0]), ACT.Silu)\
                        .then_inc(bk.empty_sem(("g", b)), 1)
                    if b == 0:
                        jcopy(("pickT",), pickT, bank(6, 0, 256).rearrange("p (t s) -> p t s", t=NT))
                    if b >= 1:
                        jcopy(("T", b - 1), hidT1, bank(7))
                jcopy(("T", NB - 1), hidT1, bank(7))
                jcopy(("y", 0), y_sb[:, 0:512], bank(0))
                jcopy(("gather", 0), picked[:, 0:4, :], bank(4).rearrange("p (k s) -> p k s", k=4))
            act.wait_ge(tables_ok, 2)
            for tt in range(NT):
                square_sum(FPOST1, tt, xn[:, tt, :], esum[:, tt, :])

        @block.vector
        def _(dve):
            links = [0]

            def link(ins):
                links[0] += 1
                ins.then_inc(dve_chain, 1)
                dve.wait_ge(dve_chain, links[0])

            def copy(label, out, src, scale=None):
                dve.wait_ge(*bk.full(label))
                ins = dve.tensor_copy(out, src) if scale is None else \
                    dve.tensor_scalar(out, src, scale, None, ALU.mult)
                ins.then_inc(bk.empty_sem(label), 1)

            def scale_rows(norm, tt, out, src, labels=()):
                if tt == 0:
                    dve.wait_ge(gain_in[norm % NG], 16 * (norm // NG + 1))
                dve.wait_ge(rstd_ok, NT * norm + tt + 1)
                ins = dve.scalar_tensor_tensor(out=out, in0=src, scalar=rstd[:, norm, tt:tt + 1],
                                               in1=gains[:, norm % NG, :], op0=ALU.mult, op1=ALU.mult)
                ins.then_inc(scaled, 1)
                dve.wait_ge(scaled, NT * norm + tt + 1)

            def drain_turned(tag, dst):
                for tt in range(NT):
                    label = (tag, tt, 1)
                    copy(label, dst[:, 4:8, tt * P:(tt + 1) * P],
                         bank(bk.at[label][0]).rearrange("p (c s) -> p c s", c=4))

            def post_norm(norm, labels, src, out):
                for tt in range(NT):
                    scale_rows(norm, tt, out[:, tt, :], src(tt))
                    for label in labels[tt]:
                        dve.sem_inc(bk.empty_sem(label), 1)
                    dve.tensor_tensor(hres[:, tt, :], hres[:, tt, :], out[:, tt, :], ALU.add)\
                        .then_inc(added, 1)

            def pre_norm(norm, src):
                for tt in range(NT):
                    scale_rows(norm, tt, xn[:, tt, :], src[:, tt, :])

            def row_max(u, layer, i, tt, nk):
                for b in range(2):
                    dve.wait_ge(*bk.full(("s", u, b)))
                if u >= 2 and u != UNITS1[0][0] and u != UNITS1[1][0]:
                    for b in range(2):
                        dve.wait_ge(*bk.full(("pT", u - 2, b)))
                K = nk * P
                mask = band[:, 2 * P - K:2 * P]
                for b in range(2):
                    x = probs[:, u % 2, b, :, 0:K]
                    src = bank(2 * (u % 2) + b, 0, 2 * K).rearrange("p (h k) -> p h k", h=2)
                    if layer == 0 and i < NKV:
                        ins = dve.scalar_tensor_tensor(out=x, in0=src, scalar=SCALE,
                                                       in1=mask.unsqueeze(1).to_broadcast((P, 2, K)),
                                                       op0=ALU.mult, op1=ALU.add)
                    else:
                        ins = dve.tensor_scalar(x, src, SCALE, None, ALU.mult)
                    ins.then_inc(bk.empty_sem(("s", u, b)), 1)
                for b in range(2):
                    dve.wait_ge(*bk.empty(("s", u, b)))
                for b in range(2):
                    ins = dve.tensor_reduce(nmax[:, u, b:4:2], probs[:, u % 2, b, :, 0:K], AX.X, ALU.max)
                link(ins)
                if layer == 0 and i < NKV:
                    link(dve.scalar_tensor_tensor(out=nmax[:, u, :], in0=nmax[:, u, :], scalar=-1.0,
                                                  in1=nsinks[:, 4 * i:4 * i + 4], op0=ALU.mult, op1=ALU.min))
                    dve.tensor_tensor(esink[:, u, :], nmax[:, u, :], sinks[:, 4 * i:4 * i + 4], ALU.add)\
                        .then_inc(max_ok, 1)
                else:
                    dve.tensor_scalar(nmax[:, u, :], nmax[:, u, :], -1.0, None, ALU.mult).then_inc(max_ok, 1)

            def normalise(u, layer, i, nk):
                dve.wait_ge(exp_ok, u + 1)
                if layer == 0 and i < NKV:
                    link(dve.tensor_tensor(psum_e[:, u, :], psum_e[:, u, :], esink[:, u, :], ALU.add))
                link(dve.reciprocal(recip[:, u, :], psum_e[:, u, :]))
                for b in range(2):
                    x = probs[:, u % 2, b, :, 0:nk * P]
                    ins = dve.tensor_tensor(x, x, recip[:, u, b:4:2].unsqueeze(2).to_broadcast((P, 2, nk * P)),
                                            ALU.mult)
                ins.then_inc(norm_ok, 1)

            def attend(units):
                for s in range(len(units) + 2):
                    if s < len(units):
                        u, layer, i, tt, keys = (units[s][x] for x in (0, 1, 2, 3, 6))
                        row_max(u, layer, i, tt, (keys[1] - keys[0]) // P)
                    if 1 <= s <= len(units):
                        u, layer, i, keys = (units[s - 1][x] for x in (0, 1, 2, 6))
                        nk = (keys[1] - keys[0]) // P
                        normalise(u, layer, i, nk)
                        copy(("pT", u, 1), probsT[:, u % 2, 1, :, 0:nk, :],
                             bank(5).rearrange("p (h k q) -> p h k q", h=2, k=2)[:, :, 0:nk, :])

            dve.wait_ge(small_in, 16 * 3)
            dve.wait_ge(consts, 1)
            link(dve.tensor_copy(pos_f[:, :], pos_i[:, :]))
            dve.tensor_scalar(nsinks[:, :], sinks[:, :], -1.0, None, ALU.mult)
            for tt in range(NT):
                ins = dve.tensor_scalar(rope_s[:, 0, tt, :], invf[:, :], pos_f[:, tt:tt + 1], None, ALU.mult)
            link(ins)
            a, n = rope_s[:, 0, :, :], rope_s[:, 1, :, :]
            link(dve.tensor_scalar(n, a, 1.0 / TWO_PI, ROUND, ALU.mult, ALU.add))
            link(dve.tensor_scalar(n, n, -ROUND, None, ALU.add))
            for part in (TP1, TP2, TP3):
                link(dve.scalar_tensor_tensor(out=a, in0=n, scalar=-part, in1=a, op0=ALU.mult, op1=ALU.add))
            link(dve.tensor_scalar(a, a, 3.1415925, -3.1415925, ALU.min, ALU.max))
            link(dve.tensor_scalar(n, a, -1.0, None, ALU.mult))
            dve.tensor_tensor(n, a, n, ALU.max).then_inc(angles, 1)

            for tt in range(NT):
                scale_rows(MEM0, tt, xn[:, tt, :], memb[:, tt, :])
            drain_turned("mem0T", memT)
            pre_norm(PRE0, hres)
            drain_turned("x0T", xT)
            dve.wait_ge(sines, 1)
            H2 = HD // 2
            for half in range(2):
                dve.tensor_copy(cos2[:, :, half * H2:(half + 1) * H2], rope_s[:, 3, :, :])
            dve.tensor_scalar(sin2[:, :, 0:H2], rope_s[:, 2, :, :], -1.0, None, ALU.mult)
            link(dve.tensor_copy(sin2[:, :, H2:HD], rope_s[:, 2, :, :]))

            for n, (tag, tt) in enumerate([("a", 0), ("a", 1), ("b", 0), ("b", 1)]):
                label = ("q" + tag, tt)
                nh = 8 if tag == "a" else 7
                bb = bk.at[label][0]
                x = bank(bb, 0, nh * HD).rearrange("p (h c) -> p h c", c=HD)
                ra = rope_a[:, 0:nh * HD].rearrange("p (h c) -> p h c", c=HD)
                rb = rope_b[:, 0:nh * HD].rearrange("p (h c) -> p h c", c=HD)
                dve.wait_ge(*bk.full(label))
                dve.tensor_tensor(ra, x, cos2[:, tt, :].unsqueeze(1).to_broadcast((P, nh, HD)), ALU.mult)
                dve.tensor_tensor(rb[:, :, 0:H2], x[:, :, H2:HD],
                                  sin2[:, tt, 0:H2].unsqueeze(1).to_broadcast((P, nh, H2)), ALU.mult)
                ins = dve.tensor_tensor(rb[:, :, H2:HD], x[:, :, 0:H2],
                                        sin2[:, tt, H2:HD].unsqueeze(1).to_broadcast((P, nh, H2)), ALU.mult)
                if tag == "b":
                    ins = dve.tensor_copy(v[:, tt, 0:64], bank(bb, 448, 512))
                ins.then_inc(bk.empty_sem(label), 1)
                dve.wait_ge(*bk.empty(label))
                if n >= 2:
                    dve.wait_ge(*bk.full(("qT", "a", n - 2)))
                nq = 8 if tag == "a" else 4
                ins = dve.tensor_tensor(rope_q[:, n % 2, 0:nq * HD], rope_a[:, 0:nq * HD],
                                        rope_b[:, 0:nq * HD], ALU.add)
                if tag == "b":
                    for dup in range(2):
                        ins = dve.tensor_tensor(kdup[:, tt, :, dup, :], ra[:, 4:7, :], rb[:, 4:7, :], ALU.add)
                ins.then_inc(roped, 1)
                dve.wait_ge(roped, n + 1)
            for tt in range(NT):
                copy(("kT", tt), kT[:, 0:NKV, tt * P:(tt + 1) * P],
                     bank(1 + tt, 0, NKV * P).rearrange("p (c s) -> p c s", c=NKV))
            attend(UNITS0)

            two_banks = lambda tt: psum[:, 2 * tt:2 * tt + 2, :].rearrange("p a b -> p (a b)")
            post_norm(POST0, [[("mix", 0, tt, hf) for hf in range(2)] for tt in range(NT)], two_banks, xn)
            pre_norm(FPRE0, hres)
            drain_turned("f0T", xT)
            pre_norm(MEM1, memb)

            for b in range(NB):
                for tt in range(NT):
                    label = ("u0", b, tt)
                    dve.wait_ge(*bk.empty(("g0", b, tt)))
                    dve.wait_ge(*bk.full(label))
                    dve.tensor_tensor(hid0[:, b % 2, tt, :].rearrange("p (c q) -> p q c", c=CB),
                                      act0[:, tt, :].rearrange("p (q c) -> p q c", c=CB),
                                      bank(bk.at[label][0]).rearrange("p (q c) -> p q c", c=CB),
                                      ALU.mult).then_inc(bk.empty_sem(label), 1)
            drain_turned("mem1T", memT)
            post_norm(FPOST0, [[("y0", tt, hf) for hf in range(2)] for tt in range(NT)], two_banks,
                      mixT[:, :, :].rearrange("p (t a) s -> p t (a s)", t=NT))
            pre_norm(PRE1, hres)
            drain_turned("x1T", xT)

            def heads(i, dst, scale=None):
                copy(("p", i), dst, bank(bk.at["p", i][0]).rearrange("p (c s) -> p c s", c=2), scale)

            heads(1, qT[:, 2:4, :], SCALE)
            heads(3, kT[:, 0:2, :])
            heads(5, kT[:, 4:6, :])
            copy(("v1a", 1), v[:, 1, 0:512], bank(1))
            copy(("v1b", 1), v[:, 1, 512:768], bank(3, 0, 256))

            def softplus(p):
                x = soft[:, p % 2, :, :]
                dve.wait_ge(soft_a, p + 1)
                for b in range(2):
                    dve.scalar_tensor_tensor(out=x[:, b, :], in0=bank(2 * (p % 3) + b, 0, 384), scalar=0.0,
                                             in1=x[:, b, :], op0=ALU.max, op1=ALU.add)\
                        .then_inc(bk.empty_sem(("z", p, b)), 1)
                for b in range(2):
                    dve.wait_ge(*bk.empty(("z", p, b)))
                clear(x).then_inc(soft_b, 1)

            def clear(x):
                dve.tensor_tensor(x[:, :, 0:P], x[:, :, 0:P], clamp[:, :].unsqueeze(1).to_broadcast((P, 2, P)),
                                  ALU.min)
                return dve.tensor_tensor(x[:, :, 2 * P:3 * P], x[:, :, 2 * P:3 * P],
                                         clamp[:, :].unsqueeze(1).to_broadcast((P, 2, P)), ALU.min)

            NP = NH // 2
            for s in range(NP + 1):
                if s < NP:
                    softplus(s)
                if s >= 1:
                    for b in range(2):
                        dve.wait_ge(*bk.empty(("zc", s - 1, b)))
                    clear(stick[:, (s - 1) % 2, :, :]).then_inc(stick_b, 1)
            attend(UNITS1)
            post_norm(POST1, [[("mix", 1, tt, hf) for hf in range(2)] for tt in range(NT)], two_banks, xn)
            pre_norm(FPRE1, hres)
            drain_turned("f1T", xT)

            dve.wait_ge(*bk.full(("logits",)))
            dve.tensor_copy(logits[:, :, :], bank(4, 0, NT * NE).rearrange("p (t e) -> p t e", t=NT))\
                .then_inc(bk.empty_sem(("logits",)), 1)
            dve.wait_ge(*bk.empty(("logits",)))
            for tt in range(NT):
                ins = dve.max(top_v[:, tt, :], logits[:, tt, :])
            link(ins)
            for tt in range(NT):
                dve.max_index(top_i[:, tt, :], top_v[:, tt, :], logits[:, tt, :])
            dve.tensor_tensor(gate2[:, :, 0:1], top_v[:, :, 1:2], top_v[:, :, 0:1], ALU.subtract)\
                .then_inc(gap_ok, 1)
            dve.wait_ge(gap_ok, 1)
            link(dve.tensor_copy(top_f[:, :, :], top_i[:, :, :]))
            for tt in range(NT):
                for c in range(2):
                    ins = dve.tensor_scalar(mask2[:, tt, c, :], iota_s[:, 0:NE], top_f[:, tt, c:c + 1], None,
                                            ALU.is_equal)
            link(ins)
            dve.tensor_tensor(chosen[:, :, :], mask2[:, :, 0, :], mask2[:, :, 1, :], ALU.add)\
                .then_inc(chosen_ok, 1)
            dve.wait_ge(gexp_ok, 1)
            link(dve.tensor_scalar(gate2[:, :, 2:3], gate2[:, :, 1:2], 1.0, None, ALU.add))
            link(dve.reciprocal(gate2[:, :, 2:3], gate2[:, :, 2:3]))
            link(dve.tensor_tensor(gate2[:, :, 3:4], gate2[:, :, 1:2], gate2[:, :, 2:3], ALU.mult))
            for tt in range(NT):
                ins = dve.tensor_scalar(gates[:, tt, :], mask2[:, tt, 0, :], gate2[:, tt, 2:3], None, ALU.mult)
            link(ins)
            for tt in range(NT):
                ins = dve.scalar_tensor_tensor(out=gates[:, tt, :], in0=mask2[:, tt, 1, :],
                                               scalar=gate2[:, tt, 3:4], in1=gates[:, tt, :],
                                               op0=ALU.mult, op1=ALU.add)
            link(ins)
            dve.wait_ge(*bk.full(("rank",)))
            dve.tensor_copy(over[:, 0, :], bank(5, 2 * NE, 3 * NE))
            dve.scalar_tensor_tensor(out=rank[:, :, :], in0=bank(5, 0, NT * NE).rearrange("p (t e) -> p t e", t=NT),
                                     scalar=1.0, in1=chosen[:, :, :], op0=ALU.add, op1=ALU.mult)\
                .then_inc(bk.empty_sem(("rank",)), 1)
            dve.wait_ge(*bk.empty(("rank",)))
            dve.memset(slot_of[:, :, NE + 3:MAX_JOBS + 1], -1.0)
            dve.memset(gate_of[:, :, NE + 3:MAX_JOBS + 1], 0.0)
            dve.tensor_scalar(slot_of[:, :, 0:NE], rank[:, :, :], -1.0, None, ALU.add)
            dve.tensor_copy(gate_of[:, :, 0:NE], gates[:, :, :])
            link(dve.tensor_scalar(over[:, 1, :], over[:, 0, :], float(CAP), None, ALU.is_gt))
            link(dve.tensor_tensor_scan(over[:, 2, :], ones[:, 0:NE], over[:, 1, :], 0.0, ALU.mult, ALU.add))
            for o in range(3):
                ins = dve.scalar_tensor_tensor(out=over_sel[:, o, :], in0=over[:, 2, :], scalar=float(o + 1),
                                               in1=over[:, 1, :], op0=ALU.is_equal, op1=ALU.mult)
            link(ins)
            for o in range(3):
                for tt in range(NT):
                    link(dve.scalar_tensor_tensor(out=junk8[:, 0:NE], in0=slot_of[:, tt, 0:NE],
                                                  scalar=-float(CAP), in1=over_sel[:, o, :], op0=ALU.add,
                                                  op1=ALU.mult, accum_out=slot_of[:, tt, NE + o:NE + o + 1]))
                    link(dve.scalar_tensor_tensor(out=junk8[:, 0:NE], in0=gates[:, tt, :], scalar=1.0,
                                                  in1=over_sel[:, o, :], op0=ALU.mult, op1=ALU.mult,
                                                  accum_out=gate_of[:, tt, NE + o:NE + o + 1]))
                link(dve.scalar_tensor_tensor(out=junk8[:, 0:NE], in0=iota_s[:, 0:NE], scalar=1.0,
                                              in1=over_sel[:, o, :], op0=ALU.mult, op1=ALU.mult,
                                              accum_out=job_f[:, o:o + 1]))
            link(dve.tensor_scalar(job_f[:, 3:4], over[:, 2, NE - 1:NE], float(NE), None, ALU.add))
            dve.tensor_copy(job_i[:, :], job_f[:, :]).then_inc(tables_ok, 1)

            for tt in range(NT):
                ins = dve.tensor_scalar(pick[:, tt, :], iota_s[:, :], slot_of[:, tt, 0:1], None, ALU.is_equal)
            ins.then_inc(pick_ok, 1)
            link(dve.memset(esum[:, :, :], 0.0))
            copy(("pre-gather", 1), picked[:, 4:8, :], bank(5).rearrange("p (k s) -> p k s", k=4))
            dve.wait_ge(tables_ok, 1)
            n_jobs = dve.value_load(job_i[0:1, 3:4], min_val=NE, max_val=MAX_JOBS)
            with dve.Fori(0, n_jobs) as j:
                def full(label):
                    dve.wait_ge(*bk.full(label, j))

                for b in range(NB):
                    dve.wait_ge(*bk.empty(("g", b), j))
                    full(("u", b))
                    dve.tensor_tensor(hid1[:, b % 2, :].rearrange("p (c q) -> p q c", c=CB),
                                      act1[:, b % 2, :].rearrange("p (q c) -> p q c", c=CB),
                                      bank(bk.at["u", b][0]).rearrange("p (q c) -> p q c", c=CB),
                                      ALU.mult).then_inc(bk.empty_sem(("u", b)), 1)
                    if b == 0:
                        full(("pickT",))
                        for tt in range(NT):
                            ins = dve.tensor_scalar(pick[:, tt, :], iota_s[:, :],
                                                    slot_of[:, tt, bass.ds(j + 1, 1)], None, ALU.is_equal)
                        ins.then_inc(pick_ok, 1)
                full(("y", 1))
                dve.tensor_copy(y_sb[:, 512:1024], bank(1)).then_inc(bk.empty_sem(("y", 1)), 1)
                full(("gather", 1))
                dve.tensor_copy(picked[:, 4:8, :], bank(5).rearrange("p (k s) -> p k s", k=4))\
                    .then_inc(bk.empty_sem(("gather", 1)), 1)
                for tt, hf in [(0, 0), (0, 1), (1, 0), (1, 1)]:
                    full(("back", tt, hf))
                    e = esum[:, tt, hf * 512:(hf + 1) * 512]
                    dve.scalar_tensor_tensor(out=e, in0=bank(bk.at["back", tt, hf][0]),
                                             scalar=gate_of[:, tt, bass.ds(j, 1)], in1=e, op0=ALU.mult,
                                             op1=ALU.add).then_inc(bk.empty_sem(("back", tt, hf)), 1)
            for label in [("back", tt, hf) for tt in range(NT) for hf in range(2)]:
                dve.wait_ge(*bk.empty(label, n_jobs - 1))
            dve.sem_inc(tables_ok, 1)
            for tt in range(NT):
                scale_rows(FPOST1, tt, xn[:, tt, :], esum[:, tt, :])
                dve.tensor_tensor(hres[:, tt, :], hres[:, tt, :], xn[:, tt, :], ALU.add).then_inc(added, 1)

        @block.gpsimd
        def _(pool):
            links = [0]

            def link(ins):
                links[0] += 1
                ins.then_inc(pool_chain, 1)
                pool.wait_ge(pool_chain, links[0])

            def load_gain(n):
                g = t[NORMS[n]].rearrange("(a d) -> a d", a=1).to_broadcast((P, D))
                pool.dma_start(gains[:, n % NG, :], g).then_inc(gain_in[n % NG], 16)

            for n in range(NG):
                load_gain(n)
            for m, val in ((ident, 0.0), (upper_neg, 0.0), (ones_neg, -1.0), (ones, 1.0), (before, 0.0),
                           (band, 0.0), (clamp, 0.0), (mhalf, -0.5), (halfpi, TWO_PI / 4)):
                pool.memset(m[:, :], val)
            for i in range(HD // 2):
                pool.memset(invf[:, i:i + 1], THETA ** (-2.0 * i / HD))
            link(pool.iota(iota_i[:, :], pattern=[[1, P]], base=0, channel_multiplier=0))
            pool.tensor_copy(iota_s[:, :], iota_i[:, :])

            def where(m, lo, cmp, fill, step, ch):
                x = m[:, lo:lo + P]
                return pool.affine_select(out=x, in_=x, compare_op=cmp, fill=fill, base=0, pattern=[[step, P]],
                                          channel_multiplier=ch)

            where(ident, 0, ALU.not_equal, 1.0, -1, 1)
            where(upper_neg, 0, ALU.is_gt, -1.0, 1, -1)
            where(before, 0, ALU.is_ge, 1.0, -1, 1)
            where(band, 0, ALU.is_gt, NEG, 1, -1)
            where(band, P, ALU.is_ge, NEG, -1, 1)
            link(where(clamp, 0, ALU.is_ge, BIG, -1, 1))
            pool.sem_inc(consts, 1)

            for norm in range(len(NORMS)):
                for tt in range(NT):
                    x = rstd[:, norm, tt:tt + 1]
                    pool.wait_ge(summed, NT * norm + tt + 1)
                    link(pool.tensor_scalar(x, ssq[:, norm, tt:tt + 1], 1.0 / D, EPS, ALU.mult, ALU.add))
                    pool.tensor_tensor(x, x, mhalf[:, 0:1], ALU.pow).then_inc(rstd_ok, 1)
                if norm + NG < len(NORMS):
                    pool.wait_ge(scaled, NT * (norm + 1))
                    load_gain(norm + NG)

        @block.sync
        def _(sp):
            sp.dma_start(memb[:, :, :], t["mem"].rearrange("a (t p) d -> p (a t) d", p=P)).then_inc(mem_in, 16)
            sp.dma_start(hres[:, :, :], t["x"].rearrange("a (t p) d -> p (a t) d", p=P)).then_inc(x_in, 16)
            with nc.allow_non_contiguous_dma(reason="256 positions and 12 sinks"):
                sp.dma_start(pos_i[:, :], t["positions"].rearrange("a (t p) -> p (a t)", p=P)).then_inc(small_in, 16)
                sp.dma_start(sinks[:, :], t["l0_sinks"].rearrange("(a h) -> a h", a=1).to_broadcast((P, NH)))\
                    .then_inc(small_in, 16)
                sp.dma_start(wr[:, :, :], t["l1_w_router"].rearrange("(k p) e -> p k e", p=P)).then_inc(small_in, 16)
            def load(n, src):
                _, c, w = src.shape
                sp.dma_start(slot(n, c, w), src).then_inc(slot_full[n % SLOTS], 16)

            for n, src in enumerate(loads):
                if n >= SLOTS:
                    sp.wait_ge(*free_after[n - SLOTS])
                load(n, src)

            def expert_load(e, n, wait_job):
                kind, b = {m: x for x, m in place.items()}[n]
                if wait_job is None:
                    sp.wait_ge(*free_after[PRE + n - SLOTS])
                else:
                    last = job_free[(n - SLOTS) % PER]
                    if isinstance(last, tuple):
                        sp.wait_ge(*bk.full(last, wait_job))
                    else:
                        sp.wait_ge(downs, last + (NB - 1) * wait_job)
                if kind == "d":
                    w = t["l1_w_down"][bass.ds(e, 1), b * FB:(b + 1) * FB, :]
                    src = w.rearrange("e (p c) n -> p (e c) n", c=CB)
                else:
                    w = t["l1_w_gate" if kind == "g" else "l1_w_up"]
                    src = w[bass.ds(e, 1), :, b * FB:(b + 1) * FB].rearrange("e (k p) n -> p (e k) n", p=P)
                load(n, src)

            for n in range(SLOTS):
                expert_load(0, n, None)
            with sp.Fori(0, NE - 1) as j:
                for n in range(SLOTS, PER):
                    expert_load(j, n, j)
                for n in range(SLOTS):
                    expert_load(j + 1, n, j)
            for n in range(SLOTS, PER):
                expert_load(NE - 1, n, NE - 1)
            sp.wait_ge(tables_ok, 1)
            n_jobs = sp.value_load(job_i[0:1, 3:4], min_val=NE, max_val=MAX_JOBS)
            with sp.If(n_jobs > NE):
                with sp.Fori(NE, n_jobs) as j:
                    e = sp.value_load(job_i[0:1, bass.ds(j - NE, 1)], min_val=0, max_val=NE - 1)
                    for n in range(PER):
                        expert_load(e, n, j - 1 if n < SLOTS else j)
            for tt in range(NT):
                sp.wait_ge(added, 6 + tt + 1)
                sp.dma_start(t["out"][0, tt * P:(tt + 1) * P, :], hres[:, tt, :]).then_inc(stored, 16)
            sp.wait_ge(stored, 16 * NT)


_INS = ["x", "mem", "positions", "l0_attn_pre_g", "l0_mem_g", "l0_w_in", "l0_w_mem_kv", "l0_sinks", "l0_w_out",
        "l0_attn_post_g", "l0_ffn_pre_g", "l0_w_gate", "l0_w_up", "l0_w_down", "l0_ffn_post_g",
        "l1_attn_pre_g", "l1_mem_g", "l1_w_in", "l1_w_mem_kv", "l1_w_out", "l1_attn_post_g", "l1_ffn_pre_g",
        "l1_w_router", "l1_w_gate", "l1_w_up", "l1_w_down", "l1_ffn_post_g"]


def kernel(**inputs):
    import numpy as np
    import concourse.bacc as bacc
    from concourse.bass_utils import run_bass_kernel_spmd

    nc = bacc.Bacc("TRN2", target_bir_lowering=False, num_devices=1)
    arrays, t = {}, {}
    for name in _INS:
        a = np.ascontiguousarray(inputs[name])
        arrays[f"in_{name}"] = a
        t[name] = nc.dram_tensor(f"in_{name}", a.shape, mybir.dt.from_np(a.dtype), kind="ExternalInput").ap()
    t["out"] = nc.dram_tensor("out", (1, S, D), F32, kind="ExternalOutput").ap()
    trunk(nc, t)
    r = run_bass_kernel_spmd(nc, [arrays], core_ids=[0])
    return r.results[0]["out"]
```

```python
from contextlib import ExitStack

import concourse.bass as bass
from concourse import mybir

P = 128
D = 1024
KD = D // P
S = 256
NT = S // P
HD = 64
NH = 12
NKV = 3
NC = 4
GQ = NH // NKV
MEM = 256
FF = 3584
FB = 512
NB = FF // FB
CB = FB // P
NE = 8
CAP = P
MAX_JOBS = NE + NE // 2 - 1
EPS = 1e-6
SCALE = HD ** -0.5
THETA = 10000.0
PW = KD * FB // 2
RAW = 6
CUT = 3
NPC = 6 * NB
NEG = -1.0e30
BIG = 3.0e38
TWO_PI = 6.283185307179586
TP1 = 6.28125
TP2 = 0.0019350051879882812
TP3 = TWO_PI - TP1 - TP2
ROUND = 12582912.0

ALU = mybir.AluOpType
ACT = mybir.ActivationFunctionType
AX = mybir.AxisListType
F32 = mybir.dt.float32
F32R = mybir.dt.float32r
I32 = mybir.dt.int32
U32 = mybir.dt.uint32

NORMS = ["l0_mem_g", "l0_attn_pre_g", "l0_attn_post_g", "l0_ffn_pre_g", "l1_mem_g", "l0_ffn_post_g",
         "l1_attn_pre_g", "l1_attn_post_g", "l1_ffn_pre_g", "l1_ffn_post_g"]
MEM0, PRE0, POST0, FPRE0, MEM1, FPOST0, PRE1, POST1, FPRE1, FPOST1 = range(len(NORMS))
NG = 2


TURN = (1, 1, 4, 4, 5, 5, 2, 8)
USED_TURN = 27


class Banks:

    def __init__(self, filled, drained):
        self.filled, self.drained = filled, drained
        self.count = [0] * len(filled)
        self.at = {}

    def fill(self, label, bank, j=0):
        n = self.count[bank]
        self.count[bank] += 1
        self.at[label] = (bank, n + 1)
        return self.drained[bank], n + j * TURN[bank]

    def full(self, label, j=0):
        bank, n = self.at[label]
        return self.filled[bank], n + j * TURN[bank]

    def empty(self, label, j=0):
        bank, n = self.at[label]
        return self.drained[bank], n + j * TURN[bank]

    def full_sem(self, label):
        return self.filled[self.at[label][0]]

    def empty_sem(self, label):
        return self.drained[self.at[label][0]]


def trunk(nc, t):
    with ExitStack() as ctx:
        def sb(name, shape, dt=F32):
            return ctx.enter_context(nc.sbuf_tensor(name, shape, dt))

        def sem(name):
            return ctx.enter_context(nc.semaphore(name))

        raw = sb("raw", [P, RAW, PW])
        w_hi = sb("w_hi", [P, CUT, PW], F32R)
        w_lo = sb("w_lo", [P, CUT, PW], F32R)
        x_hi = sb("x_hi", [P, KD, S], F32R)
        x_lo = sb("x_lo", [P, KD, S], F32R)
        h_hi = sb("h_hi", [P, 2, FB], F32R)
        h_lo = sb("h_lo", [P, 2, FB], F32R)
        hres = sb("hres", [P, NT, D])
        memb = sb("memb", [P, NT, D])
        xn = sb("xn", [P, NT, D])
        reg_a = sb("reg_a", [P, 2 * D])
        reg_b = sb("reg_b", [P, 2 * D])
        mixT = sb("mixT", [P, KD, S])
        gains = sb("gains", [P, NG, D])
        work = sb("work", [P, 5632])
        ident = sb("ident", [P, P])
        upper_neg = sb("upper_neg", [P, P])
        ones_neg = sb("ones_neg", [P, P])
        ones = sb("ones", [P, P])
        before = sb("before", [P, P])
        band = sb("band", [P, 2 * P])
        clamp = sb("clamp", [P, P])
        iota_s = sb("iota_s", [P, P])
        iota_i = work[:, 0:P].bitcast(I32)
        cos2 = sb("cos2", [P, NT, HD])
        sin2 = sb("sin2", [P, NT, HD])
        rope_s = sb("rope_s", [P, 4, NT, HD // 2])
        invf = sb("invf", [P, HD // 2])
        pos_i = sb("pos_i", [P, NT], I32)
        pos_f = sb("pos_f", [P, NT])
        sinks = sb("sinks", [P, NH])
        nsinks = sb("nsinks", [P, NH])
        mhalf = sb("mhalf", [P, 1])
        halfpi = sb("halfpi", [P, 1])
        ssq = sb("ssq", [P, len(NORMS), NT])
        rstd = sb("rstd", [P, len(NORMS), NT])
        NU = 2 * (NKV + 1) * NT
        nmax = sb("nmax", [P, NU, 4])
        psum_e = sb("psum_e", [P, NU, 4])
        esink = sb("esink", [P, NU, 4])
        recip = sb("recip", [P, NU, 4])
        wr = sb("wr", [P, KD, NE])
        logits = sb("logits", [P, NT, NE])
        top_v = sb("top_v", [P, NT, 8])
        top_i = sb("top_i", [P, NT, 8], U32)
        top_f = sb("top_f", [P, NT, 8])
        gate2 = sb("gate2", [P, NT, 4])
        mask2 = sb("mask2", [P, NT, 2, NE])
        chosen = sb("chosen", [P, NT, NE])
        gates = sb("gates", [P, NT, NE])
        rank = sb("rank", [P, NT, NE])
        over = sb("over", [P, 3, NE])
        over_sel = sb("over_sel", [P, 3, NE])
        junk8 = sb("junk8", [P, 16])
        slot_of = sb("slot_of", [P, NT, MAX_JOBS + 1])
        gate_of = sb("gate_of", [P, NT, MAX_JOBS + 1])
        job_f = sb("job_f", [P, 4])
        job_i = sb("job_i", [P, 4], I32)

        psum = ctx.enter_context(nc.psum_tensor("psum", [P, 8, 512], F32))

        memT = reg_a[:, :].rearrange("p (k s) -> p k s", k=KD)
        xT = reg_b[:, :].rearrange("p (k s) -> p k s", k=KD)
        probs = reg_a[:, :].rearrange("p (u b h k) -> p u b h k", u=2, b=2, h=2)
        probsT = reg_b[:, :].rearrange("p (u b h k q) -> p u b h k q", u=2, b=2, h=2, k=2)
        rope_q = reg_a[:, 0:1024].rearrange("p (u c) -> p u c", u=2)
        rope_a = reg_a[:, 1024:1536]
        rope_b = reg_a[:, 1536:2048]
        soft = reg_a[:, 0:1536].rearrange("p (u b c) -> p u b c", u=2, b=2)
        stick = reg_b[:, 0:1536].rearrange("p (u b c) -> p u b c", u=2, b=2)
        qT = work[:, 0:1536].rearrange("p (c s) -> p c s", c=6)
        kT = work[:, 1536:3072].rearrange("p (c s) -> p c s", c=6)
        v = work[:, 3072:4608].rearrange("p (t c) -> p t c", t=NT)
        kmT = work[:, 4608:5120].rearrange("p (c s) -> p c s", c=2)
        vm = work[:, 5120:5632].rearrange("p (t c) -> p t c", t=NT)
        qcT = mixT[:, 6:8, :]
        kdup = mixT[:, 0:3, :].rearrange("p k s -> p (k s)").rearrange("p (t g u c) -> p t g u c", t=NT, g=NKV, u=2)
        act0 = work[:, 0:1024].rearrange("p (t c) -> p t c", t=2)
        hid0 = work[:, 1024:3072].rearrange("p (u t c) -> p u t c", u=2, t=NT)
        act1 = act0
        hid1 = work[:, 1024:2048].rearrange("p (u c) -> p u c", u=2)
        pick = work[:, 2560:2816].rearrange("p (t s) -> p t s", t=NT)
        pickT = work[:, 2816:3072].rearrange("p (t s) -> p t s", t=NT)
        picked_hi, picked_lo = x_hi[:, :, 0:CAP], x_lo[:, :, 0:CAP]
        y_sb = work[:, 4096:5120]
        esum = memb

        def unit(u, layer, i, tt):
            if layer == 0 and i < NKV:
                return u, layer, i, tt, qT, kT, (0, (tt + 1) * P), v, 0
            return u, layer, i, tt, qcT, kmT, (0, MEM), vm, 0

        UNITS0 = [unit(NT * i + tt, 0, i, tt) for i in range(NKV + 1) for tt in range(NT)]
        UNITS1 = [unit(len(UNITS0) + tt, 1, NKV, tt) for tt in range(NT)]

        def bank(b, lo=0, hi=512):
            return psum[:, b, lo:hi]

        filled = [sem(f"bank{b}_filled") for b in range(8)]
        drained = [sem(f"bank{b}_drained") for b in range(8)]
        raw_full = [sem(f"raw{s}_full") for s in range(RAW)]
        hi_ok = sem("hi_ok")
        lo_ok = sem("lo_ok")
        used = sem("used")
        part_hi = sem("part_hi")
        x_in, mem_in, small_in = sem("x_in"), sem("mem_in"), sem("small_in")
        gain_in = [sem(f"gain{i}_in") for i in range(NG)]
        consts = sem("consts")
        summed, rstd_ok, scaled, added = sem("summed"), sem("rstd_ok"), sem("scaled"), sem("added")
        act_chain, dve_chain, pool_chain = sem("act_chain"), sem("dve_chain"), sem("pool_chain")
        angles, sines = sem("angles"), sem("sines")
        roped = sem("roped")
        max_ok, exp_ok, norm_ok = sem("max_ok"), sem("exp_ok"), sem("norm_ok")
        soft_a, soft_b, stick_a, stick_b = sem("soft_a"), sem("soft_b"), sem("stick_a"), sem("stick_b")
        silu_ok = sem("silu_ok")
        gap_ok, gexp_ok, chosen_ok, tables_ok = sem("gap_ok"), sem("gexp_ok"), sem("chosen_ok"), sem("tables_ok")
        pick_ok = sem("pick_ok")
        silu1_ok = sem("silu1_ok")
        stored = sem("stored")
        sp_step = sem("sp_step")

        bk = Banks(filled, drained)

        def cols(w, lo, hi):
            w = w.rearrange("(k p) n -> p k n", p=P)
            return [w[:, 4 * half:4 * half + 4, lo:hi] for half in range(2)]

        def down_rows(w, b):
            w = w[b * FB:(b + 1) * FB, :].rearrange("(p c) n -> p c n", c=CB)
            return [w[:, 2 * half:2 * half + 2, :] for half in range(2)]

        pieces = []
        for b in range(NB + 1):
            pieces += [(kind, b, half) for kind in "gu" for half in range(2) if b < NB]
            pieces += [("d", b - 1, half) for half in range(2) if b >= 1]
        place = {x: n for n, x in enumerate(pieces)}
        assert len(pieces) == NPC

        IN0 = [(0, 512), (512, 1024), (1024, 1152), (1152, 1408)]
        IN1 = [(i * 512, (i + 1) * 512) for i in range(5)]
        loads = cols(t["l0_w_mem_kv"], 0, 512)
        for lo, hi in IN0:
            loads += cols(t["l0_w_in"], lo, hi)
        for lo in (0, 512):
            loads += cols(t["l0_w_out"], lo, lo + 512)
        FFN0 = len(loads)
        for kind, b, half in pieces:
            if kind == "d":
                loads.append(down_rows(t["l0_w_down"], b)[half])
            else:
                loads.append(cols(t["l0_w_gate" if kind == "g" else "l0_w_up"], b * FB, (b + 1) * FB)[half])
        loads += cols(t["l1_w_mem_kv"], 0, 512)
        for lo, hi in IN1:
            loads += cols(t["l1_w_in"], lo, hi)
        for lo in (0, 512):
            loads += cols(t["l1_w_out"], lo, lo + 512)
        PRE = len(loads)
        assert PRE % RAW == 0 and NPC % RAW == 0 and NPC % CUT == 0

        free_after = {}
        cut_free = {}
        job_free = {}

        def raw_at(n, c, w):
            return raw[:, n % RAW, 0:c * w].rearrange("p (c n) -> p c n", c=c)

        def cut_at(m, kind):
            c = 2 if kind == "d" else 4
            return [x[:, m % CUT, :].rearrange("p (c n) -> p c n", c=c) for x in (w_hi, w_lo)]

        block = ctx.enter_context(nc.Block())

        @block.tensor
        def _(pe):
            n_raw = [0]

            class Block:

                def __init__(self, w=FB):
                    self.n, self.w = n_raw[0], w
                    for n in (self.n, self.n + 1):
                        pe.wait_ge(raw_full[n % RAW], 16 * (n // RAW + 1))
                    n_raw[0] += 2

                def at(self, k, lo, hi):
                    return raw_at(self.n + k // 4, 4, self.w)[:, k % 4, lo:hi]

                def done(self, label):
                    free_after[self.n] = free_after[self.n + 1] = bk.full(label)

            def begin(label, b):
                s, n = bk.fill(label, b)
                if n > 0:
                    pe.wait_ge(s, n)

            def end(ins, label):
                ins.then_inc(bk.full_sem(label), 1)

            def turn(norm, tag, banks):
                for tt in range(NT):
                    pe.wait_ge(scaled, NT * norm + tt + 1)
                    for hf in range(2):
                        label = (tag, tt, hf)
                        begin(label, banks[2 * tt + hf])
                        for c in range(4):
                            k = 4 * hf + c
                            ins = pe.transpose(bank(banks[2 * tt + hf], c * P, (c + 1) * P),
                                               xn[:, tt, k * P:(k + 1) * P], ident[:, :])
                        end(ins, label)

            def turned(tag, tt=None):
                for u in range(NT):
                    if tt in (None, u):
                        for hf in range(2):
                            pe.wait_ge(*bk.empty((tag, u, hf)))

            def memory_kv(layer, srcT, banks):
                w = Block()
                begin(("kmT", layer), banks[0])
                for c in range(2):
                    for k in range(KD):
                        ins = pe.matmul(bank(banks[0], c * S, (c + 1) * S), w.at(k, c * P, (c + 1) * P),
                                        srcT[:, k, :], start=(k == 0), stop=(k == KD - 1))
                end(ins, ("kmT", layer))
                begin(("vm", layer), banks[1])
                for tt in range(NT):
                    for k in range(KD):
                        ins = pe.matmul(bank(banks[1], tt * 256, (tt + 1) * 256),
                                        srcT[:, k, tt * P:(tt + 1) * P], w.at(k, 256, 512),
                                        start=(k == 0), stop=(k == KD - 1))
                end(ins, ("vm", layer))
                w.done(("vm", layer))

            def rows(label, b, srcT, tt, w, lo, hi, at=0, first=True, last=True):
                if first:
                    begin(label, b)
                for k in range(KD):
                    ins = pe.matmul(bank(b, at, at + hi - lo), srcT[:, k, tt * P:(tt + 1) * P],
                                    w.at(k, lo, hi), start=(k == 0), stop=(k == KD - 1))
                if last:
                    end(ins, label)
                return ins

            def turned_cols(label, b, w, los):
                begin(label, b)
                for i, lo in enumerate(los):
                    for k in range(KD):
                        ins = pe.matmul(bank(b, i * S, (i + 1) * S), w.at(k, lo, lo + P), xT[:, k, :],
                                        start=(k == 0), stop=(k == KD - 1))
                end(ins, label)
                return ins

            def scores(u, layer, i, tt, q, k, keys):
                lo, hi = keys
                for b in range(2):
                    begin(("s", u, b), 2 * (u % 2) + b)
                for s2 in range(2):
                    for b in range(2):
                        r = slice(HD * b, HD * b + HD)
                        kc = k[r, i if layer == 0 and i < NKV else s2, lo:hi]
                        qc = q[r, (2 * i if i < NKV else 0) + s2, tt * P:(tt + 1) * P]
                        ins = pe.matmul(bank(2 * (u % 2) + b, s2 * (hi - lo), (s2 + 1) * (hi - lo)), qc, kc,
                                        start=True, stop=True)
                        if s2 == 1:
                            end(ins, ("s", u, b))

            def turn_probs(u, nk):
                pe.wait_ge(norm_ok, u + 1)
                for b in range(2):
                    begin(("pT", u, b), 4 + b)
                    for s2 in range(2):
                        for kt in range(nk):
                            ins = pe.transpose(bank(4 + b, (s2 * 2 + kt) * P, (s2 * 2 + kt + 1) * P),
                                               probs[:, u % 2, b, s2, kt * P:(kt + 1) * P], ident[:, :])
                    end(ins, ("pT", u, b))

            def weigh(u, i, nk, val, kt0):
                begin(("o", u), 6 + u % 2)
                for b in range(2):
                    pe.wait_ge(*bk.empty(("pT", u, b)))
                for s2 in range(2):
                    for b in range(2):
                        h = (0 if i < NKV else 2 * s2 + b) * HD + (i * HD if i < NKV else 0)
                        for kt in range(nk):
                            ins = pe.matmul(psum[HD * b:HD * b + HD, 6 + u % 2, s2 * P:(s2 + 1) * P],
                                            val[:, kt0 + kt, h:h + HD], probsT[:, u % 2, b, s2, kt, :],
                                            start=(kt == 0), stop=(kt == nk - 1), skip_group_check=True)
                end(ins, ("o", u))

            def attend(units):
                for s in range(len(units) + 2):
                    if s < len(units):
                        u, layer, i, tt, q, k, keys, val, kt0 = units[s]
                        scores(u, layer, i, tt, q, k, keys)
                    if 1 <= s <= len(units):
                        u, keys = units[s - 1][0], units[s - 1][6]
                        turn_probs(u, (keys[1] - keys[0]) // P)
                    if s >= 2:
                        u, i, keys, val, kt0 = (units[s - 2][x] for x in (0, 2, 6, 7, 8))
                        weigh(u, i, (keys[1] - keys[0]) // P, val, kt0)

            def project_out(layer, last_unit_labels):
                for label in last_unit_labels:
                    pe.wait_ge(*bk.empty(label))
                for hf in range(2):
                    w = Block()
                    for tt in range(NT):
                        rows(("mix", layer, tt, hf), 2 * tt + hf, mixT, tt, w, 0, FB)
                    w.done(("mix", layer, NT - 1, hf))

            pe.wait_ge(consts, 1)
            turn(MEM0, "mem0T", (0, 1, 2, 3))
            turned("mem0T")
            memory_kv(0, memT, (6, 7))
            turn(PRE0, "x0T", (0, 1, 2, 3))
            turned("x0T")
            w = Block()
            for tt in range(NT):
                rows(("qa", tt), tt, xT, tt, w, 0, 512)
            w.done(("qa", 1))
            w = Block()
            for tt in range(NT):
                rows(("qb", tt), 2 + tt, xT, tt, w, 0, 512)
            w.done(("qb", 1))
            w = Block(P)
            for tt in range(NT):
                rows(("vc", tt), 6 + tt, xT, tt, w, 0, P)
            w.done(("vc", 1))
            w = Block(2 * P)
            turned_cols(("qcT", 0), 4, w, (0, P))
            w.done(("qcT", 0))
            for n, (tag, tt) in enumerate([("a", 0), ("a", 1), ("b", 0), ("b", 1)]):
                pe.wait_ge(roped, n + 1)
                label = ("qT", tag, tt)
                begin(label, 5 if n % 2 == 0 else 0)
                b = bk.at[label][0]
                for c in range(4 if tag == "a" else 2):
                    ins = pe.transpose(bank(b, c * P, (c + 1) * P), rope_q[:, n % 2, c * P:(c + 1) * P],
                                       ident[:, :])
                end(ins, label)
                if tag == "b":
                    label = ("kT", tt)
                    begin(label, 1 + tt)
                    for g in range(NKV):
                        ins = pe.transpose(bank(1 + tt, g * P, (g + 1) * P),
                                           kdup[:, tt, g, :, :].rearrange("p u c -> p (u c)"), ident[:, :])
                    end(ins, label)
            for label in [("qT", x, tt) for x in "ab" for tt in range(NT)] + \
                    [("kT", 0), ("kT", 1), ("qcT", 0), ("kmT", 0), ("vm", 0), ("vc", 0), ("vc", 1)]:
                pe.wait_ge(*bk.empty(label))
            attend(UNITS0)
            project_out(0, [("o", u[0]) for u in UNITS0[-2:]])

            turn(FPRE0, "f0T", (4, 5, 6, 7))
            turned("f0T")
            def thrice(out, x, w, first, last):
                pe.matmul(out, x[0], w[0], start=first, stop=False, skip_group_check=True)
                pe.matmul(out, x[0], w[1], start=False, stop=False, skip_group_check=True)
                return pe.matmul(out, x[1], w[0], start=False, stop=last, skip_group_check=True)

            rot = [0]
            n_used = [0]

            def gate_up(kind, b, tt):
                label = (kind + "0", b, tt)
                begin(label, 4 + rot[0] % 3)
                rot[0] += 1
                for half in range(2):
                    m = place[kind, b, half]
                    pe.wait_ge(lo_ok, m + 1)
                    w = cut_at(m, kind)
                    for c in range(4):
                        k = 4 * half + c
                        x = [y[:, k, tt * P:(tt + 1) * P] for y in (x_hi, x_lo)]
                        ins = thrice(bank(bk.at[label][0]), x, [y[:, c, :] for y in w], k == 0, k == KD - 1)
                    if half == 0 and tt == NT - 1:
                        ins.then_inc(used, 1)
                        n_used[0] += 1
                        cut_free[m] = (used, n_used[0])
                end(ins, label)
                if tt == NT - 1:
                    cut_free[m] = bk.full(label)

            def turn_hidden(b, tt):
                pe.wait_ge(*bk.empty(("u0", b, tt)))
                begin(("h0T", b, tt), 7)
                for c in range(CB):
                    ins = pe.transpose(bank(7, c * P, (c + 1) * P), hid0[:, b % 2, tt, c * P:(c + 1) * P],
                                       ident[:, :])
                end(ins, ("h0T", b, tt))

            def down(b, tt):
                if b == 0:
                    for hf in range(2):
                        begin(("y0", tt, hf), 2 * tt + hf)
                pe.wait_ge(*bk.empty(("h0T", b, tt)))
                for half in range(2):
                    m = place["d", b, half]
                    pe.wait_ge(lo_ok, m + 1)
                    w = cut_at(m, "d")
                    for hf in range(2):
                        for c in range(2):
                            cc = 2 * half + c
                            h = [y[:, tt, cc * P:(cc + 1) * P] for y in (h_hi, h_lo)]
                            ins = thrice(bank(2 * tt + hf), h, [y[:, c, hf * 512:(hf + 1) * 512] for y in w],
                                         b == 0 and cc == 0, b == NB - 1 and cc == CB - 1)
                        if b == NB - 1 and half == 1:
                            end(ins, ("y0", tt, hf))
                    if tt == NT - 1:
                        if b == NB - 1 and half == 1:
                            cut_free[m] = bk.full(("y0", tt, 1))
                        else:
                            ins.then_inc(used, 1)
                            n_used[0] += 1
                            cut_free[m] = (used, n_used[0])

            for b in range(NB):
                gate_up("g", b, 0)
                if b >= 1:
                    turn_hidden(b - 1, 0)
                gate_up("g", b, 1)
                if b >= 1:
                    turn_hidden(b - 1, 1)
                gate_up("u", b, 0)
                gate_up("u", b, 1)
                if b >= 1:
                    down(b - 1, 0)
                    if b == NB - 1:
                        turn_hidden(b, 0)
                    down(b - 1, 1)
            turn_hidden(NB - 1, 1)
            down(NB - 1, 0)
            down(NB - 1, 1)
            n_raw[0] = FFN0 + NPC

            turn(MEM1, "mem1T", (4, 5, 6, 7))
            turned("mem1T")
            memory_kv(1, memT, (4, 5))
            turn(PRE1, "x1T", (0, 1, 2, 3))
            turned("x1T")
            for i, b in enumerate((6, 4, 6)):
                w = Block()
                turned_cols(("p", 2 * i), b, w, (0, 128))
                turned_cols(("p", 2 * i + 1), b + 1, w, (256, 384))
                w.done(("p", 2 * i + 1))
            w = Block()
            for tt in range(NT):
                rows(("v1a", tt), tt, xT, tt, w, 0, 512)
            w.done(("v1a", 1))
            w = Block()
            for tt in range(NT):
                rows(("v1b", tt), 2 + tt, xT, tt, w, 0, 256)
            turned_cols(("qcT", 1), 4, w, (256, 384))
            w.done(("qcT", 1))

            def stick_scores(p):
                for b in range(2):
                    bb = 2 * (p % 3) + b
                    begin(("z", p, b), bb)
                    r = slice(HD * b, HD * b + HD)
                    pe.matmul(bank(bb, 0, 256), kT[r, p, 0:P], qT[r, p, :], start=True, stop=False,
                              skip_group_check=True)
                    ins = pe.matmul(bank(bb, 256, 384), kT[r, p, P:2 * P], qT[r, p, P:2 * P], start=False,
                                    stop=False, skip_group_check=True)
                    end(ins, ("z", p, b))

            def stick_sum(p):
                pe.wait_ge(soft_b, p + 1)
                for b in range(2):
                    bb = 2 * (p % 3) + b
                    begin(("zc", p, b), bb)
                    pe.matmul(bank(bb, 0, 256), upper_neg[:, :], soft[:, p % 2, b, 0:256], start=False,
                              stop=False, skip_group_check=True)
                    pe.matmul(bank(bb, P, 2 * P), ones_neg[:, :], soft[:, p % 2, b, 256:384], start=False,
                              stop=False, skip_group_check=True)
                    ins = pe.matmul(bank(bb, 256, 384), upper_neg[:, :], soft[:, p % 2, b, 256:384],
                                    start=False, stop=True, skip_group_check=True)
                    end(ins, ("zc", p, b))

            def stick_weigh(p):
                pe.wait_ge(stick_b, p + 1)
                begin(("os", p), 6 + p % 2)
                for b in range(2):
                    h = (2 * p + b) * HD
                    o = psum[HD * b:HD * b + HD, 6 + p % 2, :]
                    pe.matmul(o[:, 0:256], v[:, 0, h:h + HD], stick[:, p % 2, b, 0:256], start=True,
                              stop=False, skip_group_check=True)
                    ins = pe.matmul(o[:, P:2 * P], v[:, 1, h:h + HD], stick[:, p % 2, b, 256:384],
                                    start=False, stop=True, skip_group_check=True)
                end(ins, ("os", p))

            for label in [("p", i) for i in range(6)] + [("v1a", 0), ("v1a", 1), ("v1b", 0), ("v1b", 1)]:
                pe.wait_ge(*bk.empty(label))
            NP = NH // 2
            for s in range(NP + 2):
                if s < NP:
                    stick_scores(s)
                if 1 <= s <= NP:
                    stick_sum(s - 1)
                if s >= 2:
                    stick_weigh(s - 2)
            for label in [("qcT", 1), ("kmT", 1), ("vm", 1)]:
                pe.wait_ge(*bk.empty(label))
            attend(UNITS1)
            project_out(1, [("os", NP - 1), ("os", NP - 2)] + [("o", u[0]) for u in UNITS1])

            turn(FPRE1, "f1T", (4, 5, 6, 7))
            turned("f1T")
            pe.wait_ge(small_in, 16 * 3)
            begin(("logits",), 4)
            for tt in range(NT):
                for k in range(KD):
                    ins = pe.matmul(bank(4, tt * NE, (tt + 1) * NE), xT[:, k, tt * P:(tt + 1) * P],
                                    wr[:, k, :], start=(k == 0), stop=(k == KD - 1))
            end(ins, ("logits",))
            pe.wait_ge(chosen_ok, 1)
            begin(("rank",), 5)
            pe.matmul(bank(5, 0, NE), before[:, :], chosen[:, 0, :], start=True, stop=True)
            pe.matmul(bank(5, NE, 2 * NE), ones[:, :], chosen[:, 0, :], start=True, stop=False)
            pe.matmul(bank(5, NE, 2 * NE), before[:, :], chosen[:, 1, :], start=False, stop=True)
            pe.matmul(bank(5, 2 * NE, 3 * NE), ones[:, :], chosen[:, 0, :], start=True, stop=False)
            ins = pe.matmul(bank(5, 2 * NE, 3 * NE), ones[:, :], chosen[:, 1, :], start=False, stop=True)
            end(ins, ("rank",))

            def gather(labels, waits):
                for hf in range(2):
                    s, n = waits[hf]
                    pe.wait_ge(s, n)
                    for c in range(4):
                        k = 4 * hf + c
                        for tt in range(NT):
                            ins = pe.matmul(bank(4 + hf, c * P, (c + 1) * P), xn[:, tt, k * P:(k + 1) * P],
                                            pick[:, tt, :], start=(tt == 0), stop=(tt == NT - 1))
                    end(ins, labels[hf])

            pe.wait_ge(pick_ok, 1)
            gather([("pre-gather", 0), ("pre-gather", 1)],
                   [bk.fill(("pre-gather", hf), 4 + hf) for hf in range(2)])
            base = list(bk.count)
            used_before = n_used[0]
            pe.wait_ge(tables_ok, 1)
            n_jobs = pe.value_load(job_i[0:1, 3:4], min_val=NE, max_val=MAX_JOBS)
            for hf in range(2):
                pe.wait_ge(*bk.empty(("pre-gather", hf)))
            with pe.Fori(0, n_jobs) as j:
                def jbegin(label, b):
                    pe.wait_ge(*bk.fill(label, b, j))

                def jcut(m, kind):
                    pe.wait_ge(lo_ok, NPC * j + (NPC + m + 1))
                    return cut_at(m, kind)

                def use(ins, m):
                    ins.then_inc(used, 1)
                    n_used[0] += 1
                    job_free[m] = n_used[0]

                def expert_rows(kind, b):
                    label = (kind, b)
                    bb = 2 + 2 * (b % 2) + (kind == "u")
                    jbegin(label, bb)
                    for half in range(2):
                        m = place[kind, b, half]
                        w = jcut(m, kind)
                        for c in range(4):
                            k = 4 * half + c
                            ins = thrice(bank(bb), (picked_hi[:, k, :], picked_lo[:, k, :]),
                                         [y[:, c, :] for y in w], k == 0, k == KD - 1)
                        if half == 0:
                            use(ins, m)
                    end(ins, label)
                    job_free[m] = label

                def expert_turn(b):
                    jbegin(("T", b), 7)
                    pe.wait_ge(*bk.empty(("u", b), j))
                    for c in range(CB):
                        ins = pe.transpose(bank(7, c * P, (c + 1) * P), hid1[:, b % 2, c * P:(c + 1) * P],
                                           ident[:, :])
                    end(ins, ("T", b))

                def expert_down(b, half):
                    if b == 0 and half == 0:
                        for hf in range(2):
                            jbegin(("y", hf), hf)
                    if half == 0:
                        pe.wait_ge(*bk.empty(("T", b), j))
                    m = place["d", b, half]
                    w = jcut(m, "d")
                    for hf in range(2):
                        for c in range(2):
                            cc = 2 * half + c
                            h = [y[:, b % 2, cc * P:(cc + 1) * P] for y in (h_hi, h_lo)]
                            ins = thrice(bank(hf), h, [y[:, c, hf * 512:(hf + 1) * 512] for y in w],
                                         b == 0 and cc == 0, b == NB - 1 and cc == CB - 1)
                        if b == NB - 1 and half == 1:
                            end(ins, ("y", hf))
                    if b == NB - 1 and half == 1:
                        job_free[m] = ("y", 1)
                    else:
                        use(ins, m)

                for b in range(NB):
                    expert_rows("g", b)
                    if b >= 1:
                        expert_turn(b - 1)
                    expert_rows("u", b)
                    if b == 0:
                        jbegin(("pickT",), 6)
                        for tt in range(NT):
                            ins = pe.transpose(bank(6, tt * P, (tt + 1) * P), pick[:, tt, :], ident[:, :])
                        end(ins, ("pickT",))
                    else:
                        expert_down(b - 1, 0)
                        if b == NB - 1:
                            expert_turn(b)
                        expert_down(b - 1, 1)
                expert_down(NB - 1, 0)
                expert_down(NB - 1, 1)
                pe.wait_ge(pick_ok, j + 2)
                gather([("gather", 0), ("gather", 1)],
                       [bk.fill(("gather", hf), 4 + hf, j) for hf in range(2)])
                pe.wait_ge(*bk.empty(("pickT",), j))
                for hf in range(2):
                    pe.wait_ge(*bk.empty(("y", hf), j))
                for i, (tt, hf, bb) in enumerate([(0, 0, 6), (0, 1, 7), (1, 0, 4), (1, 1, 5)]):
                    jbegin(("back", tt, hf), bb)
                    ins = pe.matmul(bank(bb), pickT[:, tt, :], y_sb[:, hf * 512:(hf + 1) * 512],
                                    start=True, stop=True)
                    end(ins, ("back", tt, hf))
                for hf in range(2):
                    pe.wait_ge(*bk.empty(("gather", hf), j))
            assert tuple(bk.count[b] - base[b] for b in range(8)) == TURN
            assert n_used[0] - used_before == USED_TURN

        @block.scalar
        def _(act):
            links = [0]

            def link(ins):
                links[0] += 1
                ins.then_inc(act_chain, 1)
                act.wait_ge(act_chain, links[0])

            def copy(label, out, src, scale=None):
                act.wait_ge(*bk.full(label))
                act.activation(out, src, ACT.Copy, scale=1.0 if scale is None else scale)\
                    .then_inc(bk.empty_sem(label), 1)

            def square_sum(norm, tt, out, src):
                act.activation(out, src, ACT.Square, accum_out=ssq[:, norm, tt:tt + 1]).then_inc(summed, 1)

            def drain_turned(tag, dst, banks_half=0):
                for tt in range(NT):
                    label = (tag, tt, 0)
                    copy(label, dst[:, 0:4, tt * P:(tt + 1) * P],
                         bank(bk.at[label][0]).rearrange("p (c s) -> p c s", c=4))

            def exps(u, i, layer, nk):
                act.wait_ge(max_ok, u + 1)
                for b in range(2):
                    for s2 in range(2):
                        x = probs[:, u % 2, b, s2, 0:nk * P]
                        ins = act.activation(x, x, ACT.Exp, bias=nmax[:, u, 2 * s2 + b:2 * s2 + b + 1],
                                             accum_out=psum_e[:, u, 2 * s2 + b:2 * s2 + b + 1])
                if layer == 0 and i < NKV:
                    ins = act.activation(esink[:, u, :], esink[:, u, :], ACT.Exp)
                ins.then_inc(exp_ok, 1)

            def attend(units):
                for s in range(len(units) + 2):
                    if s < len(units):
                        u, layer, i, keys = (units[s][x] for x in (0, 1, 2, 6))
                        exps(u, i, layer, (keys[1] - keys[0]) // P)
                    if 1 <= s <= len(units):
                        u, keys = units[s - 1][0], units[s - 1][6]
                        nk = (keys[1] - keys[0]) // P
                        copy(("pT", u, 0), probsT[:, u % 2, 0, :, 0:nk, :],
                             bank(4).rearrange("p (h k q) -> p h k q", h=2, k=2)[:, :, 0:nk, :])
                    if s >= 2:
                        u, i, tt = (units[s - 2][x] for x in (0, 2, 3))
                        c = 2 * i
                        copy(("o", u), mixT[:, c:c + 2, tt * P:(tt + 1) * P],
                             bank(6 + u % 2, 0, 256).rearrange("p (c s) -> p c s", c=2))

            def raise_part(label, out, src, j=0):
                act.wait_ge(*bk.full(label, j))
                act.activation(out, src, ACT.Copy).then_inc(part_hi, 1)

            def cut_high(m, n, round_no, free):
                act.wait_ge(raw_full[n % RAW], round_no)
                if free is not None:
                    act.wait_ge(*free)
                act.activation(w_hi[:, m % CUT, :], raw[:, n % RAW, :], ACT.Copy).then_inc(hi_ok, 1)

            def cut_high0(m):
                n = FFN0 + m
                cut_high(m, n, 16 * (n // RAW + 1), cut_free[m - CUT] if m >= CUT else None)

            act.wait_ge(mem_in, 16)
            for tt in range(NT):
                square_sum(MEM0, tt, xn[:, tt, :], memb[:, tt, :])
            drain_turned("mem0T", memT)
            act.wait_ge(x_in, 16)
            for tt in range(NT):
                act.wait_ge(*bk.full(("mem0T", tt, 1)))
                square_sum(PRE0, tt, xn[:, tt, :], hres[:, tt, :])
            act.wait_ge(angles, 1)
            act.wait_ge(consts, 1)
            act.activation(rope_s[:, 2, :, :], rope_s[:, 0, :, :], ACT.Sin)
            act.activation(rope_s[:, 3, :, :], rope_s[:, 1, :, :], ACT.Sin, scale=-1.0,
                           bias=halfpi[:, 0:1]).then_inc(sines, 1)
            copy(("kmT", 0), kmT, bank(6).rearrange("p (c s) -> p c s", c=2))
            copy(("vm", 0), vm, bank(7).rearrange("p (c s) -> p c s", c=2))
            drain_turned("x0T", xT)
            for tt in range(NT):
                copy(("vc", tt), v[:, tt, 64:192], bank(6 + tt, 0, 128))
            copy(("qcT", 0), qcT, bank(4).rearrange("p (c s) -> p c s", c=2))
            for tag in "ab":
                for tt in range(NT):
                    label = ("qT", tag, tt)
                    n = 4 if tag == "a" else 2
                    copy(label, qT[:, 0:4, tt * P:(tt + 1) * P] if tag == "a" else
                         qT[:, 4:6, tt * P:(tt + 1) * P],
                         bank(bk.at[label][0], 0, n * P).rearrange("p (c s) -> p c s", c=n))
            attend(UNITS0)

            def post_norm(norm, labels, src, out):
                for tt in range(NT):
                    for label in labels[tt]:
                        act.wait_ge(*bk.full(label))
                    square_sum(norm, tt, out[:, tt, :], src(tt))

            two_banks = lambda tt: psum[:, 2 * tt:2 * tt + 2, :].rearrange("p a b -> p (a b)")
            post_norm(POST0, [[("mix", 0, tt, hf) for hf in range(2)] for tt in range(NT)], two_banks, xn)

            def pre_norm(norm, n_added):
                for tt in range(NT):
                    act.wait_ge(added, n_added + tt + 1)
                    square_sum(norm, tt, xn[:, tt, :], hres[:, tt, :])

            pre_norm(FPRE0, 0)
            for m in range(CUT):
                cut_high0(m)
            for tt in range(NT):
                for hf in range(2):
                    label = ("f0T", tt, hf)
                    raise_part(label, x_hi[:, 4 * hf:4 * hf + 4, tt * P:(tt + 1) * P],
                               bank(bk.at[label][0]).rearrange("p (c s) -> p c s", c=4))
            for tt in range(NT):
                act.wait_ge(*bk.full(("f0T", tt, 1)))
                square_sum(MEM1, tt, xn[:, tt, :], memb[:, tt, :])

            for i, (kind, b, half) in enumerate(pieces):
                tt = half
                if kind == "g":
                    label = ("g0", b, tt)
                    act.wait_ge(*bk.full(label))
                    if b >= 1:
                        act.wait_ge(*bk.empty(("u0", b - 1, tt)))
                    act.activation(act0[:, tt, :], bank(bk.at[label][0]), ACT.Silu)\
                        .then_inc(bk.empty_sem(label), 1)
                if (kind == "g" and b >= 1) or (kind, b) == ("d", NB - 2):
                    hb = b - 1 if kind == "g" else NB - 1
                    raise_part(("h0T", hb, tt), h_hi[:, tt, :], bank(7))
                if i + CUT < NPC:
                    cut_high0(i + CUT)
            drain_turned("mem1T", memT)
            post_norm(FPOST0, [[("y0", tt, hf) for hf in range(2)] for tt in range(NT)], two_banks,
                      mixT[:, :, :].rearrange("p (t a) s -> p t (a s)", t=NT))
            copy(("kmT", 1), kmT, bank(4).rearrange("p (c s) -> p c s", c=2))
            copy(("vm", 1), vm, bank(5).rearrange("p (c s) -> p c s", c=2))
            pre_norm(PRE1, 2)
            drain_turned("x1T", xT)

            def heads(i, dst, scale=None):
                copy(("p", i), dst, bank(bk.at["p", i][0]).rearrange("p (c s) -> p c s", c=2), scale)

            heads(0, qT[:, 0:2, :], SCALE)
            heads(2, qT[:, 4:6, :], SCALE)
            heads(4, kT[:, 2:4, :])
            copy(("v1a", 0), v[:, 0, 0:512], bank(0))
            copy(("v1b", 0), v[:, 0, 512:768], bank(2, 0, 256))
            copy(("qcT", 1), qcT, bank(4).rearrange("p (c s) -> p c s", c=2))

            def z_view(p):
                return psum[:, 2 * (p % 3):2 * (p % 3) + 2, 0:384]

            def log_terms(p):
                for b in range(2):
                    act.wait_ge(*bk.full(("z", p, b)))
                x = soft[:, p % 2, :, :]
                if p >= 2:
                    act.wait_ge(*bk.full(("zc", p - 2, 1)))
                link(act.activation(x, z_view(p), ACT.Abs))
                link(act.activation(x, x, ACT.Exp, scale=-1.0))
                act.activation(x, x, ACT.Ln, bias=1.0).then_inc(soft_a, 1)

            def stick_exp(p):
                for b in range(2):
                    act.wait_ge(*bk.full(("zc", p, b)))
                if p >= 2:
                    act.wait_ge(*bk.full(("os", p - 2)))
                for b in range(2):
                    ins = act.activation(stick[:, p % 2, b, :], bank(2 * (p % 3) + b, 0, 384), ACT.Exp)
                    ins.then_inc(bk.empty_sem(("zc", p, b)), 1)

            NP = NH // 2
            for s in range(NP + 2):
                if s < NP:
                    log_terms(s)
                if 1 <= s <= NP:
                    stick_exp(s - 1)
                if s >= 2:
                    copy(("os", s - 2), mixT[:, s - 2, :], bank(6 + s % 2, 0, 256))
            attend(UNITS1)
            post_norm(POST1, [[("mix", 1, tt, hf) for hf in range(2)] for tt in range(NT)], two_banks, xn)
            pre_norm(FPRE1, 4)
            drain_turned("f1T", xT)

            act.wait_ge(gap_ok, 1)
            act.activation(gate2[:, :, 1:2], gate2[:, :, 0:1], ACT.Exp).then_inc(gexp_ok, 1)

            def cut_high1(j, m):
                i = m - CUT
                free = None
                if i >= 0:
                    last = job_free[i]
                    free = bk.full(last, j) if isinstance(last, tuple) else (used, last + USED_TURN * j)
                cut_high(m, m, (16 * NPC // RAW) * j + 16 * (PRE // RAW + m // RAW + 1), free)

            def gathered(label, hf, j=0):
                raise_part(label, picked_hi[:, 4 * hf:4 * hf + 4, :],
                           bank(4 + hf).rearrange("p (k s) -> p k s", k=4), j)

            for m in range(CUT):
                cut_high1(0, m)
            for hf in range(2):
                gathered(("pre-gather", hf), hf)
            act.wait_ge(tables_ok, 1)
            n_jobs = act.value_load(job_i[0:1, 3:4], min_val=NE, max_val=MAX_JOBS)
            with act.Fori(0, n_jobs) as j:
                def full(label):
                    act.wait_ge(*bk.full(label, j))

                def jcopy(label, out, src):
                    full(label)
                    act.activation(out, src, ACT.Copy).then_inc(bk.empty_sem(label), 1)

                for i, (kind, b, half) in enumerate(pieces):
                    if (kind, half) == ("g", 1):
                        full(("g", b))
                        act.activation(act1[:, b % 2, :], bank(bk.at["g", b][0]), ACT.Silu)\
                            .then_inc(bk.empty_sem(("g", b)), 1)
                        if b >= 1:
                            raise_part(("T", b - 1), h_hi[:, (b - 1) % 2, :], bank(7), j)
                    if (kind, b, half) == ("d", 0, 0):
                        jcopy(("pickT",), pickT, bank(6, 0, 256).rearrange("p (t s) -> p t s", t=NT))
                    if (kind, b, half) == ("d", NB - 2, 0):
                        raise_part(("T", NB - 1), h_hi[:, (NB - 1) % 2, :], bank(7), j)
                    if i == NPC - 1:
                        jcopy(("y", 0), y_sb[:, 0:512], bank(0))
                    cut_high1(j, i + CUT)
                for hf in range(2):
                    gathered(("gather", hf), hf, j)
            act.wait_ge(tables_ok, 2)
            for tt in range(NT):
                square_sum(FPOST1, tt, xn[:, tt, :], esum[:, tt, :])

        @block.vector
        def _(dve):
            links = [0]

            def link(ins):
                links[0] += 1
                ins.then_inc(dve_chain, 1)
                dve.wait_ge(dve_chain, links[0])

            def copy(label, out, src, scale=None):
                dve.wait_ge(*bk.full(label))
                ins = dve.tensor_copy(out, src) if scale is None else \
                    dve.tensor_scalar(out, src, scale, None, ALU.mult)
                ins.then_inc(bk.empty_sem(label), 1)

            def scale_rows(norm, tt, out, src, labels=()):
                if tt == 0:
                    dve.wait_ge(gain_in[norm % NG], 16 * (norm // NG + 1))
                dve.wait_ge(rstd_ok, NT * norm + tt + 1)
                ins = dve.scalar_tensor_tensor(out=out, in0=src, scalar=rstd[:, norm, tt:tt + 1],
                                               in1=gains[:, norm % NG, :], op0=ALU.mult, op1=ALU.mult)
                ins.then_inc(scaled, 1)
                dve.wait_ge(scaled, NT * norm + tt + 1)

            def drain_turned(tag, dst):
                for tt in range(NT):
                    label = (tag, tt, 1)
                    copy(label, dst[:, 4:8, tt * P:(tt + 1) * P],
                         bank(bk.at[label][0]).rearrange("p (c s) -> p c s", c=4))

            def post_norm(norm, labels, src, out):
                for tt in range(NT):
                    scale_rows(norm, tt, out[:, tt, :], src(tt))
                    for label in labels[tt]:
                        dve.sem_inc(bk.empty_sem(label), 1)
                    dve.tensor_tensor(hres[:, tt, :], hres[:, tt, :], out[:, tt, :], ALU.add)\
                        .then_inc(added, 1)

            def pre_norm(norm, src):
                for tt in range(NT):
                    scale_rows(norm, tt, xn[:, tt, :], src[:, tt, :])

            def row_max(u, layer, i, tt, nk):
                for b in range(2):
                    dve.wait_ge(*bk.full(("s", u, b)))
                if u >= 2 and u != UNITS1[0][0] and u != UNITS1[1][0]:
                    for b in range(2):
                        dve.wait_ge(*bk.full(("pT", u - 2, b)))
                K = nk * P
                mask = band[:, 2 * P - K:2 * P]
                for b in range(2):
                    x = probs[:, u % 2, b, :, 0:K]
                    src = bank(2 * (u % 2) + b, 0, 2 * K).rearrange("p (h k) -> p h k", h=2)
                    if layer == 0 and i < NKV:
                        ins = dve.scalar_tensor_tensor(out=x, in0=src, scalar=SCALE,
                                                       in1=mask.unsqueeze(1).to_broadcast((P, 2, K)),
                                                       op0=ALU.mult, op1=ALU.add)
                    else:
                        ins = dve.tensor_scalar(x, src, SCALE, None, ALU.mult)
                    ins.then_inc(bk.empty_sem(("s", u, b)), 1)
                for b in range(2):
                    dve.wait_ge(*bk.empty(("s", u, b)))
                for b in range(2):
                    ins = dve.tensor_reduce(nmax[:, u, b:4:2], probs[:, u % 2, b, :, 0:K], AX.X, ALU.max)
                link(ins)
                if layer == 0 and i < NKV:
                    link(dve.scalar_tensor_tensor(out=nmax[:, u, :], in0=nmax[:, u, :], scalar=-1.0,
                                                  in1=nsinks[:, 4 * i:4 * i + 4], op0=ALU.mult, op1=ALU.min))
                    dve.tensor_tensor(esink[:, u, :], nmax[:, u, :], sinks[:, 4 * i:4 * i + 4], ALU.add)\
                        .then_inc(max_ok, 1)
                else:
                    dve.tensor_scalar(nmax[:, u, :], nmax[:, u, :], -1.0, None, ALU.mult).then_inc(max_ok, 1)

            def normalise(u, layer, i, nk):
                dve.wait_ge(exp_ok, u + 1)
                if layer == 0 and i < NKV:
                    link(dve.tensor_tensor(psum_e[:, u, :], psum_e[:, u, :], esink[:, u, :], ALU.add))
                link(dve.reciprocal(recip[:, u, :], psum_e[:, u, :]))
                for b in range(2):
                    x = probs[:, u % 2, b, :, 0:nk * P]
                    ins = dve.tensor_tensor(x, x, recip[:, u, b:4:2].unsqueeze(2).to_broadcast((P, 2, nk * P)),
                                            ALU.mult)
                ins.then_inc(norm_ok, 1)

            def attend(units):
                for s in range(len(units) + 2):
                    if s < len(units):
                        u, layer, i, tt, keys = (units[s][x] for x in (0, 1, 2, 3, 6))
                        row_max(u, layer, i, tt, (keys[1] - keys[0]) // P)
                    if 1 <= s <= len(units):
                        u, layer, i, keys = (units[s - 1][x] for x in (0, 1, 2, 6))
                        nk = (keys[1] - keys[0]) // P
                        normalise(u, layer, i, nk)
                        copy(("pT", u, 1), probsT[:, u % 2, 1, :, 0:nk, :],
                             bank(5).rearrange("p (h k q) -> p h k q", h=2, k=2)[:, :, 0:nk, :])

            n_part = [0]

            def lower_part(label, out, src, high, j=None):
                n_part[0] += 1
                dve.wait_ge(part_hi, n_part[0] if j is None else n_part[0] + 9 * j)
                dve.tensor_tensor(out, src, high.bitcast(F32), ALU.subtract).then_inc(bk.empty_sem(label), 1)

            def cut_rest(m, n, count):
                dve.wait_ge(hi_ok, count)
                dve.tensor_tensor(w_lo[:, m % CUT, :], raw[:, n % RAW, :],
                                  w_hi[:, m % CUT, :].bitcast(F32), ALU.subtract).then_inc(lo_ok, 1)

            dve.wait_ge(small_in, 16 * 3)
            dve.wait_ge(consts, 1)
            link(dve.tensor_copy(pos_f[:, :], pos_i[:, :]))
            dve.tensor_scalar(nsinks[:, :], sinks[:, :], -1.0, None, ALU.mult)
            for tt in range(NT):
                ins = dve.tensor_scalar(rope_s[:, 0, tt, :], invf[:, :], pos_f[:, tt:tt + 1], None, ALU.mult)
            link(ins)
            a, n = rope_s[:, 0, :, :], rope_s[:, 1, :, :]
            link(dve.tensor_scalar(n, a, 1.0 / TWO_PI, ROUND, ALU.mult, ALU.add))
            link(dve.tensor_scalar(n, n, -ROUND, None, ALU.add))
            for part in (TP1, TP2, TP3):
                link(dve.scalar_tensor_tensor(out=a, in0=n, scalar=-part, in1=a, op0=ALU.mult, op1=ALU.add))
            link(dve.tensor_scalar(a, a, 3.1415925, -3.1415925, ALU.min, ALU.max))
            link(dve.tensor_scalar(n, a, -1.0, None, ALU.mult))
            dve.tensor_tensor(n, a, n, ALU.max).then_inc(angles, 1)

            for tt in range(NT):
                scale_rows(MEM0, tt, xn[:, tt, :], memb[:, tt, :])
            drain_turned("mem0T", memT)
            pre_norm(PRE0, hres)
            drain_turned("x0T", xT)
            dve.wait_ge(sines, 1)
            H2 = HD // 2
            for half in range(2):
                dve.tensor_copy(cos2[:, :, half * H2:(half + 1) * H2], rope_s[:, 3, :, :])
            dve.tensor_scalar(sin2[:, :, 0:H2], rope_s[:, 2, :, :], -1.0, None, ALU.mult)
            link(dve.tensor_copy(sin2[:, :, H2:HD], rope_s[:, 2, :, :]))

            for n, (tag, tt) in enumerate([("a", 0), ("a", 1), ("b", 0), ("b", 1)]):
                label = ("q" + tag, tt)
                nh = 8 if tag == "a" else 7
                bb = bk.at[label][0]
                x = bank(bb, 0, nh * HD).rearrange("p (h c) -> p h c", c=HD)
                ra = rope_a[:, 0:nh * HD].rearrange("p (h c) -> p h c", c=HD)
                rb = rope_b[:, 0:nh * HD].rearrange("p (h c) -> p h c", c=HD)
                dve.wait_ge(*bk.full(label))
                dve.tensor_tensor(ra, x, cos2[:, tt, :].unsqueeze(1).to_broadcast((P, nh, HD)), ALU.mult)
                dve.tensor_tensor(rb[:, :, 0:H2], x[:, :, H2:HD],
                                  sin2[:, tt, 0:H2].unsqueeze(1).to_broadcast((P, nh, H2)), ALU.mult)
                ins = dve.tensor_tensor(rb[:, :, H2:HD], x[:, :, 0:H2],
                                        sin2[:, tt, H2:HD].unsqueeze(1).to_broadcast((P, nh, H2)), ALU.mult)
                if tag == "b":
                    ins = dve.tensor_copy(v[:, tt, 0:64], bank(bb, 448, 512))
                ins.then_inc(bk.empty_sem(label), 1)
                dve.wait_ge(*bk.empty(label))
                if n >= 2:
                    dve.wait_ge(*bk.full(("qT", "a", n - 2)))
                nq = 8 if tag == "a" else 4
                ins = dve.tensor_tensor(rope_q[:, n % 2, 0:nq * HD], rope_a[:, 0:nq * HD],
                                        rope_b[:, 0:nq * HD], ALU.add)
                if tag == "b":
                    for dup in range(2):
                        ins = dve.tensor_tensor(kdup[:, tt, :, dup, :], ra[:, 4:7, :], rb[:, 4:7, :], ALU.add)
                ins.then_inc(roped, 1)
                dve.wait_ge(roped, n + 1)
            for tt in range(NT):
                copy(("kT", tt), kT[:, 0:NKV, tt * P:(tt + 1) * P],
                     bank(1 + tt, 0, NKV * P).rearrange("p (c s) -> p c s", c=NKV))
            attend(UNITS0)

            two_banks = lambda tt: psum[:, 2 * tt:2 * tt + 2, :].rearrange("p a b -> p (a b)")
            post_norm(POST0, [[("mix", 0, tt, hf) for hf in range(2)] for tt in range(NT)], two_banks, xn)
            pre_norm(FPRE0, hres)
            for m in range(CUT):
                cut_rest(m, FFN0 + m, m + 1)
            for tt in range(NT):
                for hf in range(2):
                    label = ("f0T", tt, hf)
                    part = (slice(None), slice(4 * hf, 4 * hf + 4), slice(tt * P, (tt + 1) * P))
                    lower_part(label, x_lo[part], bank(bk.at[label][0]).rearrange("p (c s) -> p c s", c=4),
                               x_hi[part])
            pre_norm(MEM1, memb)

            for i, (kind, b, half) in enumerate(pieces):
                tt = half
                if (kind == "g" and b >= 1) or (kind, b) == ("d", NB - 2):
                    hb = b - 1 if kind == "g" else NB - 1
                    lower_part(("h0T", hb, tt), h_lo[:, tt, :], bank(7), h_hi[:, tt, :])
                if kind == "u":
                    label = ("u0", b, tt)
                    dve.wait_ge(*bk.empty(("g0", b, tt)))
                    dve.wait_ge(*bk.full(label))
                    dve.tensor_tensor(hid0[:, b % 2, tt, :].rearrange("p (c q) -> p q c", c=CB),
                                      act0[:, tt, :].rearrange("p (q c) -> p q c", c=CB),
                                      bank(bk.at[label][0]).rearrange("p (q c) -> p q c", c=CB),
                                      ALU.mult).then_inc(bk.empty_sem(label), 1)
                if i + CUT < NPC:
                    cut_rest(i + CUT, FFN0 + i + CUT, i + CUT + 1)
            drain_turned("mem1T", memT)
            post_norm(FPOST0, [[("y0", tt, hf) for hf in range(2)] for tt in range(NT)], two_banks,
                      mixT[:, :, :].rearrange("p (t a) s -> p t (a s)", t=NT))
            pre_norm(PRE1, hres)
            drain_turned("x1T", xT)

            def heads(i, dst, scale=None):
                copy(("p", i), dst, bank(bk.at["p", i][0]).rearrange("p (c s) -> p c s", c=2), scale)

            heads(1, qT[:, 2:4, :], SCALE)
            heads(3, kT[:, 0:2, :])
            heads(5, kT[:, 4:6, :])
            copy(("v1a", 1), v[:, 1, 0:512], bank(1))
            copy(("v1b", 1), v[:, 1, 512:768], bank(3, 0, 256))

            def softplus(p):
                x = soft[:, p % 2, :, :]
                dve.wait_ge(soft_a, p + 1)
                for b in range(2):
                    dve.scalar_tensor_tensor(out=x[:, b, :], in0=bank(2 * (p % 3) + b, 0, 384), scalar=0.0,
                                             in1=x[:, b, :], op0=ALU.max, op1=ALU.add)\
                        .then_inc(bk.empty_sem(("z", p, b)), 1)
                for b in range(2):
                    dve.wait_ge(*bk.empty(("z", p, b)))
                clear(x).then_inc(soft_b, 1)

            def clear(x):
                dve.tensor_tensor(x[:, :, 0:P], x[:, :, 0:P], clamp[:, :].unsqueeze(1).to_broadcast((P, 2, P)),
                                  ALU.min)
                return dve.tensor_tensor(x[:, :, 2 * P:3 * P], x[:, :, 2 * P:3 * P],
                                         clamp[:, :].unsqueeze(1).to_broadcast((P, 2, P)), ALU.min)

            NP = NH // 2
            for s in range(NP + 1):
                if s < NP:
                    softplus(s)
                if s >= 1:
                    for b in range(2):
                        dve.wait_ge(*bk.empty(("zc", s - 1, b)))
                    clear(stick[:, (s - 1) % 2, :, :]).then_inc(stick_b, 1)
            attend(UNITS1)
            post_norm(POST1, [[("mix", 1, tt, hf) for hf in range(2)] for tt in range(NT)], two_banks, xn)
            pre_norm(FPRE1, hres)
            drain_turned("f1T", xT)

            dve.wait_ge(*bk.full(("logits",)))
            dve.tensor_copy(logits[:, :, :], bank(4, 0, NT * NE).rearrange("p (t e) -> p t e", t=NT))\
                .then_inc(bk.empty_sem(("logits",)), 1)
            dve.wait_ge(*bk.empty(("logits",)))
            for tt in range(NT):
                ins = dve.max(top_v[:, tt, :], logits[:, tt, :])
            link(ins)
            for tt in range(NT):
                dve.max_index(top_i[:, tt, :], top_v[:, tt, :], logits[:, tt, :])
            dve.tensor_tensor(gate2[:, :, 0:1], top_v[:, :, 1:2], top_v[:, :, 0:1], ALU.subtract)\
                .then_inc(gap_ok, 1)
            dve.wait_ge(gap_ok, 1)
            link(dve.tensor_copy(top_f[:, :, :], top_i[:, :, :]))
            for tt in range(NT):
                for c in range(2):
                    ins = dve.tensor_scalar(mask2[:, tt, c, :], iota_s[:, 0:NE], top_f[:, tt, c:c + 1], None,
                                            ALU.is_equal)
            link(ins)
            dve.tensor_tensor(chosen[:, :, :], mask2[:, :, 0, :], mask2[:, :, 1, :], ALU.add)\
                .then_inc(chosen_ok, 1)
            dve.wait_ge(gexp_ok, 1)
            link(dve.tensor_scalar(gate2[:, :, 2:3], gate2[:, :, 1:2], 1.0, None, ALU.add))
            link(dve.reciprocal(gate2[:, :, 2:3], gate2[:, :, 2:3]))
            link(dve.tensor_tensor(gate2[:, :, 3:4], gate2[:, :, 1:2], gate2[:, :, 2:3], ALU.mult))
            for tt in range(NT):
                ins = dve.tensor_scalar(gates[:, tt, :], mask2[:, tt, 0, :], gate2[:, tt, 2:3], None, ALU.mult)
            link(ins)
            for tt in range(NT):
                ins = dve.scalar_tensor_tensor(out=gates[:, tt, :], in0=mask2[:, tt, 1, :],
                                               scalar=gate2[:, tt, 3:4], in1=gates[:, tt, :],
                                               op0=ALU.mult, op1=ALU.add)
            link(ins)
            dve.wait_ge(*bk.full(("rank",)))
            dve.tensor_copy(over[:, 0, :], bank(5, 2 * NE, 3 * NE))
            dve.scalar_tensor_tensor(out=rank[:, :, :], in0=bank(5, 0, NT * NE).rearrange("p (t e) -> p t e", t=NT),
                                     scalar=1.0, in1=chosen[:, :, :], op0=ALU.add, op1=ALU.mult)\
                .then_inc(bk.empty_sem(("rank",)), 1)
            dve.wait_ge(*bk.empty(("rank",)))
            dve.memset(slot_of[:, :, NE + 3:MAX_JOBS + 1], -1.0)
            dve.memset(gate_of[:, :, NE + 3:MAX_JOBS + 1], 0.0)
            dve.tensor_scalar(slot_of[:, :, 0:NE], rank[:, :, :], -1.0, None, ALU.add)
            dve.tensor_copy(gate_of[:, :, 0:NE], gates[:, :, :])
            link(dve.tensor_scalar(over[:, 1, :], over[:, 0, :], float(CAP), None, ALU.is_gt))
            link(dve.tensor_tensor_scan(over[:, 2, :], ones[:, 0:NE], over[:, 1, :], 0.0, ALU.mult, ALU.add))
            for o in range(3):
                ins = dve.scalar_tensor_tensor(out=over_sel[:, o, :], in0=over[:, 2, :], scalar=float(o + 1),
                                               in1=over[:, 1, :], op0=ALU.is_equal, op1=ALU.mult)
            link(ins)
            for o in range(3):
                for tt in range(NT):
                    link(dve.scalar_tensor_tensor(out=junk8[:, 0:NE], in0=slot_of[:, tt, 0:NE],
                                                  scalar=-float(CAP), in1=over_sel[:, o, :], op0=ALU.add,
                                                  op1=ALU.mult, accum_out=slot_of[:, tt, NE + o:NE + o + 1]))
                    link(dve.scalar_tensor_tensor(out=junk8[:, 0:NE], in0=gates[:, tt, :], scalar=1.0,
                                                  in1=over_sel[:, o, :], op0=ALU.mult, op1=ALU.mult,
                                                  accum_out=gate_of[:, tt, NE + o:NE + o + 1]))
                link(dve.scalar_tensor_tensor(out=junk8[:, 0:NE], in0=iota_s[:, 0:NE], scalar=1.0,
                                              in1=over_sel[:, o, :], op0=ALU.mult, op1=ALU.mult,
                                              accum_out=job_f[:, o:o + 1]))
            link(dve.tensor_scalar(job_f[:, 3:4], over[:, 2, NE - 1:NE], float(NE), None, ALU.add))
            dve.tensor_copy(job_i[:, :], job_f[:, :]).then_inc(tables_ok, 1)

            for tt in range(NT):
                ins = dve.tensor_scalar(pick[:, tt, :], iota_s[:, :], slot_of[:, tt, 0:1], None, ALU.is_equal)
            ins.then_inc(pick_ok, 1)
            link(dve.memset(esum[:, :, :], 0.0))
            def gathered(label, hf, j=None):
                part = (slice(None), slice(4 * hf, 4 * hf + 4), slice(None))
                lower_part(label, picked_lo[part], bank(4 + hf).rearrange("p (k s) -> p k s", k=4),
                           picked_hi[part], j)

            for m in range(CUT):
                cut_rest(m, m, NPC + m + 1)
            for hf in range(2):
                gathered(("pre-gather", hf), hf)
            dve.wait_ge(tables_ok, 1)
            n_jobs = dve.value_load(job_i[0:1, 3:4], min_val=NE, max_val=MAX_JOBS)
            with dve.Fori(0, n_jobs) as j:
                def full(label):
                    dve.wait_ge(*bk.full(label, j))

                for i, (kind, b, half) in enumerate(pieces):
                    if (kind, half) == ("g", 1) and b >= 1:
                        lower_part(("T", b - 1), h_lo[:, (b - 1) % 2, :], bank(7), h_hi[:, (b - 1) % 2, :], j)
                    if (kind, half) == ("u", 1):
                        dve.wait_ge(*bk.empty(("g", b), j))
                        full(("u", b))
                        dve.tensor_tensor(hid1[:, b % 2, :].rearrange("p (c q) -> p q c", c=CB),
                                          act1[:, b % 2, :].rearrange("p (q c) -> p q c", c=CB),
                                          bank(bk.at["u", b][0]).rearrange("p (q c) -> p q c", c=CB),
                                          ALU.mult).then_inc(bk.empty_sem(("u", b)), 1)
                    if (kind, b, half) == ("d", 0, 0):
                        full(("pickT",))
                        for tt in range(NT):
                            ins = dve.tensor_scalar(pick[:, tt, :], iota_s[:, :],
                                                    slot_of[:, tt, bass.ds(j + 1, 1)], None, ALU.is_equal)
                        ins.then_inc(pick_ok, 1)
                    if (kind, b, half) == ("d", NB - 2, 0):
                        lower_part(("T", NB - 1), h_lo[:, (NB - 1) % 2, :], bank(7), h_hi[:, (NB - 1) % 2, :], j)
                    if i == NPC - 1:
                        full(("y", 1))
                        dve.tensor_copy(y_sb[:, 512:1024], bank(1)).then_inc(bk.empty_sem(("y", 1)), 1)
                    cut_rest(i + CUT, i + CUT, NPC * j + (NPC + i + CUT + 1))
                for hf in range(2):
                    gathered(("gather", hf), hf, j)
                for tt, hf in [(0, 0), (0, 1), (1, 0), (1, 1)]:
                    full(("back", tt, hf))
                    e = esum[:, tt, hf * 512:(hf + 1) * 512]
                    dve.scalar_tensor_tensor(out=e, in0=bank(bk.at["back", tt, hf][0]),
                                             scalar=gate_of[:, tt, bass.ds(j, 1)], in1=e, op0=ALU.mult,
                                             op1=ALU.add).then_inc(bk.empty_sem(("back", tt, hf)), 1)
            for label in [("back", tt, hf) for tt in range(NT) for hf in range(2)]:
                dve.wait_ge(*bk.empty(label, n_jobs - 1))
            dve.sem_inc(tables_ok, 1)
            for tt in range(NT):
                scale_rows(FPOST1, tt, xn[:, tt, :], esum[:, tt, :])
                dve.tensor_tensor(hres[:, tt, :], hres[:, tt, :], xn[:, tt, :], ALU.add).then_inc(added, 1)

        @block.gpsimd
        def _(pool):
            links = [0]

            def link(ins):
                links[0] += 1
                ins.then_inc(pool_chain, 1)
                pool.wait_ge(pool_chain, links[0])

            def load_gain(n):
                g = t[NORMS[n]].rearrange("(a d) -> a d", a=1).to_broadcast((P, D))
                pool.dma_start(gains[:, n % NG, :], g).then_inc(gain_in[n % NG], 16)

            for n in range(NG):
                load_gain(n)
            for m, val in ((ident, 0.0), (upper_neg, 0.0), (ones_neg, -1.0), (ones, 1.0), (before, 0.0),
                           (band, 0.0), (clamp, 0.0), (mhalf, -0.5), (halfpi, TWO_PI / 4)):
                pool.memset(m[:, :], val)
            for i in range(HD // 2):
                pool.memset(invf[:, i:i + 1], THETA ** (-2.0 * i / HD))
            link(pool.iota(iota_i, pattern=[[1, P]], base=0, channel_multiplier=0))
            pool.tensor_copy(iota_s[:, :], iota_i)

            def where(m, lo, cmp, fill, step, ch):
                x = m[:, lo:lo + P]
                return pool.affine_select(out=x, in_=x, compare_op=cmp, fill=fill, base=0, pattern=[[step, P]],
                                          channel_multiplier=ch)

            where(ident, 0, ALU.not_equal, 1.0, -1, 1)
            where(upper_neg, 0, ALU.is_gt, -1.0, 1, -1)
            where(before, 0, ALU.is_ge, 1.0, -1, 1)
            where(band, 0, ALU.is_gt, NEG, 1, -1)
            where(band, P, ALU.is_ge, NEG, -1, 1)
            link(where(clamp, 0, ALU.is_ge, BIG, -1, 1))
            pool.sem_inc(consts, 1)

            for norm in range(len(NORMS)):
                for tt in range(NT):
                    x = rstd[:, norm, tt:tt + 1]
                    pool.wait_ge(summed, NT * norm + tt + 1)
                    link(pool.tensor_scalar(x, ssq[:, norm, tt:tt + 1], 1.0 / D, EPS, ALU.mult, ALU.add))
                    pool.tensor_tensor(x, x, mhalf[:, 0:1], ALU.pow).then_inc(rstd_ok, 1)
                if norm + NG < len(NORMS):
                    pool.wait_ge(scaled, NT * (norm + 1))
                    load_gain(norm + NG)

        @block.sync
        def _(sp):
            sp.dma_start(memb[:, :, :], t["mem"].rearrange("a (t p) d -> p (a t) d", p=P)).then_inc(mem_in, 16)
            sp.dma_start(hres[:, :, :], t["x"].rearrange("a (t p) d -> p (a t) d", p=P)).then_inc(x_in, 16)
            with nc.allow_non_contiguous_dma(reason="256 positions and 12 sinks"):
                sp.dma_start(pos_i[:, :], t["positions"].rearrange("a (t p) -> p (a t)", p=P)).then_inc(small_in, 16)
                sp.dma_start(sinks[:, :], t["l0_sinks"].rearrange("(a h) -> a h", a=1).to_broadcast((P, NH)))\
                    .then_inc(small_in, 16)
                sp.dma_start(wr[:, :, :], t["l1_w_router"].rearrange("(k p) e -> p k e", p=P)).then_inc(small_in, 16)
            def load(n, src):
                _, c, w = src.shape
                sp.dma_start(raw_at(n, c, w), src).then_inc(raw_full[n % RAW], 16)

            for m in range(NPC):
                free_after[FFN0 + m] = (lo_ok, m + 1)

            for n, src in enumerate(loads):
                if n >= RAW:
                    sp.wait_ge(*free_after[n - RAW])
                load(n, src)

            def expert_load(e, m, free):
                kind, b, half = pieces[m]
                sp.wait_ge(*free)
                if (kind, b, half) == ("d", 0, 0):
                    sp.sem_inc(sp_step, 1)
                if kind == "d":
                    w = t["l1_w_down"][bass.ds(e, 1), b * FB:(b + 1) * FB, :]
                    src = w.rearrange("e (p c) n -> p (e c) n", c=CB)[:, 2 * half:2 * half + 2, :]
                else:
                    w = t["l1_w_gate" if kind == "g" else "l1_w_up"]
                    src = w[bass.ds(e, 1), 4 * half * P:4 * (half + 1) * P, b * FB:(b + 1) * FB]\
                        .rearrange("e (k p) n -> p (e k) n", p=P)
                load(m, src)

            def cut_of(j, m):
                return lo_ok, NPC * j + (NPC + m - RAW + 1)

            for m in range(RAW):
                expert_load(0, m, free_after[PRE + m - RAW])
            with sp.Fori(0, NE - 1) as j:
                for m in range(RAW, NPC):
                    expert_load(j, m, cut_of(j, m))
                for m in range(RAW):
                    expert_load(j + 1, m, cut_of(j, NPC + m))
            for m in range(RAW, NPC):
                expert_load(NE - 1, m, cut_of(NE - 1, m))
            sp.wait_ge(tables_ok, 1)
            n_jobs = sp.value_load(job_i[0:1, 3:4], min_val=NE, max_val=MAX_JOBS)
            with sp.If(n_jobs > NE):
                with sp.Fori(NE, n_jobs) as j:
                    e = sp.value_load(job_i[0:1, bass.ds(j - NE, 1)], min_val=0, max_val=NE - 1)
                    for m in range(NPC):
                        expert_load(e, m, cut_of(j, m))
            for m in range(CUT):
                expert_load(0, m, cut_of(n_jobs, m))
            for tt in range(NT):
                sp.wait_ge(added, 6 + tt + 1)
                sp.dma_start(t["out"][0, tt * P:(tt + 1) * P, :], hres[:, tt, :]).then_inc(stored, 16)
            sp.wait_ge(stored, 16 * NT)


_INS = ["x", "mem", "positions", "l0_attn_pre_g", "l0_mem_g", "l0_w_in", "l0_w_mem_kv", "l0_sinks", "l0_w_out",
        "l0_attn_post_g", "l0_ffn_pre_g", "l0_w_gate", "l0_w_up", "l0_w_down", "l0_ffn_post_g",
        "l1_attn_pre_g", "l1_mem_g", "l1_w_in", "l1_w_mem_kv", "l1_w_out", "l1_attn_post_g", "l1_ffn_pre_g",
        "l1_w_router", "l1_w_gate", "l1_w_up", "l1_w_down", "l1_ffn_post_g"]


def kernel(**inputs):
    import numpy as np
    import concourse.bacc as bacc
    from concourse.bass_utils import run_bass_kernel_spmd

    nc = bacc.Bacc("TRN2", target_bir_lowering=False, num_devices=1)
    arrays, t = {}, {}
    for name in _INS:
        a = np.ascontiguousarray(inputs[name])
        arrays[f"in_{name}"] = a
        t[name] = nc.dram_tensor(f"in_{name}", a.shape, mybir.dt.from_np(a.dtype), kind="ExternalInput").ap()
    t["out"] = nc.dram_tensor("out", (1, S, D), F32, kind="ExternalOutput").ap()
    trunk(nc, t)
    r = run_bass_kernel_spmd(nc, [arrays], core_ids=[0])
    return r.results[0]["out"]
```

```python
from contextlib import ExitStack

import concourse.bass as bass
from concourse import mybir

P = 128
D = 1024
KD = D // P
S = 256
NT = S // P
HD = 64
NH = 12
NKV = 3
NC = 4
GQ = NH // NKV
MEM = 256
FF = 3584
FB = 512
NB = FF // FB
CB = FB // P
NE = 8
CAP = P
MAX_JOBS = NE + NE // 2 - 1
EPS = 1e-6
SCALE = HD ** -0.5
THETA = 10000.0
PW = KD * FB // 2
RAW = 6
CUT = 3
NPC = 6 * NB
NEG = -1.0e30
BIG = 3.0e38
TWO_PI = 6.283185307179586
TP1 = 6.28125
TP2 = 0.0019350051879882812
TP3 = TWO_PI - TP1 - TP2
ROUND = 12582912.0

ALU = mybir.AluOpType
ACT = mybir.ActivationFunctionType
AX = mybir.AxisListType
F32 = mybir.dt.float32
F32R = mybir.dt.float32r
BF16 = mybir.dt.bfloat16
I32 = mybir.dt.int32
U32 = mybir.dt.uint32

NORMS = ["l0_mem_g", "l0_attn_pre_g", "l0_attn_post_g", "l0_ffn_pre_g", "l1_mem_g", "l0_ffn_post_g",
         "l1_attn_pre_g", "l1_attn_post_g", "l1_ffn_pre_g", "l1_ffn_post_g"]
MEM0, PRE0, POST0, FPRE0, MEM1, FPOST0, PRE1, POST1, FPRE1, FPOST1 = range(len(NORMS))
NORM_ORDER = [(MEM0, 0), (MEM0, 1), (PRE0, 0), (PRE0, 1), (POST0, 0), (FPRE0, 0), (POST0, 1), (FPRE0, 1),
              (MEM1, 0), (MEM1, 1), (FPOST0, 0), (PRE1, 0), (FPOST0, 1), (PRE1, 1),
              (POST1, 0), (FPRE1, 0), (POST1, 1), (FPRE1, 1), (FPOST1, 0), (FPOST1, 1)]
NORM_COUNT = {x: n + 1 for n, x in enumerate(NORM_ORDER)}
NG = 2


TURN = (1, 1, 4, 4, 5, 5, 2, 8)
USED_TURN = 27


class Banks:

    def __init__(self, filled, drained):
        self.filled, self.drained = filled, drained
        self.count = [0] * len(filled)
        self.at = {}

    def fill(self, label, bank, j=0):
        n = self.count[bank]
        self.count[bank] += 1
        self.at[label] = (bank, n + 1)
        return self.drained[bank], n + j * TURN[bank]

    def full(self, label, j=0):
        bank, n = self.at[label]
        return self.filled[bank], n + j * TURN[bank]

    def empty(self, label, j=0):
        bank, n = self.at[label]
        return self.drained[bank], n + j * TURN[bank]

    def full_sem(self, label):
        return self.filled[self.at[label][0]]

    def empty_sem(self, label):
        return self.drained[self.at[label][0]]


def trunk(nc, t):
    with ExitStack() as ctx:
        def sb(name, shape, dt=F32):
            return ctx.enter_context(nc.sbuf_tensor(name, shape, dt))

        def sem(name):
            return ctx.enter_context(nc.semaphore(name))

        raw = sb("raw", [P, RAW, PW])
        w_hi = sb("w_hi", [P, CUT, PW], F32R)
        w_lo = sb("w_lo", [P, CUT, PW], F32R)
        x_hi = sb("x_hi", [P, KD, S], F32R)
        x_lo = sb("x_lo", [P, KD, S], F32R)
        h_hi = sb("h_hi", [P, 2, FB], F32R)
        h_lo = sb("h_lo", [P, 2, FB], F32R)
        hres = sb("hres", [P, NT, D])
        memb = sb("memb", [P, NT, D])
        xn = sb("xn", [P, NT, D])
        reg_a = sb("reg_a", [P, 2 * D])
        reg_b = sb("reg_b", [P, 2 * D])
        mixT = sb("mixT", [P, KD, S])
        gains = sb("gains", [P, NG, D])
        work = sb("work", [P, 5632])
        ident = sb("ident", [P, P])
        upper_neg = sb("upper_neg", [P, P])
        ones_neg = sb("ones_neg", [P, P])
        ones = sb("ones", [P, P])
        band = sb("band", [P, 2 * P])
        clamp = sb("clamp", [P, P])
        iota_s = sb("iota_s", [P, P])
        iota_i = work[:, 0:P].bitcast(I32)
        before = work[:, P:2 * P]
        cos2 = sb("cos2", [P, NT, HD])
        sin2 = sb("sin2", [P, NT, HD])
        rope_s = sb("rope_s", [P, 4, NT, HD // 2])
        invf = sb("invf", [P, HD // 2])
        pos_i = sb("pos_i", [P, NT], I32)
        pos_f = sb("pos_f", [P, NT])
        sinks = sb("sinks", [P, NH])
        nsinks = sb("nsinks", [P, NH])
        mhalf = sb("mhalf", [P, 1])
        halfpi = sb("halfpi", [P, 1])
        ssq = sb("ssq", [P, len(NORMS), NT])
        rstd = sb("rstd", [P, len(NORMS), NT])
        NU = 2 * (NKV + 1) * NT
        nmax = sb("nmax", [P, NU, 4])
        psum_e = sb("psum_e", [P, NU, 4])
        esink = sb("esink", [P, NU, 4])
        recip = sb("recip", [P, NU, 4])
        wr = sb("wr", [P, KD, NE])
        logits = sb("logits", [P, NT, NE])
        top_v = sb("top_v", [P, NT, 8])
        top_i = sb("top_i", [P, NT, 8], U32)
        top_f = sb("top_f", [P, NT, 8])
        gate2 = sb("gate2", [P, NT, 4])
        mask2 = sb("mask2", [P, NT, 2, NE])
        chosen = sb("chosen", [P, NT, NE])
        chosen_b = sb("chosen_b", [P, NT, NE], BF16)
        ones_b = sb("ones_b", [P, P], BF16)
        before_b = sb("before_b", [P, P], BF16)
        gates = sb("gates", [P, NT, NE])
        rank = sb("rank", [P, NT, NE])
        over = sb("over", [P, 3, NE])
        over_sel = sb("over_sel", [P, 3, NE])
        junk8 = sb("junk8", [P, 16])
        slot_of = sb("slot_of", [P, NT, MAX_JOBS + 1])
        gate_of = sb("gate_of", [P, NT, MAX_JOBS + 1])
        job_f = sb("job_f", [P, 4])
        job_i = sb("job_i", [P, 4], I32)

        psum = ctx.enter_context(nc.psum_tensor("psum", [P, 8, 512], F32))

        memT = reg_a[:, :].rearrange("p (k s) -> p k s", k=KD)
        xT = reg_b[:, :].rearrange("p (k s) -> p k s", k=KD)
        probs = reg_a[:, :].rearrange("p (u b h k) -> p u b h k", u=2, b=2, h=2)
        probsT0 = reg_b[:, :].rearrange("p (u b h k q) -> p u b h k q", u=2, b=2, h=2, k=2)
        probsT1 = xn[:, :, :].rearrange("p u (b h k q) -> p u b h k q", b=2, h=2, k=2)
        rope_q = reg_a[:, 0:1024].rearrange("p (u c) -> p u c", u=2)
        rope_a = reg_a[:, 1024:1536]
        rope_b = reg_a[:, 1536:2048]
        soft = reg_a[:, 0:1536].rearrange("p (u b c) -> p u b c", u=2, b=2)
        stick = reg_b[:, 0:1536].rearrange("p (u b c) -> p u b c", u=2, b=2)
        qT = work[:, 0:1536].rearrange("p (c s) -> p c s", c=6)
        kT = work[:, 1536:3072].rearrange("p (c s) -> p c s", c=6)
        v = work[:, 3072:4608].rearrange("p (t c) -> p t c", t=NT)
        kmT = work[:, 4608:5120].rearrange("p (c s) -> p c s", c=2)
        vm = work[:, 5120:5632].rearrange("p (t c) -> p t c", t=NT)
        qcT = mixT[:, 6:8, :]
        kdup = mixT[:, 0:3, :].rearrange("p k s -> p (k s)").rearrange("p (t g u c) -> p t g u c", t=NT, g=NKV, u=2)
        act0 = work[:, 0:1024].rearrange("p (t c) -> p t c", t=2)
        hid0 = work[:, 1024:3072].rearrange("p (u t c) -> p u t c", u=2, t=NT)
        act1 = act0
        hid1 = work[:, 1024:2048].rearrange("p (u c) -> p u c", u=2)
        pick = work[:, 2560:2816].rearrange("p (t s) -> p t s", t=NT)
        pickT = work[:, 2816:3072].rearrange("p (t s) -> p t s", t=NT)
        picked_hi, picked_lo = x_hi[:, :, 0:CAP], x_lo[:, :, 0:CAP]
        y_sb = work[:, 4096:5120]
        esum = memb

        def unit(u, layer, i, tt):
            if layer == 0 and i < NKV:
                return u, layer, i, tt, qT, kT, (0, (tt + 1) * P), v, 0
            return u, layer, i, tt, qcT, kmT, (0, MEM), vm, 0

        UNITS0 = [unit(NT * i + tt, 0, i, tt) for i in range(NKV + 1) for tt in range(NT)]
        UNITS1 = [unit(len(UNITS0) + tt, 1, NKV, tt) for tt in range(NT)]

        def probsT(u):
            return (probsT0 if u < len(UNITS0) else probsT1)[:, u % 2]

        def bank(b, lo=0, hi=512):
            return psum[:, b, lo:hi]

        filled = [sem(f"bank{b}_filled") for b in range(8)]
        drained = [sem(f"bank{b}_drained") for b in range(8)]
        raw_full = [sem(f"raw{s}_full") for s in range(RAW)]
        hi_ok = sem("hi_ok")
        lo_ok = sem("lo_ok")
        used = sem("used")
        part_hi = sem("part_hi")
        x_in, mem_in = [[sem(f"{name}{tt}_in") for tt in range(NT)] for name in ("x", "mem")]
        small_in = sem("small_in")
        gain_in = [sem(f"gain{i}_in") for i in range(NG)]
        consts, ident_ok = sem("consts"), sem("ident_ok")
        summed, rstd_ok, scaled, added = sem("summed"), sem("rstd_ok"), sem("scaled"), sem("added")
        act_chain, dve_chain, pool_chain = sem("act_chain"), sem("dve_chain"), sem("pool_chain")
        angles, sines = sem("angles"), sem("sines")
        roped = sem("roped")
        max_ok, exp_ok, norm_ok = sem("max_ok"), sem("exp_ok"), sem("norm_ok")
        soft_a, soft_b, stick_b = sem("soft_a"), sem("soft_b"), sem("stick_b")
        gap_ok, gexp_ok, chosen_ok, tables_ok = sem("gap_ok"), sem("gexp_ok"), sem("chosen_ok"), sem("tables_ok")
        pick_ok = sem("pick_ok")
        stored = sem("stored")
        sp_step = sem("sp_step")

        bk = Banks(filled, drained)

        def cols(w, lo, hi):
            w = w.rearrange("(k p) n -> p k n", p=P)
            return [w[:, 4 * half:4 * half + 4, lo:hi] for half in range(2)]

        def down_rows(w, b):
            w = w[b * FB:(b + 1) * FB, :].rearrange("(p c) n -> p c n", c=CB)
            return [w[:, 2 * half:2 * half + 2, :] for half in range(2)]

        pieces = []
        for b in range(NB + 1):
            pieces += [(kind, b, half) for kind in "gu" for half in range(2) if b < NB]
            pieces += [("d", b - 1, half) for half in range(2) if b >= 1]
        place = {x: n for n, x in enumerate(pieces)}
        assert len(pieces) == NPC

        IN0 = [(0, 512), (512, 1024), (1024, 1152), (1152, 1408)]
        IN1 = [(i * 512, (i + 1) * 512) for i in (4, 0, 1, 2, 3)]
        loads = cols(t["l0_w_mem_kv"], 0, 512)
        for lo, hi in IN0:
            loads += cols(t["l0_w_in"], lo, hi)
        for lo in (0, 512):
            loads += cols(t["l0_w_out"], lo, lo + 512)
        FFN0 = len(loads)
        for kind, b, half in pieces:
            if kind == "d":
                loads.append(down_rows(t["l0_w_down"], b)[half])
            else:
                loads.append(cols(t["l0_w_gate" if kind == "g" else "l0_w_up"], b * FB, (b + 1) * FB)[half])
        loads += cols(t["l1_w_mem_kv"], 0, 512)
        for lo, hi in IN1:
            loads += cols(t["l1_w_in"], lo, hi)
        for lo in (0, 512):
            loads += cols(t["l1_w_out"], lo, lo + 512)
        PRE = len(loads)
        assert PRE % RAW == 0 and NPC % RAW == 0 and NPC % CUT == 0

        free_after = {}
        cut_free = {}
        job_free = {}

        def raw_at(n, c, w):
            return raw[:, n % RAW, 0:c * w].rearrange("p (c n) -> p c n", c=c)

        def cut_at(m, kind):
            c = 2 if kind == "d" else 4
            return [x[:, m % CUT, :].rearrange("p (c n) -> p c n", c=c) for x in (w_hi, w_lo)]

        block = ctx.enter_context(nc.Block())

        @block.tensor
        def _(pe):
            n_raw = [0]

            class Block:

                def __init__(self, w=FB):
                    self.n, self.w = n_raw[0], w
                    for n in (self.n, self.n + 1):
                        pe.wait_ge(raw_full[n % RAW], 16 * (n // RAW + 1))
                    n_raw[0] += 2

                def at(self, k, lo, hi):
                    return raw_at(self.n + k // 4, 4, self.w)[:, k % 4, lo:hi]

                def done(self, label):
                    free_after[self.n] = free_after[self.n + 1] = bk.full(label)

            def begin(label, b):
                s, n = bk.fill(label, b)
                if n > 0:
                    pe.wait_ge(s, n)

            def end(ins, label):
                ins.then_inc(bk.full_sem(label), 1)

            def turn(norm, tag, banks, tiles=range(NT), src=xn):
                for tt in tiles:
                    pe.wait_ge(scaled, NORM_COUNT[norm, tt])
                    for hf in range(2):
                        label = (tag, tt, hf)
                        begin(label, banks[2 * tt + hf])
                        for c in range(4):
                            k = 4 * hf + c
                            ins = pe.transpose(bank(banks[2 * tt + hf], c * P, (c + 1) * P),
                                               src[:, tt, k * P:(k + 1) * P], ident[:, :])
                        end(ins, label)

            def turned(tag, tt=None):
                for u in range(NT):
                    if tt in (None, u):
                        for hf in range(2):
                            pe.wait_ge(*bk.empty((tag, u, hf)))

            def memory_kv(layer, srcT, banks):
                w = Block()
                begin(("kmT", layer), banks[0])
                for c in range(2):
                    for k in range(KD):
                        ins = pe.matmul(bank(banks[0], c * S, (c + 1) * S), w.at(k, c * P, (c + 1) * P),
                                        srcT[:, k, :], start=(k == 0), stop=(k == KD - 1))
                end(ins, ("kmT", layer))
                begin(("vm", layer), banks[1])
                for tt in range(NT):
                    for k in range(KD):
                        ins = pe.matmul(bank(banks[1], tt * 256, (tt + 1) * 256),
                                        srcT[:, k, tt * P:(tt + 1) * P], w.at(k, 256, 512),
                                        start=(k == 0), stop=(k == KD - 1))
                end(ins, ("vm", layer))
                w.done(("vm", layer))

            def rows(label, b, srcT, tt, w, lo, hi, at=0, first=True, last=True):
                if first:
                    begin(label, b)
                for k in range(KD):
                    ins = pe.matmul(bank(b, at, at + hi - lo), srcT[:, k, tt * P:(tt + 1) * P],
                                    w.at(k, lo, hi), start=(k == 0), stop=(k == KD - 1))
                if last:
                    end(ins, label)
                return ins

            def turned_cols(label, b, w, los):
                begin(label, b)
                for i, lo in enumerate(los):
                    for k in range(KD):
                        ins = pe.matmul(bank(b, i * S, (i + 1) * S), w.at(k, lo, lo + P), xT[:, k, :],
                                        start=(k == 0), stop=(k == KD - 1))
                end(ins, label)
                return ins

            def scores(u, layer, i, tt, q, k, keys):
                lo, hi = keys
                for b in range(2):
                    begin(("s", u, b), 2 * (u % 2) + b)
                for s2 in range(2):
                    for b in range(2):
                        r = slice(HD * b, HD * b + HD)
                        kc = k[r, i if layer == 0 and i < NKV else s2, lo:hi]
                        qc = q[r, (2 * i if i < NKV else 0) + s2, tt * P:(tt + 1) * P]
                        ins = pe.matmul(bank(2 * (u % 2) + b, s2 * (hi - lo), (s2 + 1) * (hi - lo)), qc, kc,
                                        start=True, stop=True)
                        if s2 == 1:
                            end(ins, ("s", u, b))

            def turn_probs(u, nk):
                pe.wait_ge(norm_ok, u + 1)
                for b in range(2):
                    begin(("pT", u, b), 4 + b)
                    for s2 in range(2):
                        for kt in range(nk):
                            ins = pe.transpose(bank(4 + b, (s2 * 2 + kt) * P, (s2 * 2 + kt + 1) * P),
                                               probs[:, u % 2, b, s2, kt * P:(kt + 1) * P], ident[:, :])
                    end(ins, ("pT", u, b))

            def weigh(u, i, nk, val, kt0):
                begin(("o", u), 6 + u % 2)
                for b in range(2):
                    pe.wait_ge(*bk.empty(("pT", u, b)))
                for s2 in range(2):
                    for b in range(2):
                        h = (0 if i < NKV else 2 * s2 + b) * HD + (i * HD if i < NKV else 0)
                        for kt in range(nk):
                            ins = pe.matmul(psum[HD * b:HD * b + HD, 6 + u % 2, s2 * P:(s2 + 1) * P],
                                            val[:, kt0 + kt, h:h + HD], probsT(u)[:, b, s2, kt, :],
                                            start=(kt == 0), stop=(kt == nk - 1), skip_group_check=True)
                end(ins, ("o", u))

            def attend(units):
                for s in range(-1, len(units) + 2):
                    if s + 1 < len(units):
                        u, layer, i, tt, q, k, keys, val, kt0 = units[s + 1]
                        scores(u, layer, i, tt, q, k, keys)
                    if s >= 2:
                        u, i, keys, val, kt0 = (units[s - 2][x] for x in (0, 2, 6, 7, 8))
                        weigh(u, i, (keys[1] - keys[0]) // P, val, kt0)
                    if 1 <= s <= len(units):
                        u, keys = units[s - 1][0], units[s - 1][6]
                        turn_probs(u, (keys[1] - keys[0]) // P)

            def project_out(layer, last_unit_labels):
                for label in last_unit_labels:
                    pe.wait_ge(*bk.empty(label))
                ws = []
                for tt in range(NT):
                    for hf in range(2):
                        if tt == 0:
                            ws.append(Block())
                        rows(("mix", layer, tt, hf), 2 * tt + hf, mixT, tt, ws[hf], 0, FB)
                for hf in range(2):
                    ws[hf].done(("mix", layer, NT - 1, hf))

            pe.wait_ge(ident_ok, 1)
            turn(MEM0, "mem0T", (0, 1, 2, 3))
            turned("mem0T")
            memory_kv(0, memT, (6, 7))
            turn(PRE0, "x0T", (0, 1, 2, 3))
            turned("x0T")
            w = Block()
            for tt in range(NT):
                rows(("qa", tt), tt, xT, tt, w, 0, 512)
            w.done(("qa", 1))
            w = Block()
            for tt in range(NT):
                rows(("qb", tt), 2 + tt, xT, tt, w, 0, 512)
            w.done(("qb", 1))
            w = Block(P)
            for tt in range(NT):
                rows(("vc", tt), 6 + tt, xT, tt, w, 0, P)
            w.done(("vc", 1))
            w = Block(2 * P)
            turned_cols(("qcT", 0), 4, w, (0, P))
            w.done(("qcT", 0))
            pe.wait_ge(consts, 1)
            for n, (tag, tt) in enumerate([("a", 0), ("a", 1), ("b", 0), ("b", 1)]):
                pe.wait_ge(roped, n + 1)
                label = ("qT", tag, tt)
                begin(label, 5 if n % 2 == 0 else 0)
                b = bk.at[label][0]
                for c in range(4 if tag == "a" else 2):
                    ins = pe.transpose(bank(b, c * P, (c + 1) * P), rope_q[:, n % 2, c * P:(c + 1) * P],
                                       ident[:, :])
                end(ins, label)
                if tag == "b":
                    label = ("kT", tt)
                    begin(label, 1 + tt)
                    for g in range(NKV):
                        ins = pe.transpose(bank(1 + tt, g * P, (g + 1) * P),
                                           kdup[:, tt, g, :, :].rearrange("p u c -> p (u c)"), ident[:, :])
                    end(ins, label)
            for label in [("qT", x, tt) for x in "ab" for tt in range(NT)] + \
                    [("kT", 0), ("kT", 1), ("qcT", 0), ("kmT", 0), ("vm", 0), ("vc", 0), ("vc", 1)]:
                pe.wait_ge(*bk.empty(label))
            attend(UNITS0)
            project_out(0, [("o", u[0]) for u in UNITS0[-2:]])

            turn(FPRE0, "f0T", (4, 5, 6, 7), [0])
            def thrice(out, x, w, first, last):
                pe.matmul(out, x[0], w[0], start=first, stop=False, skip_group_check=True)
                pe.matmul(out, x[0], w[1], start=False, stop=False, skip_group_check=True)
                return pe.matmul(out, x[1], w[0], start=False, stop=last, skip_group_check=True)

            rot = [0]
            n_used = [0]

            def gate_up(kind, b, tt):
                label = (kind + "0", b, tt)
                begin(label, 4 + rot[0] % 3)
                rot[0] += 1
                for half in range(2):
                    m = place[kind, b, half]
                    pe.wait_ge(lo_ok, m + 1)
                    w = cut_at(m, kind)
                    for c in range(4):
                        k = 4 * half + c
                        x = [y[:, k, tt * P:(tt + 1) * P] for y in (x_hi, x_lo)]
                        ins = thrice(bank(bk.at[label][0]), x, [y[:, c, :] for y in w], k == 0, k == KD - 1)
                    if half == 0 and tt == NT - 1:
                        ins.then_inc(used, 1)
                        n_used[0] += 1
                        cut_free[m] = (used, n_used[0])
                end(ins, label)
                if tt == NT - 1:
                    cut_free[m] = bk.full(label)

            def turn_hidden(b, tt):
                pe.wait_ge(*bk.empty(("u0", b, tt)))
                begin(("h0T", b, tt), 7)
                for c in range(CB):
                    ins = pe.transpose(bank(7, c * P, (c + 1) * P), hid0[:, b % 2, tt, c * P:(c + 1) * P],
                                       ident[:, :])
                end(ins, ("h0T", b, tt))

            def down(b, tt):
                if b == 0:
                    for hf in range(2):
                        begin(("y0", tt, hf), 2 * tt + hf)
                pe.wait_ge(*bk.empty(("h0T", b, tt)))
                for half in range(2):
                    m = place["d", b, half]
                    pe.wait_ge(lo_ok, m + 1)
                    w = cut_at(m, "d")
                    for hf in range(2):
                        for c in range(2):
                            cc = 2 * half + c
                            h = [y[:, tt, cc * P:(cc + 1) * P] for y in (h_hi, h_lo)]
                            ins = thrice(bank(2 * tt + hf), h, [y[:, c, hf * 512:(hf + 1) * 512] for y in w],
                                         b == 0 and cc == 0, b == NB - 1 and cc == CB - 1)
                        if b == NB - 1 and half == 1:
                            end(ins, ("y0", tt, hf))
                    if tt == NT - 1:
                        if b == NB - 1 and half == 1:
                            cut_free[m] = bk.full(("y0", tt, 1))
                        else:
                            ins.then_inc(used, 1)
                            n_used[0] += 1
                            cut_free[m] = (used, n_used[0])

            for b in range(NB):
                if b == 0:
                    turned("f0T", 0)
                gate_up("g", b, 0)
                if b == 0:
                    turn(FPRE0, "f0T", (4, 5, 6, 7), [1])
                    turned("f0T", 1)
                else:
                    turn_hidden(b - 1, 0)
                gate_up("g", b, 1)
                if b >= 1:
                    turn_hidden(b - 1, 1)
                gate_up("u", b, 0)
                gate_up("u", b, 1)
                if b >= 1:
                    down(b - 1, 0)
                    if b == NB - 1:
                        turn_hidden(b, 0)
                    down(b - 1, 1)
            turn_hidden(NB - 1, 1)
            down(NB - 1, 0)
            down(NB - 1, 1)
            n_raw[0] = FFN0 + NPC

            turn(MEM1, "mem1T", (4, 5, 6, 7), src=memb)
            turned("mem1T")
            memory_kv(1, memT, (4, 5))
            turn(PRE1, "x1T", (0, 1, 2, 3))
            turned("x1T")
            w = Block()
            for tt in range(NT):
                rows(("v1b", tt), 6 + tt, xT, tt, w, 0, 256)
            turned_cols(("qcT", 1), 4, w, (256, 384))
            w.done(("qcT", 1))
            for label in [("qcT", 1), ("kmT", 1), ("vm", 1)]:
                pe.wait_ge(*bk.empty(label))
            for i, b in enumerate((6, 0, 2)):
                for u, layer, g, tt, q, k, keys, val, kt0 in UNITS1:
                    if i == 0:
                        scores(u, layer, g, tt, q, k, keys)
                    elif i == 1:
                        turn_probs(u, (keys[1] - keys[0]) // P)
                    else:
                        weigh(u, g, (keys[1] - keys[0]) // P, val, kt0)
                w = Block()
                turned_cols(("p", 2 * i), b, w, (0, 128))
                turned_cols(("p", 2 * i + 1), b + 1, w, (256, 384))
                w.done(("p", 2 * i + 1))
            w = Block()
            for tt in range(NT):
                rows(("v1a", tt), tt, xT, tt, w, 0, 512)
            w.done(("v1a", 1))

            def stick_scores(p):
                for b in range(2):
                    bb = 2 * (p % 3) + b
                    begin(("z", p, b), bb)
                    r = slice(HD * b, HD * b + HD)
                    pe.matmul(bank(bb, 0, 256), kT[r, p, 0:P], qT[r, p, :], start=True, stop=False,
                              skip_group_check=True)
                    ins = pe.matmul(bank(bb, 256, 384), kT[r, p, P:2 * P], qT[r, p, P:2 * P], start=False,
                                    stop=False, skip_group_check=True)
                    end(ins, ("z", p, b))

            def stick_sum(p):
                pe.wait_ge(soft_b, p + 1)
                for b in range(2):
                    bb = 2 * (p % 3) + b
                    begin(("zc", p, b), bb)
                    pe.matmul(bank(bb, 0, 256), upper_neg[:, :], soft[:, p % 2, b, 0:256], start=False,
                              stop=False, skip_group_check=True)
                    pe.matmul(bank(bb, P, 2 * P), ones_neg[:, :], soft[:, p % 2, b, 256:384], start=False,
                              stop=False, skip_group_check=True)
                    ins = pe.matmul(bank(bb, 256, 384), upper_neg[:, :], soft[:, p % 2, b, 256:384],
                                    start=False, stop=True, skip_group_check=True)
                    end(ins, ("zc", p, b))

            def stick_weigh(p):
                pe.wait_ge(stick_b, p + 1)
                begin(("os", p), 6 + p % 2)
                for b in range(2):
                    h = (2 * p + b) * HD
                    o = psum[HD * b:HD * b + HD, 6 + p % 2, :]
                    pe.matmul(o[:, 0:256], v[:, 0, h:h + HD], stick[:, p % 2, b, 0:256], start=True,
                              stop=False, skip_group_check=True)
                    ins = pe.matmul(o[:, P:2 * P], v[:, 1, h:h + HD], stick[:, p % 2, b, 256:384],
                                    start=False, stop=True, skip_group_check=True)
                end(ins, ("os", p))

            for label in [("p", i) for i in range(6)] + [("v1a", 0), ("v1a", 1), ("v1b", 0), ("v1b", 1)]:
                pe.wait_ge(*bk.empty(label))
            NP = NH // 2
            for s in range(NP + 2):
                if s < NP:
                    stick_scores(s)
                if 1 <= s <= NP:
                    stick_sum(s - 1)
                if s >= 2:
                    stick_weigh(s - 2)
            project_out(1, [("os", NP - 1), ("os", NP - 2)] + [("o", u[0]) for u in UNITS1])

            pe.wait_ge(small_in, 16 * 3)
            begin(("logits",), 0)
            for tt in range(NT):
                turn(FPRE1, "f1T", (4, 5, 6, 7), [tt])
                turned("f1T", tt)
                for k in range(KD):
                    ins = pe.matmul(bank(0, tt * NE, (tt + 1) * NE), xT[:, k, tt * P:(tt + 1) * P],
                                    wr[:, k, :], start=(k == 0), stop=(k == KD - 1))
            end(ins, ("logits",))
            pe.wait_ge(chosen_ok, 1)
            begin(("rank",), 5)
            pe.matmul(bank(5, 0, NE), before_b[:, :], chosen_b[:, 0, :], start=True, stop=True)
            pe.matmul(bank(5, NE, 2 * NE), ones_b[:, :], chosen_b[:, 0, :], start=True, stop=False)
            pe.matmul(bank(5, NE, 2 * NE), before_b[:, :], chosen_b[:, 1, :], start=False, stop=True)
            pe.matmul(bank(5, 2 * NE, 3 * NE), ones_b[:, :], chosen_b[:, 0, :], start=True, stop=False)
            ins = pe.matmul(bank(5, 2 * NE, 3 * NE), ones_b[:, :], chosen_b[:, 1, :], start=False, stop=True)
            end(ins, ("rank",))

            def gather(labels, waits):
                for hf in range(2):
                    s, n = waits[hf]
                    pe.wait_ge(s, n)
                    for c in range(4):
                        k = 4 * hf + c
                        for tt in range(NT):
                            ins = pe.matmul(bank(4 + hf, c * P, (c + 1) * P), xn[:, tt, k * P:(k + 1) * P],
                                            pick[:, tt, :], start=(tt == 0), stop=(tt == NT - 1))
                    end(ins, labels[hf])

            pe.wait_ge(pick_ok, 1)
            gather([("pre-gather", 0), ("pre-gather", 1)],
                   [bk.fill(("pre-gather", hf), 4 + hf) for hf in range(2)])
            base = list(bk.count)
            used_before = n_used[0]
            pe.wait_ge(tables_ok, 1)
            n_jobs = pe.value_load(job_i[0:1, 3:4], min_val=NE, max_val=MAX_JOBS)
            for hf in range(2):
                pe.wait_ge(*bk.empty(("pre-gather", hf)))
            with pe.Fori(0, n_jobs) as j:
                def jbegin(label, b):
                    pe.wait_ge(*bk.fill(label, b, j))

                def jcut(m, kind):
                    pe.wait_ge(lo_ok, NPC * j + (NPC + m + 1))
                    return cut_at(m, kind)

                def use(ins, m):
                    ins.then_inc(used, 1)
                    n_used[0] += 1
                    job_free[m] = n_used[0]

                def expert_rows(kind, b):
                    label = (kind, b)
                    bb = 2 + 2 * (b % 2) + (kind == "u")
                    jbegin(label, bb)
                    for half in range(2):
                        m = place[kind, b, half]
                        w = jcut(m, kind)
                        for c in range(4):
                            k = 4 * half + c
                            ins = thrice(bank(bb), (picked_hi[:, k, :], picked_lo[:, k, :]),
                                         [y[:, c, :] for y in w], k == 0, k == KD - 1)
                        if half == 0:
                            use(ins, m)
                    end(ins, label)
                    job_free[m] = label

                def expert_turn(b):
                    jbegin(("T", b), 7)
                    pe.wait_ge(*bk.empty(("u", b), j))
                    for c in range(CB):
                        ins = pe.transpose(bank(7, c * P, (c + 1) * P), hid1[:, b % 2, c * P:(c + 1) * P],
                                           ident[:, :])
                    end(ins, ("T", b))

                def expert_down(b, half):
                    if b == 0 and half == 0:
                        for hf in range(2):
                            jbegin(("y", hf), hf)
                    if half == 0:
                        pe.wait_ge(*bk.empty(("T", b), j))
                    m = place["d", b, half]
                    w = jcut(m, "d")
                    for hf in range(2):
                        for c in range(2):
                            cc = 2 * half + c
                            h = [y[:, b % 2, cc * P:(cc + 1) * P] for y in (h_hi, h_lo)]
                            ins = thrice(bank(hf), h, [y[:, c, hf * 512:(hf + 1) * 512] for y in w],
                                         b == 0 and cc == 0, b == NB - 1 and cc == CB - 1)
                        if b == NB - 1 and half == 1:
                            end(ins, ("y", hf))
                    if b == NB - 1 and half == 1:
                        job_free[m] = ("y", 1)
                    else:
                        use(ins, m)

                for b in range(NB):
                    expert_rows("g", b)
                    if b >= 1:
                        expert_turn(b - 1)
                    expert_rows("u", b)
                    if b == 0:
                        jbegin(("pickT",), 6)
                        for tt in range(NT):
                            ins = pe.transpose(bank(6, tt * P, (tt + 1) * P), pick[:, tt, :], ident[:, :])
                        end(ins, ("pickT",))
                    else:
                        expert_down(b - 1, 0)
                        if b == NB - 1:
                            expert_turn(b)
                        expert_down(b - 1, 1)
                expert_down(NB - 1, 0)
                expert_down(NB - 1, 1)
                pe.wait_ge(pick_ok, j + 2)
                gather([("gather", 0), ("gather", 1)],
                       [bk.fill(("gather", hf), 4 + hf, j) for hf in range(2)])
                pe.wait_ge(*bk.empty(("pickT",), j))
                for hf in range(2):
                    pe.wait_ge(*bk.empty(("y", hf), j))
                for i, (tt, hf, bb) in enumerate([(0, 0, 6), (0, 1, 7), (1, 0, 4), (1, 1, 5)]):
                    jbegin(("back", tt, hf), bb)
                    ins = pe.matmul(bank(bb), pickT[:, tt, :], y_sb[:, hf * 512:(hf + 1) * 512],
                                    start=True, stop=True)
                    end(ins, ("back", tt, hf))
                for hf in range(2):
                    pe.wait_ge(*bk.empty(("gather", hf), j))
            assert tuple(bk.count[b] - base[b] for b in range(8)) == TURN
            assert n_used[0] - used_before == USED_TURN

        @block.scalar
        def _(act):
            links = [0]

            def link(ins):
                links[0] += 1
                ins.then_inc(act_chain, 1)
                act.wait_ge(act_chain, links[0])

            def copy(label, out, src, scale=None):
                act.wait_ge(*bk.full(label))
                act.activation(out, src, ACT.Copy, scale=1.0 if scale is None else scale)\
                    .then_inc(bk.empty_sem(label), 1)

            def square_sum(norm, tt, out, src):
                act.activation(out, src, ACT.Square, accum_out=ssq[:, norm, tt:tt + 1]).then_inc(summed, 1)

            def drain_turned(tag, dst, tiles=range(NT)):
                for tt in tiles:
                    label = (tag, tt, 0)
                    copy(label, dst[:, 0:4, tt * P:(tt + 1) * P],
                         bank(bk.at[label][0]).rearrange("p (c s) -> p c s", c=4))

            def exps(u, i, layer, nk):
                act.wait_ge(max_ok, u + 1)
                for b in range(2):
                    for s2 in range(2):
                        x = probs[:, u % 2, b, s2, 0:nk * P]
                        ins = act.activation(x, x, ACT.Exp, bias=nmax[:, u, 2 * s2 + b:2 * s2 + b + 1],
                                             accum_out=psum_e[:, u, 2 * s2 + b:2 * s2 + b + 1])
                if layer == 0 and i < NKV:
                    ins = act.activation(esink[:, u, :], esink[:, u, :], ACT.Exp)
                ins.then_inc(exp_ok, 1)

            def turned_probs(u, nk):
                copy(("pT", u, 0), probsT(u)[:, 0, :, 0:nk, :],
                     bank(4).rearrange("p (h k q) -> p h k q", h=2, k=2)[:, :, 0:nk, :])

            def mixed(u, i, tt):
                copy(("o", u), mixT[:, 2 * i:2 * i + 2, tt * P:(tt + 1) * P],
                     bank(6 + u % 2, 0, 256).rearrange("p (c s) -> p c s", c=2))

            def attend(units):
                for s in range(len(units) + 2):
                    if s >= 2:
                        u, keys = units[s - 2][0], units[s - 2][6]
                        nk = (keys[1] - keys[0]) // P
                        turned_probs(u, nk)
                    if s < len(units):
                        u, layer, i, keys = (units[s][x] for x in (0, 1, 2, 6))
                        exps(u, i, layer, (keys[1] - keys[0]) // P)
                    if s >= 2:
                        mixed(*(units[s - 2][x] for x in (0, 2, 3)))

            def raise_part(label, out, src, j=0):
                act.wait_ge(*bk.full(label, j))
                act.activation(out, src, ACT.Copy).then_inc(part_hi, 1)

            def cut_high(m, n, round_no, free):
                act.wait_ge(raw_full[n % RAW], round_no)
                if free is not None:
                    act.wait_ge(*free)
                act.activation(w_hi[:, m % CUT, :], raw[:, n % RAW, :], ACT.Copy).then_inc(hi_ok, 1)

            def cut_high0(m):
                n = FFN0 + m
                cut_high(m, n, 16 * (n // RAW + 1), cut_free[m - CUT] if m >= CUT else None)

            for tt in range(NT):
                act.wait_ge(mem_in[tt], 16)
                square_sum(MEM0, tt, xn[:, tt, :], memb[:, tt, :])
            drain_turned("mem0T", memT)
            for tt in range(NT):
                act.wait_ge(x_in[tt], 16)
                act.wait_ge(*bk.full(("mem0T", tt, 1)))
                square_sum(PRE0, tt, xn[:, tt, :], hres[:, tt, :])
            copy(("kmT", 0), kmT, bank(6).rearrange("p (c s) -> p c s", c=2))
            copy(("vm", 0), vm, bank(7).rearrange("p (c s) -> p c s", c=2))
            drain_turned("x0T", xT)
            act.wait_ge(angles, 1)
            act.wait_ge(consts, 1)
            act.activation(rope_s[:, 2, :, :], rope_s[:, 0, :, :], ACT.Sin)
            act.activation(rope_s[:, 3, :, :], rope_s[:, 1, :, :], ACT.Sin, scale=-1.0,
                           bias=halfpi[:, 0:1]).then_inc(sines, 1)
            for tt in range(NT):
                copy(("vc", tt), v[:, tt, 64:192], bank(6 + tt, 0, 128))
            copy(("qcT", 0), qcT, bank(4).rearrange("p (c s) -> p c s", c=2))
            for tag in "ab":
                for tt in range(NT):
                    label = ("qT", tag, tt)
                    n = 4 if tag == "a" else 2
                    copy(label, qT[:, 0:4, tt * P:(tt + 1) * P] if tag == "a" else
                         qT[:, 4:6, tt * P:(tt + 1) * P],
                         bank(bk.at[label][0], 0, n * P).rearrange("p (c s) -> p c s", c=n))
            attend(UNITS0)

            def post_norm(norm, tt, labels, out):
                for hf in range(2):
                    act.wait_ge(*bk.full(labels + (tt, hf)))
                square_sum(norm, tt, out[:, tt, :], psum[:, 2 * tt:2 * tt + 2, :].rearrange("p a b -> p (a b)"))

            def pre_norm(norm, tt, n_added):
                act.wait_ge(added, n_added + tt + 1)
                square_sum(norm, tt, xn[:, tt, :], hres[:, tt, :])

            def raise_f0(tt):
                for hf in range(2):
                    label = ("f0T", tt, hf)
                    raise_part(label, x_hi[:, 4 * hf:4 * hf + 4, tt * P:(tt + 1) * P],
                               bank(bk.at[label][0]).rearrange("p (c s) -> p c s", c=4))

            post_norm(POST0, 0, ("mix", 0), xn)
            pre_norm(FPRE0, 0, 0)
            cut_high0(0)
            cut_high0(1)
            post_norm(POST0, 1, ("mix", 0), xn)
            raise_f0(0)
            pre_norm(FPRE0, 1, 0)
            cut_high0(2)
            raise_f0(1)
            for tt in range(NT):
                act.wait_ge(*bk.full(("f0T", tt, 1)))
                square_sum(MEM1, tt, xn[:, tt, :], memb[:, tt, :])

            for i, (kind, b, half) in enumerate(pieces):
                tt = half
                if kind == "g":
                    label = ("g0", b, tt)
                    act.wait_ge(*bk.full(label))
                    if b >= 1:
                        act.wait_ge(*bk.empty(("u0", b - 1, tt)))
                    act.activation(act0[:, tt, :], bank(bk.at[label][0]), ACT.Silu)\
                        .then_inc(bk.empty_sem(label), 1)
                if (kind == "g" and b >= 1) or (kind, b) == ("d", NB - 2):
                    hb = b - 1 if kind == "g" else NB - 1
                    raise_part(("h0T", hb, tt), h_hi[:, tt, :], bank(7))
                if i + CUT < NPC:
                    cut_high0(i + CUT)
            temp = mixT[:, :, :].rearrange("p (t a) s -> p t (a s)", t=NT)
            post_norm(FPOST0, 0, ("y0",), temp)
            pre_norm(PRE1, 0, 2)
            drain_turned("mem1T", memT)
            post_norm(FPOST0, 1, ("y0",), temp)
            pre_norm(PRE1, 1, 2)
            copy(("kmT", 1), kmT, bank(4).rearrange("p (c s) -> p c s", c=2))
            copy(("vm", 1), vm, bank(5).rearrange("p (c s) -> p c s", c=2))
            drain_turned("x1T", xT)

            def heads(i, dst, scale=None):
                copy(("p", i), dst, bank(bk.at["p", i][0]).rearrange("p (c s) -> p c s", c=2), scale)

            copy(("v1b", 0), v[:, 0, 512:768], bank(6, 0, 256))
            copy(("qcT", 1), qcT, bank(4).rearrange("p (c s) -> p c s", c=2))
            for u, *_ in UNITS1:
                exps(u, NKV, 1, MEM // P)
            heads(0, qT[:, 0:2, :], SCALE)
            for u, *_ in UNITS1:
                turned_probs(u, MEM // P)
            heads(2, qT[:, 4:6, :], SCALE)
            for u, _, i, tt, *_ in UNITS1:
                mixed(u, i, tt)
            heads(4, kT[:, 2:4, :])
            copy(("v1a", 0), v[:, 0, 0:512], bank(0))

            def z_view(p):
                return psum[:, 2 * (p % 3):2 * (p % 3) + 2, 0:384]

            def log_terms(p):
                for b in range(2):
                    act.wait_ge(*bk.full(("z", p, b)))
                x = soft[:, p % 2, :, :]
                if p >= 2:
                    act.wait_ge(*bk.full(("zc", p - 2, 1)))
                link(act.activation(x, z_view(p), ACT.Abs))
                link(act.activation(x, x, ACT.Exp, scale=-1.0))
                act.activation(x, x, ACT.Ln, bias=1.0).then_inc(soft_a, 1)

            def stick_exp(p):
                for b in range(2):
                    act.wait_ge(*bk.full(("zc", p, b)))
                if p >= 2:
                    act.wait_ge(*bk.full(("os", p - 2)))
                for b in range(2):
                    ins = act.activation(stick[:, p % 2, b, :], bank(2 * (p % 3) + b, 0, 384), ACT.Exp)
                    ins.then_inc(bk.empty_sem(("zc", p, b)), 1)

            NP = NH // 2
            for s in range(NP + 2):
                if s < NP:
                    log_terms(s)
                if 1 <= s <= NP:
                    stick_exp(s - 1)
                if s >= 2:
                    copy(("os", s - 2), mixT[:, s - 2, :], bank(6 + s % 2, 0, 256))

            def cut_high1(j, m):
                i = m - CUT
                free = None
                if i >= 0:
                    last = job_free[i]
                    free = bk.full(last, j) if isinstance(last, tuple) else (used, last + USED_TURN * j)
                cut_high(m, m, (16 * NPC // RAW) * j + 16 * (PRE // RAW + m // RAW + 1), free)

            cut_high1(0, 0)
            cut_high1(0, 1)
            post_norm(POST1, 0, ("mix", 1), xn)
            pre_norm(FPRE1, 0, 4)
            post_norm(POST1, 1, ("mix", 1), xn)
            drain_turned("f1T", xT, [0])
            cut_high1(0, 2)
            pre_norm(FPRE1, 1, 4)
            drain_turned("f1T", xT, [1])

            act.wait_ge(gap_ok, 1)
            act.activation(gate2[:, :, 1:2], gate2[:, :, 0:1], ACT.Exp).then_inc(gexp_ok, 1)

            def gathered(label, hf, j=0):
                raise_part(label, picked_hi[:, 4 * hf:4 * hf + 4, :],
                           bank(4 + hf).rearrange("p (k s) -> p k s", k=4), j)

            for hf in range(2):
                gathered(("pre-gather", hf), hf)
            act.wait_ge(tables_ok, 1)
            n_jobs = act.value_load(job_i[0:1, 3:4], min_val=NE, max_val=MAX_JOBS)
            with act.Fori(0, n_jobs) as j:
                def full(label):
                    act.wait_ge(*bk.full(label, j))

                def jcopy(label, out, src):
                    full(label)
                    act.activation(out, src, ACT.Copy).then_inc(bk.empty_sem(label), 1)

                for i, (kind, b, half) in enumerate(pieces):
                    if (kind, half) == ("g", 1):
                        full(("g", b))
                        act.activation(act1[:, b % 2, :], bank(bk.at["g", b][0]), ACT.Silu)\
                            .then_inc(bk.empty_sem(("g", b)), 1)
                        if b >= 1:
                            raise_part(("T", b - 1), h_hi[:, (b - 1) % 2, :], bank(7), j)
                    if (kind, b, half) == ("d", 0, 0):
                        jcopy(("pickT",), pickT, bank(6, 0, 256).rearrange("p (t s) -> p t s", t=NT))
                    if (kind, b, half) == ("d", NB - 2, 0):
                        raise_part(("T", NB - 1), h_hi[:, (NB - 1) % 2, :], bank(7), j)
                    if i == NPC - 1:
                        jcopy(("y", 0), y_sb[:, 0:512], bank(0))
                    cut_high1(j, i + CUT)
                for hf in range(2):
                    gathered(("gather", hf), hf, j)

            act.wait_ge(tables_ok, 2)
            for tt in range(NT):
                square_sum(FPOST1, tt, xn[:, tt, :], esum[:, tt, :])

        @block.vector
        def _(dve):
            links = [0]

            def link(ins):
                links[0] += 1
                ins.then_inc(dve_chain, 1)
                dve.wait_ge(dve_chain, links[0])

            def copy(label, out, src, scale=None):
                dve.wait_ge(*bk.full(label))
                ins = dve.tensor_copy(out, src) if scale is None else \
                    dve.tensor_scalar(out, src, scale, None, ALU.mult)
                ins.then_inc(bk.empty_sem(label), 1)

            def scale_rows(norm, tt, out, src, labels=()):
                if tt == 0:
                    dve.wait_ge(gain_in[norm % NG], 16 * (norm // NG + 1))
                dve.wait_ge(rstd_ok, NORM_COUNT[norm, tt])
                ins = dve.scalar_tensor_tensor(out=out, in0=src, scalar=rstd[:, norm, tt:tt + 1],
                                               in1=gains[:, norm % NG, :], op0=ALU.mult, op1=ALU.mult)
                ins.then_inc(scaled, 1)
                dve.wait_ge(scaled, NORM_COUNT[norm, tt])

            def drain_turned(tag, dst, tiles=range(NT)):
                for tt in tiles:
                    label = (tag, tt, 1)
                    copy(label, dst[:, 4:8, tt * P:(tt + 1) * P],
                         bank(bk.at[label][0]).rearrange("p (c s) -> p c s", c=4))

            def post_norm(norm, tt, labels, out):
                scale_rows(norm, tt, out[:, tt, :], psum[:, 2 * tt:2 * tt + 2, :].rearrange("p a b -> p (a b)"))
                for hf in range(2):
                    dve.sem_inc(bk.empty_sem(labels + (tt, hf)), 1)
                dve.tensor_tensor(hres[:, tt, :], hres[:, tt, :], out[:, tt, :], ALU.add).then_inc(added, 1)

            def pre_norm(norm, tt, src):
                scale_rows(norm, tt, xn[:, tt, :], src[:, tt, :])

            def row_max(u, layer, i, tt, nk):
                for b in range(2):
                    dve.wait_ge(*bk.full(("s", u, b)))
                if u >= 2 and u != UNITS1[0][0] and u != UNITS1[1][0]:
                    for b in range(2):
                        dve.wait_ge(*bk.full(("pT", u - 2, b)))
                K = nk * P
                mask = band[:, 2 * P - K:2 * P]
                for b in range(2):
                    x = probs[:, u % 2, b, :, 0:K]
                    src = bank(2 * (u % 2) + b, 0, 2 * K).rearrange("p (h k) -> p h k", h=2)
                    if layer == 0 and i < NKV:
                        ins = dve.scalar_tensor_tensor(out=x, in0=src, scalar=SCALE,
                                                       in1=mask.unsqueeze(1).to_broadcast((P, 2, K)),
                                                       op0=ALU.mult, op1=ALU.add)
                    else:
                        ins = dve.tensor_scalar(x, src, SCALE, None, ALU.mult)
                    ins.then_inc(bk.empty_sem(("s", u, b)), 1)
                for b in range(2):
                    dve.wait_ge(*bk.empty(("s", u, b)))
                for b in range(2):
                    ins = dve.tensor_reduce(nmax[:, u, b:4:2], probs[:, u % 2, b, :, 0:K], AX.X, ALU.max)
                link(ins)
                if layer == 0 and i < NKV:
                    link(dve.scalar_tensor_tensor(out=nmax[:, u, :], in0=nmax[:, u, :], scalar=-1.0,
                                                  in1=nsinks[:, 4 * i:4 * i + 4], op0=ALU.mult, op1=ALU.min))
                    dve.tensor_tensor(esink[:, u, :], nmax[:, u, :], sinks[:, 4 * i:4 * i + 4], ALU.add)\
                        .then_inc(max_ok, 1)
                else:
                    dve.tensor_scalar(nmax[:, u, :], nmax[:, u, :], -1.0, None, ALU.mult).then_inc(max_ok, 1)

            def normalise(u, layer, i, nk):
                dve.wait_ge(exp_ok, u + 1)
                if layer == 0 and i < NKV:
                    link(dve.tensor_tensor(psum_e[:, u, :], psum_e[:, u, :], esink[:, u, :], ALU.add))
                link(dve.reciprocal(recip[:, u, :], psum_e[:, u, :]))
                for b in range(2):
                    x = probs[:, u % 2, b, :, 0:nk * P]
                    ins = dve.tensor_tensor(x, x, recip[:, u, b:4:2].unsqueeze(2).to_broadcast((P, 2, nk * P)),
                                            ALU.mult)
                ins.then_inc(norm_ok, 1)

            def turned_probs(u, nk):
                copy(("pT", u, 1), probsT(u)[:, 1, :, 0:nk, :],
                     bank(5).rearrange("p (h k q) -> p h k q", h=2, k=2)[:, :, 0:nk, :])

            def attend(units):
                for s in range(len(units) + 2):
                    if s >= 2:
                        u, keys = units[s - 2][0], units[s - 2][6]
                        nk = (keys[1] - keys[0]) // P
                        turned_probs(u, nk)
                    if s < len(units):
                        u, layer, i, tt, keys = (units[s][x] for x in (0, 1, 2, 3, 6))
                        row_max(u, layer, i, tt, (keys[1] - keys[0]) // P)
                    if 1 <= s <= len(units):
                        u, layer, i, keys = (units[s - 1][x] for x in (0, 1, 2, 6))
                        normalise(u, layer, i, (keys[1] - keys[0]) // P)

            n_part = [0]

            def lower_part(label, out, src, high, j=None):
                n_part[0] += 1
                dve.wait_ge(part_hi, n_part[0] if j is None else n_part[0] + 9 * j)
                dve.tensor_tensor(out, src, high.bitcast(F32), ALU.subtract).then_inc(bk.empty_sem(label), 1)

            def cut_rest(m, n, count):
                dve.wait_ge(hi_ok, count)
                dve.tensor_tensor(w_lo[:, m % CUT, :], raw[:, n % RAW, :],
                                  w_hi[:, m % CUT, :].bitcast(F32), ALU.subtract).then_inc(lo_ok, 1)

            for tt in range(NT):
                scale_rows(MEM0, tt, xn[:, tt, :], memb[:, tt, :])
            drain_turned("mem0T", memT)
            for tt in range(NT):
                pre_norm(PRE0, tt, hres)
            drain_turned("x0T", xT)
            dve.wait_ge(small_in, 16 * 3)
            dve.wait_ge(consts, 1)
            link(dve.tensor_copy(pos_f[:, :], pos_i[:, :]))
            dve.tensor_scalar(nsinks[:, :], sinks[:, :], -1.0, None, ALU.mult)
            for tt in range(NT):
                ins = dve.tensor_scalar(rope_s[:, 0, tt, :], invf[:, :], pos_f[:, tt:tt + 1], None, ALU.mult)
            link(ins)
            a, n = rope_s[:, 0, :, :], rope_s[:, 1, :, :]
            link(dve.tensor_scalar(n, a, 1.0 / TWO_PI, ROUND, ALU.mult, ALU.add))
            link(dve.tensor_scalar(n, n, -ROUND, None, ALU.add))
            for part in (TP1, TP2, TP3):
                link(dve.scalar_tensor_tensor(out=a, in0=n, scalar=-part, in1=a, op0=ALU.mult, op1=ALU.add))
            link(dve.tensor_scalar(a, a, 3.1415925, -3.1415925, ALU.min, ALU.max))
            link(dve.tensor_scalar(n, a, -1.0, None, ALU.mult))
            dve.tensor_tensor(n, a, n, ALU.max).then_inc(angles, 1)

            dve.wait_ge(sines, 1)
            H2 = HD // 2
            for half in range(2):
                dve.tensor_copy(cos2[:, :, half * H2:(half + 1) * H2], rope_s[:, 3, :, :])
            dve.tensor_scalar(sin2[:, :, 0:H2], rope_s[:, 2, :, :], -1.0, None, ALU.mult)
            link(dve.tensor_copy(sin2[:, :, H2:HD], rope_s[:, 2, :, :]))

            for n, (tag, tt) in enumerate([("a", 0), ("a", 1), ("b", 0), ("b", 1)]):
                label = ("q" + tag, tt)
                nh = 8 if tag == "a" else 7
                bb = bk.at[label][0]
                x = bank(bb, 0, nh * HD).rearrange("p (h c) -> p h c", c=HD)
                ra = rope_a[:, 0:nh * HD].rearrange("p (h c) -> p h c", c=HD)
                rb = rope_b[:, 0:nh * HD].rearrange("p (h c) -> p h c", c=HD)
                dve.wait_ge(*bk.full(label))
                dve.tensor_tensor(ra, x, cos2[:, tt, :].unsqueeze(1).to_broadcast((P, nh, HD)), ALU.mult)
                dve.tensor_tensor(rb[:, :, 0:H2], x[:, :, H2:HD],
                                  sin2[:, tt, 0:H2].unsqueeze(1).to_broadcast((P, nh, H2)), ALU.mult)
                ins = dve.tensor_tensor(rb[:, :, H2:HD], x[:, :, 0:H2],
                                        sin2[:, tt, H2:HD].unsqueeze(1).to_broadcast((P, nh, H2)), ALU.mult)
                if tag == "b":
                    ins = dve.tensor_copy(v[:, tt, 0:64], bank(bb, 448, 512))
                ins.then_inc(bk.empty_sem(label), 1)
                dve.wait_ge(*bk.empty(label))
                if n >= 2:
                    dve.wait_ge(*bk.full(("qT", "a", n - 2)))
                nq = 8 if tag == "a" else 4
                ins = dve.tensor_tensor(rope_q[:, n % 2, 0:nq * HD], rope_a[:, 0:nq * HD],
                                        rope_b[:, 0:nq * HD], ALU.add)
                if tag == "b":
                    for dup in range(2):
                        ins = dve.tensor_tensor(kdup[:, tt, :, dup, :], ra[:, 4:7, :], rb[:, 4:7, :], ALU.add)
                ins.then_inc(roped, 1)
                dve.wait_ge(roped, n + 1)
            for tt in range(NT):
                copy(("kT", tt), kT[:, 0:NKV, tt * P:(tt + 1) * P],
                     bank(1 + tt, 0, NKV * P).rearrange("p (c s) -> p c s", c=NKV))
            attend(UNITS0)

            def lower_f0(tt):
                for hf in range(2):
                    label = ("f0T", tt, hf)
                    part = (slice(None), slice(4 * hf, 4 * hf + 4), slice(tt * P, (tt + 1) * P))
                    lower_part(label, x_lo[part], bank(bk.at[label][0]).rearrange("p (c s) -> p c s", c=4),
                               x_hi[part])

            post_norm(POST0, 0, ("mix", 0), xn)
            pre_norm(FPRE0, 0, hres)
            cut_rest(0, FFN0, 1)
            cut_rest(1, FFN0 + 1, 2)
            post_norm(POST0, 1, ("mix", 0), xn)
            lower_f0(0)
            pre_norm(FPRE0, 1, hres)
            cut_rest(2, FFN0 + 2, 3)
            lower_f0(1)
            for tt in range(NT):
                scale_rows(MEM1, tt, memb[:, tt, :], memb[:, tt, :])

            for i, (kind, b, half) in enumerate(pieces):
                tt = half
                if (kind == "g" and b >= 1) or (kind, b) == ("d", NB - 2):
                    hb = b - 1 if kind == "g" else NB - 1
                    lower_part(("h0T", hb, tt), h_lo[:, tt, :], bank(7), h_hi[:, tt, :])
                if kind == "u":
                    label = ("u0", b, tt)
                    dve.wait_ge(*bk.empty(("g0", b, tt)))
                    dve.wait_ge(*bk.full(label))
                    dve.tensor_tensor(hid0[:, b % 2, tt, :].rearrange("p (c q) -> p q c", c=CB),
                                      act0[:, tt, :].rearrange("p (q c) -> p q c", c=CB),
                                      bank(bk.at[label][0]).rearrange("p (q c) -> p q c", c=CB),
                                      ALU.mult).then_inc(bk.empty_sem(label), 1)
                if i + CUT < NPC:
                    cut_rest(i + CUT, FFN0 + i + CUT, i + CUT + 1)
            temp = mixT[:, :, :].rearrange("p (t a) s -> p t (a s)", t=NT)
            post_norm(FPOST0, 0, ("y0",), temp)
            pre_norm(PRE1, 0, hres)
            drain_turned("mem1T", memT)
            post_norm(FPOST0, 1, ("y0",), temp)
            pre_norm(PRE1, 1, hres)
            drain_turned("x1T", xT)

            def heads(i, dst, scale=None):
                copy(("p", i), dst, bank(bk.at["p", i][0]).rearrange("p (c s) -> p c s", c=2), scale)

            copy(("v1b", 1), v[:, 1, 512:768], bank(7, 0, 256))
            for u, layer, g, tt, *_ in UNITS1:
                row_max(u, layer, g, tt, MEM // P)
            for u, layer, g, tt, *_ in UNITS1:
                normalise(u, layer, g, MEM // P)
            heads(1, qT[:, 2:4, :], SCALE)
            for u, *_ in UNITS1:
                turned_probs(u, MEM // P)
            heads(3, kT[:, 0:2, :])
            heads(5, kT[:, 4:6, :])
            copy(("v1a", 1), v[:, 1, 0:512], bank(1))

            def softplus(p):
                x = soft[:, p % 2, :, :]
                dve.wait_ge(soft_a, p + 1)
                for b in range(2):
                    dve.scalar_tensor_tensor(out=x[:, b, :], in0=bank(2 * (p % 3) + b, 0, 384), scalar=0.0,
                                             in1=x[:, b, :], op0=ALU.max, op1=ALU.add)\
                        .then_inc(bk.empty_sem(("z", p, b)), 1)
                for b in range(2):
                    dve.wait_ge(*bk.empty(("z", p, b)))
                clear(x).then_inc(soft_b, 1)

            def clear(x):
                dve.tensor_tensor(x[:, :, 0:P], x[:, :, 0:P], clamp[:, :].unsqueeze(1).to_broadcast((P, 2, P)),
                                  ALU.min)
                return dve.tensor_tensor(x[:, :, 2 * P:3 * P], x[:, :, 2 * P:3 * P],
                                         clamp[:, :].unsqueeze(1).to_broadcast((P, 2, P)), ALU.min)

            NP = NH // 2
            for s in range(NP + 1):
                if s < NP:
                    softplus(s)
                if s >= 1:
                    for b in range(2):
                        dve.wait_ge(*bk.empty(("zc", s - 1, b)))
                    clear(stick[:, (s - 1) % 2, :, :]).then_inc(stick_b, 1)
            cut_rest(0, 0, NPC + 1)
            cut_rest(1, 1, NPC + 2)
            post_norm(POST1, 0, ("mix", 1), xn)
            pre_norm(FPRE1, 0, hres)
            post_norm(POST1, 1, ("mix", 1), xn)
            drain_turned("f1T", xT, [0])
            cut_rest(2, 2, NPC + 3)
            pre_norm(FPRE1, 1, hres)
            drain_turned("f1T", xT, [1])

            dve.wait_ge(*bk.full(("logits",)))
            dve.tensor_copy(logits[:, :, :], bank(0, 0, NT * NE).rearrange("p (t e) -> p t e", t=NT))\
                .then_inc(bk.empty_sem(("logits",)), 1)
            dve.wait_ge(*bk.empty(("logits",)))
            for tt in range(NT):
                ins = dve.max(top_v[:, tt, :], logits[:, tt, :])
            link(ins)
            for tt in range(NT):
                dve.max_index(top_i[:, tt, :], top_v[:, tt, :], logits[:, tt, :])
            dve.tensor_tensor(gate2[:, :, 0:1], top_v[:, :, 1:2], top_v[:, :, 0:1], ALU.subtract)\
                .then_inc(gap_ok, 1)
            dve.wait_ge(gap_ok, 1)
            link(dve.tensor_copy(top_f[:, :, :], top_i[:, :, :]))
            for tt in range(NT):
                for c in range(2):
                    ins = dve.tensor_scalar(mask2[:, tt, c, :], iota_s[:, 0:NE], top_f[:, tt, c:c + 1], None,
                                            ALU.is_equal)
            link(ins)
            dve.tensor_tensor(chosen_b[:, :, :], mask2[:, :, 0, :], mask2[:, :, 1, :], ALU.add)\
                .then_inc(chosen_ok, 1)
            link(dve.tensor_tensor(chosen[:, :, :], mask2[:, :, 0, :], mask2[:, :, 1, :], ALU.add))
            dve.wait_ge(*bk.full(("rank",)))
            dve.tensor_copy(over[:, 0, :], bank(5, 2 * NE, 3 * NE))
            dve.scalar_tensor_tensor(out=rank[:, :, :], in0=bank(5, 0, NT * NE).rearrange("p (t e) -> p t e", t=NT),
                                     scalar=1.0, in1=chosen[:, :, :], op0=ALU.add, op1=ALU.mult)\
                .then_inc(bk.empty_sem(("rank",)), 1)
            dve.wait_ge(*bk.empty(("rank",)))
            link(dve.tensor_scalar(slot_of[:, :, 0:NE], rank[:, :, :], -1.0, None, ALU.add))
            for tt in range(NT):
                ins = dve.tensor_scalar(pick[:, tt, :], iota_s[:, :], slot_of[:, tt, 0:1], None, ALU.is_equal)
            ins.then_inc(pick_ok, 1)
            dve.wait_ge(gexp_ok, 1)
            link(dve.tensor_scalar(gate2[:, :, 2:3], gate2[:, :, 1:2], 1.0, None, ALU.add))
            link(dve.reciprocal(gate2[:, :, 2:3], gate2[:, :, 2:3]))
            link(dve.tensor_tensor(gate2[:, :, 3:4], gate2[:, :, 1:2], gate2[:, :, 2:3], ALU.mult))
            for tt in range(NT):
                ins = dve.tensor_scalar(gates[:, tt, :], mask2[:, tt, 0, :], gate2[:, tt, 2:3], None, ALU.mult)
            link(ins)
            for tt in range(NT):
                ins = dve.scalar_tensor_tensor(out=gates[:, tt, :], in0=mask2[:, tt, 1, :],
                                               scalar=gate2[:, tt, 3:4], in1=gates[:, tt, :],
                                               op0=ALU.mult, op1=ALU.add)
            link(ins)
            dve.memset(slot_of[:, :, NE + 3:MAX_JOBS + 1], -1.0)
            dve.memset(gate_of[:, :, NE + 3:MAX_JOBS + 1], 0.0)
            dve.tensor_copy(gate_of[:, :, 0:NE], gates[:, :, :])
            link(dve.tensor_scalar(over[:, 1, :], over[:, 0, :], float(CAP), None, ALU.is_gt))
            link(dve.tensor_tensor_scan(over[:, 2, :], ones[:, 0:NE], over[:, 1, :], 0.0, ALU.mult, ALU.add))
            for o in range(3):
                ins = dve.scalar_tensor_tensor(out=over_sel[:, o, :], in0=over[:, 2, :], scalar=float(o + 1),
                                               in1=over[:, 1, :], op0=ALU.is_equal, op1=ALU.mult)
            link(ins)
            for o in range(3):
                for tt in range(NT):
                    link(dve.scalar_tensor_tensor(out=junk8[:, 0:NE], in0=slot_of[:, tt, 0:NE],
                                                  scalar=-float(CAP), in1=over_sel[:, o, :], op0=ALU.add,
                                                  op1=ALU.mult, accum_out=slot_of[:, tt, NE + o:NE + o + 1]))
                    link(dve.scalar_tensor_tensor(out=junk8[:, 0:NE], in0=gates[:, tt, :], scalar=1.0,
                                                  in1=over_sel[:, o, :], op0=ALU.mult, op1=ALU.mult,
                                                  accum_out=gate_of[:, tt, NE + o:NE + o + 1]))
                link(dve.scalar_tensor_tensor(out=junk8[:, 0:NE], in0=iota_s[:, 0:NE], scalar=1.0,
                                              in1=over_sel[:, o, :], op0=ALU.mult, op1=ALU.mult,
                                              accum_out=job_f[:, o:o + 1]))
            link(dve.tensor_scalar(job_f[:, 3:4], over[:, 2, NE - 1:NE], float(NE), None, ALU.add))
            dve.tensor_copy(job_i[:, :], job_f[:, :]).then_inc(tables_ok, 1)

            link(dve.memset(esum[:, :, :], 0.0))

            def gathered(label, hf, j=None):
                part = (slice(None), slice(4 * hf, 4 * hf + 4), slice(None))
                lower_part(label, picked_lo[part], bank(4 + hf).rearrange("p (k s) -> p k s", k=4),
                           picked_hi[part], j)

            for hf in range(2):
                gathered(("pre-gather", hf), hf)
            dve.wait_ge(tables_ok, 1)
            n_jobs = dve.value_load(job_i[0:1, 3:4], min_val=NE, max_val=MAX_JOBS)
            with dve.Fori(0, n_jobs) as j:
                def full(label):
                    dve.wait_ge(*bk.full(label, j))

                for i, (kind, b, half) in enumerate(pieces):
                    if (kind, half) == ("g", 1) and b >= 1:
                        lower_part(("T", b - 1), h_lo[:, (b - 1) % 2, :], bank(7), h_hi[:, (b - 1) % 2, :], j)
                    if (kind, half) == ("u", 1):
                        dve.wait_ge(*bk.empty(("g", b), j))
                        full(("u", b))
                        dve.tensor_tensor(hid1[:, b % 2, :].rearrange("p (c q) -> p q c", c=CB),
                                          act1[:, b % 2, :].rearrange("p (q c) -> p q c", c=CB),
                                          bank(bk.at["u", b][0]).rearrange("p (q c) -> p q c", c=CB),
                                          ALU.mult).then_inc(bk.empty_sem(("u", b)), 1)
                    if (kind, b, half) == ("d", 0, 0):
                        full(("pickT",))
                        for tt in range(NT):
                            ins = dve.tensor_scalar(pick[:, tt, :], iota_s[:, :],
                                                    slot_of[:, tt, bass.ds(j + 1, 1)], None, ALU.is_equal)
                        ins.then_inc(pick_ok, 1)
                    if (kind, b, half) == ("d", NB - 2, 0):
                        lower_part(("T", NB - 1), h_lo[:, (NB - 1) % 2, :], bank(7), h_hi[:, (NB - 1) % 2, :], j)
                    if i == NPC - 1:
                        full(("y", 1))
                        dve.tensor_copy(y_sb[:, 512:1024], bank(1)).then_inc(bk.empty_sem(("y", 1)), 1)
                    cut_rest(i + CUT, i + CUT, NPC * j + (NPC + i + CUT + 1))
                for hf in range(2):
                    gathered(("gather", hf), hf, j)
                for tt, hf in [(0, 0), (0, 1), (1, 0), (1, 1)]:
                    full(("back", tt, hf))
                    e = esum[:, tt, hf * 512:(hf + 1) * 512]
                    dve.scalar_tensor_tensor(out=e, in0=bank(bk.at["back", tt, hf][0]),
                                             scalar=gate_of[:, tt, bass.ds(j, 1)], in1=e, op0=ALU.mult,
                                             op1=ALU.add).then_inc(bk.empty_sem(("back", tt, hf)), 1)
            for label in [("back", tt, hf) for tt in range(NT) for hf in range(2)]:
                dve.wait_ge(*bk.empty(label, n_jobs - 1))
            dve.sem_inc(tables_ok, 1)
            for tt in range(NT):
                scale_rows(FPOST1, tt, xn[:, tt, :], esum[:, tt, :])
                dve.tensor_tensor(hres[:, tt, :], hres[:, tt, :], xn[:, tt, :], ALU.add).then_inc(added, 1)

        @block.gpsimd
        def _(pool):
            links = [0]

            def link(ins):
                links[0] += 1
                ins.then_inc(pool_chain, 1)
                pool.wait_ge(pool_chain, links[0])

            def load_gain(n):
                g = t[NORMS[n]].rearrange("(a d) -> a d", a=1).to_broadcast((P, D))
                pool.dma_start(gains[:, n % NG, :], g).then_inc(gain_in[n % NG], 16)

            for n in range(NG):
                load_gain(n)

            def where(m, lo, cmp, fill, step, ch):
                x = m[:, lo:lo + P]
                return pool.affine_select(out=x, in_=x, compare_op=cmp, fill=fill, base=0, pattern=[[step, P]],
                                          channel_multiplier=ch)

            def inverse_rms(norm, tt):
                x = rstd[:, norm, tt:tt + 1]
                pool.wait_ge(summed, NORM_COUNT[norm, tt])
                link(pool.tensor_scalar(x, ssq[:, norm, tt:tt + 1], 1.0 / D, EPS, ALU.mult, ALU.add))
                pool.tensor_tensor(x, x, mhalf[:, 0:1], ALU.pow).then_inc(rstd_ok, 1)

            pool.memset(mhalf[:, :], -0.5)
            link(pool.memset(ident[:, :], 0.0))
            where(ident, 0, ALU.not_equal, 1.0, -1, 1).then_inc(ident_ok, 1)
            for tt in range(NT):
                inverse_rms(MEM0, tt)

            for m, val in ((upper_neg, 0.0), (ones_neg, -1.0), (ones, 1.0), (before, 0.0),
                           (band, 0.0), (clamp, 0.0), (halfpi, TWO_PI / 4)):
                pool.memset(m[:, :], val)
            for i in range(HD // 2):
                pool.memset(invf[:, i:i + 1], THETA ** (-2.0 * i / HD))
            link(pool.iota(iota_i, pattern=[[1, P]], base=0, channel_multiplier=0))
            pool.tensor_copy(iota_s[:, :], iota_i)

            where(upper_neg, 0, ALU.is_gt, -1.0, 1, -1)
            where(before, 0, ALU.is_ge, 1.0, -1, 1)
            where(band, 0, ALU.is_gt, NEG, 1, -1)
            where(band, P, ALU.is_ge, NEG, -1, 1)
            link(where(clamp, 0, ALU.is_ge, BIG, -1, 1))
            pool.tensor_copy(ones_b[:, :], ones[:, :])
            link(pool.tensor_copy(before_b[:, :], before[:, :]))
            pool.sem_inc(consts, 1)

            for norm, tt in NORM_ORDER:
                if norm != MEM0:
                    inverse_rms(norm, tt)
                if tt == NT - 1 and norm + NG < len(NORMS):
                    pool.wait_ge(scaled, NORM_COUNT[norm, tt])
                    load_gain(norm + NG)

        @block.sync
        def _(sp):
            for tt in range(NT):
                sp.dma_start(memb[:, tt, :], t["mem"][0, tt * P:(tt + 1) * P, :]).then_inc(mem_in[tt], 16)
            for tt in range(NT):
                sp.dma_start(hres[:, tt, :], t["x"][0, tt * P:(tt + 1) * P, :]).then_inc(x_in[tt], 16)
            with nc.allow_non_contiguous_dma(reason="256 positions and 12 sinks"):
                sp.dma_start(pos_i[:, :], t["positions"].rearrange("a (t p) -> p (a t)", p=P)).then_inc(small_in, 16)
                sp.dma_start(sinks[:, :], t["l0_sinks"].rearrange("(a h) -> a h", a=1).to_broadcast((P, NH)))\
                    .then_inc(small_in, 16)
                sp.dma_start(wr[:, :, :], t["l1_w_router"].rearrange("(k p) e -> p k e", p=P)).then_inc(small_in, 16)

            def load(n, src):
                _, c, w = src.shape
                sp.dma_start(raw_at(n, c, w), src).then_inc(raw_full[n % RAW], 16)

            for m in range(NPC):
                free_after[FFN0 + m] = (lo_ok, m + 1)

            for n, src in enumerate(loads):
                if n >= RAW:
                    sp.wait_ge(*free_after[n - RAW])
                load(n, src)

            def expert_load(e, m, free):
                kind, b, half = pieces[m]
                sp.wait_ge(*free)
                if (kind, b, half) == ("d", 0, 0):
                    sp.sem_inc(sp_step, 1)
                if kind == "d":
                    w = t["l1_w_down"][bass.ds(e, 1), b * FB:(b + 1) * FB, :]
                    src = w.rearrange("e (p c) n -> p (e c) n", c=CB)[:, 2 * half:2 * half + 2, :]
                else:
                    w = t["l1_w_gate" if kind == "g" else "l1_w_up"]
                    src = w[bass.ds(e, 1), 4 * half * P:4 * (half + 1) * P, b * FB:(b + 1) * FB]\
                        .rearrange("e (k p) n -> p (e k) n", p=P)
                load(m, src)

            def cut_of(j, m):
                return lo_ok, NPC * j + (NPC + m - RAW + 1)

            for m in range(RAW):
                expert_load(0, m, free_after[PRE + m - RAW])
            with sp.Fori(0, NE - 1) as j:
                for m in range(RAW, NPC):
                    expert_load(j, m, cut_of(j, m))
                for m in range(RAW):
                    expert_load(j + 1, m, cut_of(j, NPC + m))
            for m in range(RAW, NPC):
                expert_load(NE - 1, m, cut_of(NE - 1, m))
            sp.wait_ge(tables_ok, 1)
            n_jobs = sp.value_load(job_i[0:1, 3:4], min_val=NE, max_val=MAX_JOBS)
            with sp.If(n_jobs > NE):
                with sp.Fori(NE, n_jobs) as j:
                    e = sp.value_load(job_i[0:1, bass.ds(j - NE, 1)], min_val=0, max_val=NE - 1)
                    for m in range(NPC):
                        expert_load(e, m, cut_of(j, m))
            for m in range(CUT):
                expert_load(0, m, cut_of(n_jobs, m))
            for tt in range(NT):
                sp.wait_ge(added, 6 + tt + 1)
                sp.dma_start(t["out"][0, tt * P:(tt + 1) * P, :], hres[:, tt, :]).then_inc(stored, 16)
            sp.wait_ge(stored, 16 * NT)


_INS = ["x", "mem", "positions", "l0_attn_pre_g", "l0_mem_g", "l0_w_in", "l0_w_mem_kv", "l0_sinks", "l0_w_out",
        "l0_attn_post_g", "l0_ffn_pre_g", "l0_w_gate", "l0_w_up", "l0_w_down", "l0_ffn_post_g",
        "l1_attn_pre_g", "l1_mem_g", "l1_w_in", "l1_w_mem_kv", "l1_w_out", "l1_attn_post_g", "l1_ffn_pre_g",
        "l1_w_router", "l1_w_gate", "l1_w_up", "l1_w_down", "l1_ffn_post_g"]


def kernel(**inputs):
    import numpy as np
    import concourse.bacc as bacc
    from concourse.bass_utils import run_bass_kernel_spmd

    nc = bacc.Bacc("TRN2", target_bir_lowering=False, num_devices=1)
    arrays, t = {}, {}
    for name in _INS:
        a = np.ascontiguousarray(inputs[name])
        arrays[f"in_{name}"] = a
        t[name] = nc.dram_tensor(f"in_{name}", a.shape, mybir.dt.from_np(a.dtype), kind="ExternalInput").ap()
    t["out"] = nc.dram_tensor("out", (1, S, D), F32, kind="ExternalOutput").ap()
    trunk(nc, t)
    r = run_bass_kernel_spmd(nc, [arrays], core_ids=[0])
    return r.results[0]["out"]
```
